# Optimizing a Trainium2 kernel written in Bass

```python
import jax
import jax.numpy as jnp
from jax import lax
import numpy as np

D_MODEL = 1024
BATCH = 1
SEQ = 256
DEPTH = 2
DEC_BATCH = 8
DEC_SEQ = 8
PAST_LEN = 2048
PAGE_SIZE = 128

ROPE_THETA = 500000.0
RMS_EPS = 1e-6
Q_BLOCK = 128
D_FF = 2816
H_A = 8
DH_A = 64
W_A = H_A * DH_A
LORA_W = 32
LORA_A = 32
LORA_G = 96
GN_EPS = 64e-5
A_COLS = 3 * W_A + LORA_W + LORA_A + LORA_G
H_B = 8
DH_B = 64
W_B = H_B * DH_B
DILATED_GROUPS = ((128, 1), (512, 4), (2048, 16))
N_GROUPS_B = len(DILATED_GROUPS)
WIN_MAX = max(w for w, _ in DILATED_GROUPS)
ROT_B = DH_B // 4
B_COLS = (N_GROUPS_B + 2) * W_B
H_C = 8
DNOPE = 64
DROPE = 32
DV = 64
Q_LORA = 384
KV_LORA = 256
W_C = H_C * DV
C_COLS = Q_LORA + KV_LORA + DROPE
N_BRANCH = 3
GATE_COLS = N_BRANCH * D_MODEL
IN_COLS = A_COLS + B_COLS + C_COLS + GATE_COLS

kernel_name = 'hybrid_rwkv7_dilated_mla_decode_step'

def rmsnorm(x, g):
    xf = x.astype(jnp.float32)
    y = xf * lax.rsqrt(jnp.mean(xf * xf, axis=-1, keepdims=True) + RMS_EPS)
    return (y * g.astype(jnp.float32)).astype(x.dtype)

def rope(x, pos):
    d = x.shape[-1]
    half = d // 2
    inv = ROPE_THETA ** (-(jnp.arange(half, dtype=jnp.float32) * 2.0 / d))
    ang = pos.astype(jnp.float32)[:, None] * inv[None, :]
    shp = (1, pos.shape[0]) + (1,) * (x.ndim - 3) + (half,)
    cos = jnp.cos(ang).reshape(shp)
    sin = jnp.sin(ang).reshape(shp)
    xf = x.astype(jnp.float32)
    x1, x2 = xf[..., :half], xf[..., half:]
    return jnp.concatenate([x1 * cos - x2 * sin, x2 * cos + x1 * sin], axis=-1).astype(x.dtype)

def partial_rope(x, pos, n_rot):
    return jnp.concatenate([rope(x[..., :n_rot], pos), x[..., n_rot:]], axis=-1)

def swiglu(x, wg, wu, wd):
    return (jax.nn.silu(x @ wg) * (x @ wu)) @ wd

def map_query_blocks(fn, qs, q_off):
    b_, t_ = qs[0].shape[:2]
    bq = min(Q_BLOCK, t_)
    nb = t_ // bq
    blocks = tuple(jnp.moveaxis(q.reshape((b_, nb, bq) + q.shape[2:]), 1, 0) for q in qs)
    starts = q_off + bq * jnp.arange(nb, dtype=jnp.int32)
    out = lax.map(lambda a: fn(a[0], a[1]), (blocks, starts))
    out = jnp.moveaxis(out, 0, 1)
    return out.reshape((b_, t_) + out.shape[3:])

def dilated_window_attention(qg, k_all, v_all, q_off):
    scale = DH_B ** -0.5

    def block(q_blk, start):
        (qb,) = q_blk
        rows = start + jnp.arange(qb.shape[1], dtype=jnp.int32)
        outs, lses = [], []
        for g, (win, dil) in enumerate(DILATED_GROUPS):
            n_keys = win // dil + 1
            idx = rows[:, None] - dil * jnp.arange(n_keys, dtype=jnp.int32)[None, :]
            valid = idx >= 0
            idx = jnp.maximum(idx, 0)
            kg = k_all[:, idx]
            vg = v_all[:, idx]
            s = jnp.einsum('bqhd,bqjhd->bqhj', qb[:, :, g], kg).astype(jnp.float32) * scale
            s = jnp.where(valid[None, :, None, :], s, -jnp.inf)
            lse = jax.nn.logsumexp(s, axis=-1)
            p = jnp.exp(s - lse[..., None])
            outs.append(jnp.einsum('bqhj,bqjhd->bqhd', p, vg.astype(jnp.float32)))
            lses.append(lse)
        wgt = jax.nn.softmax(jnp.stack(lses, axis=0), axis=0)
        o = jnp.sum(wgt[..., None] * jnp.stack(outs, axis=0), axis=0)
        return o.astype(qb.dtype)

    return map_query_blocks(block, (qg,), q_off)

def latent_attention(q_lat, q_rope, ckv_all, krope_all, q_off):
    scale = (DNOPE + DROPE) ** -0.5
    key_rows = jnp.arange(ckv_all.shape[1], dtype=jnp.int32)

    def block(q_blk, start):
        ql, qr = q_blk
        rows = start + jnp.arange(ql.shape[1], dtype=jnp.int32)
        s = (jnp.einsum('bqhc,blc->bhql', ql, ckv_all)
             + jnp.einsum('bqhr,blr->bhql', qr, krope_all)).astype(jnp.float32) * scale
        s = jnp.where(key_rows[None, :] <= rows[:, None], s, -jnp.inf)
        p = jax.nn.softmax(s, axis=-1)
        return jnp.einsum('bhql,blc->bqhc', p.astype(ckv_all.dtype), ckv_all)

    return map_query_blocks(block, (q_lat, q_rope), q_off)

def rwkv7_recurrence(r, w, k, v, kk, a, s0):
    def step(s, inp):
        r_t, w_t, k_t, v_t, kk_t, a_t = inp
        sa = jnp.einsum('bhvk,bhk->bhv', s, -kk_t)
        s = (s * w_t[:, :, None, :] + sa[..., None] * (kk_t * a_t)[:, :, None, :]
             + v_t[..., None] * k_t[:, :, None, :])
        return s, jnp.einsum('bhvk,bhk->bhv', s, r_t)
    xs = tuple(jnp.moveaxis(t, 1, 0) for t in (r, w, k, v, kk, a))
    s_fin, ys = lax.scan(step, s0, xs)
    return jnp.moveaxis(ys, 0, 1), s_fin

def rwkv7_mixer(pa, shift0, s0, l, P):
    b_, t_, _ = pa.shape
    dt = pa.dtype
    f32 = jnp.float32
    prev = jnp.concatenate([shift0[:, None].astype(dt), pa[:, :-1]], axis=1)
    xs = pa + (prev - pa) * P['a_mu'][l]
    r = xs[..., :W_A]
    k = xs[..., W_A:2 * W_A]
    v = xs[..., 2 * W_A:3 * W_A]
    o = 3 * W_A
    wd = xs[..., o:o + LORA_W]
    o += LORA_W
    ad = xs[..., o:o + LORA_A]
    o += LORA_A
    gd = xs[..., o:o + LORA_G]
    w_log = -jax.nn.softplus(-(P['a_w0'][l] + jnp.tanh(wd) @ P['a_w2'][l])) - 0.5
    decay = jnp.exp(-jnp.exp(w_log.astype(f32)))
    a = jax.nn.sigmoid(P['a_a0'][l] + ad @ P['a_a2'][l])
    g = jax.nn.sigmoid(gd) @ P['a_g2'][l]
    heads = lambda t: t.reshape(b_, t_, H_A, DH_A).astype(f32)
    kk = heads(k * P['a_kk'][l])
    kk = kk / jnp.maximum(jnp.sqrt(jnp.sum(kk * kk, axis=-1, keepdims=True)), 1e-12)
    k = k * (1.0 + (a - 1.0) * P['a_ka'][l])
    rh, kh, vh = heads(r), heads(k), heads(v)
    y, s_fin = rwkv7_recurrence(rh, heads(decay), kh, vh, kk, heads(a), s0.astype(f32))
    mu = jnp.mean(y, axis=-1, keepdims=True)
    var = jnp.mean((y - mu) ** 2, axis=-1, keepdims=True)
    yn = ((y - mu) * lax.rsqrt(var + GN_EPS)).reshape(b_, t_, W_A)
    yn = yn * P['a_ln_w'][l].astype(f32) + P['a_ln_b'][l].astype(f32)
    bonus = (jnp.sum(rh * kh * P['a_rk'][l].astype(f32), axis=-1, keepdims=True) * vh).reshape(b_, t_, W_A)
    out = ((yn + bonus) * g.astype(f32)).astype(dt)
    return out, pa[:, -1], s_fin.astype(dt)

def token_mixing(h, pos, past, keep, l, P):
    b_, t_, _ = h.shape
    proj = h @ P['w_in'][l]
    pa = proj[..., :A_COLS]
    pb = proj[..., A_COLS:A_COLS + B_COLS]
    pc = proj[..., A_COLS + B_COLS:A_COLS + B_COLS + C_COLS]
    pg = proj[..., A_COLS + B_COLS + C_COLS:]
    ya, shift_new, wkv_new = rwkv7_mixer(pa, past['shift'], past['wkv'], l, P)
    qb = partial_rope(pb[..., :N_GROUPS_B * W_B].reshape(b_, t_, N_GROUPS_B, H_B, DH_B), pos, ROT_B)
    kb = partial_rope(pb[..., N_GROUPS_B * W_B:(N_GROUPS_B + 1) * W_B].reshape(b_, t_, H_B, DH_B), pos, ROT_B)
    vb = pb[..., (N_GROUPS_B + 1) * W_B:].reshape(b_, t_, H_B, DH_B)
    k_all = jnp.concatenate([past['swa_k'].astype(kb.dtype), kb], axis=1)
    v_all = jnp.concatenate([past['swa_v'].astype(vb.dtype), vb], axis=1)
    yb = dilated_window_attention(qb, k_all, v_all, past['swa_k'].shape[1]).reshape(b_, t_, W_B)
    cq = rmsnorm(pc[..., :Q_LORA], P['c_q_norm'][l])
    q = (cq @ P['c_q_up'][l]).reshape(b_, t_, H_C, DNOPE + DROPE)
    q_nope = q[..., :DNOPE]
    q_rope = rope(q[..., DNOPE:], pos)
    ckv = rmsnorm(pc[..., Q_LORA:Q_LORA + KV_LORA], P['c_kv_norm'][l])
    krope = rope(pc[..., Q_LORA + KV_LORA:], pos)
    kv_up = P['c_kv_up'][l].reshape(KV_LORA, H_C, DNOPE + DV)
    q_lat = jnp.einsum('bthn,chn->bthc', q_nope, kv_up[..., :DNOPE])
    ckv_all = jnp.concatenate([past['ckv'].astype(ckv.dtype), ckv], axis=1)
    krope_all = jnp.concatenate([past['krope'].astype(krope.dtype), krope], axis=1)
    o_lat = latent_attention(q_lat, q_rope, ckv_all, krope_all, past['ckv'].shape[1])
    yc = jnp.einsum('bthc,chv->bthv', o_lat, kv_up[..., DNOPE:]).reshape(b_, t_, W_C)
    gates = jax.nn.sigmoid(pg + P['b_gate'][l]).reshape(b_, t_, N_BRANCH, D_MODEL)
    m = (gates[:, :, 0] * (ya @ P['w_branch_a'][l]) + gates[:, :, 1] * (yb @ P['w_branch_b'][l])
         + gates[:, :, 2] * (yc @ P['w_branch_c'][l]))
    new_state = dict(ckv=ckv, krope=krope, swa_k=k_all[:, -keep:], swa_v=v_all[:, -keep:],
                     wkv=wkv_new, shift=shift_new)
    return m @ P['w_out'][l], new_state

def trunk_layer(x, pos, past, keep, l, P):
    h = rmsnorm(x, P['n_f1_pre'][l])
    x = x + 0.5 * rmsnorm(swiglu(h, P['f1_wg'][l], P['f1_wu'][l], P['f1_wd'][l]), P['n_f1_post'][l])
    h = rmsnorm(x, P['n_mix_pre'][l])
    mixed, new_state = token_mixing(h, pos, past, keep, l, P)
    x = x + rmsnorm(mixed, P['n_mix_post'][l])
    h = rmsnorm(x, P['n_f2_pre'][l])
    x = x + 0.5 * rmsnorm(swiglu(h, P['f2_wg'][l], P['f2_wu'][l], P['f2_wd'][l]), P['n_f2_post'][l])
    return x, new_state

def setup_inputs(seed: int = 0) -> dict:
    key = jax.random.key(seed)
    ks = iter(jax.random.split(key, 64))
    nk = lambda: next(ks)
    f32 = jnp.float32
    n_pages = PAST_LEN // PAGE_SIZE
    n_pool = (DEC_BATCH * n_pages * 5) // 4
    win_buf = min(WIN_MAX, PAST_LEN)
    nrm = lambda shape, s=1.0: (s * jax.random.normal(nk(), shape, dtype=f32))
    gain = lambda shape: 1.0 + 0.1 * jax.random.normal(nk(), shape, dtype=f32)
    lin = lambda fi, fo, s=1.0: nrm((DEPTH, fi, fo), s * fi ** -0.5)
    perm = jax.random.permutation(nk(), n_pool)
    page_table = perm[:DEC_BATCH * n_pages].reshape(DEC_BATCH, n_pages).astype(jnp.int32)
    return {
        'x_prompt': nrm((BATCH, SEQ, D_MODEL)),
        'x_sample': nrm((DEC_BATCH, DEC_SEQ, D_MODEL)),
        'cache_mla_ckv': nrm((DEPTH, n_pool, PAGE_SIZE, KV_LORA)),
        'cache_mla_krope': nrm((DEPTH, n_pool, PAGE_SIZE, DROPE)),
        'cache_swa_k': nrm((DEPTH, DEC_BATCH, win_buf, H_B, DH_B)),
        'cache_swa_v': nrm((DEPTH, DEC_BATCH, win_buf, H_B, DH_B)),
        'state_rwkv_wkv': nrm((DEPTH, DEC_BATCH, H_A, DH_A, DH_A), 0.5),
        'state_rwkv_shift': nrm((DEPTH, DEC_BATCH, A_COLS)),
        'page_table': page_table,
        'w_in': lin(D_MODEL, IN_COLS),
        'b_gate': nrm((DEPTH, GATE_COLS), 0.1),
        'w_branch_a': lin(W_A, D_MODEL),
        'w_branch_b': lin(W_B, D_MODEL),
        'w_branch_c': lin(W_C, D_MODEL),
        'w_out': lin(D_MODEL, D_MODEL),
        'a_mu': jax.random.uniform(nk(), (DEPTH, A_COLS), dtype=f32),
        'a_w0': jax.random.uniform(nk(), (DEPTH, W_A), dtype=f32, minval=-6.0, maxval=0.0),
        'a_w2': lin(LORA_W, W_A, 0.5),
        'a_a0': nrm((DEPTH, W_A), 0.5),
        'a_a2': lin(LORA_A, W_A, 0.5),
        'a_g2': lin(LORA_G, W_A),
        'a_kk': 0.85 + 0.1 * jax.random.normal(nk(), (DEPTH, W_A), dtype=f32),
        'a_ka': gain((DEPTH, W_A)),
        'a_rk': nrm((DEPTH, H_A, DH_A), 0.1),
        'a_ln_w': gain((DEPTH, W_A)),
        'a_ln_b': nrm((DEPTH, W_A), 0.1),
        'c_q_norm': gain((DEPTH, Q_LORA)),
        'c_q_up': lin(Q_LORA, H_C * (DNOPE + DROPE)),
        'c_kv_norm': gain((DEPTH, KV_LORA)),
        'c_kv_up': lin(KV_LORA, H_C * (DNOPE + DV)),
        'f1_wg': lin(D_MODEL, D_FF),
        'f1_wu': lin(D_MODEL, D_FF),
        'f1_wd': lin(D_FF, D_MODEL),
        'f2_wg': lin(D_MODEL, D_FF),
        'f2_wu': lin(D_MODEL, D_FF),
        'f2_wd': lin(D_FF, D_MODEL),
        'n_f1_pre': gain((DEPTH, D_MODEL)),
        'n_f1_post': gain((DEPTH, D_MODEL)),
        'n_mix_pre': gain((DEPTH, D_MODEL)),
        'n_mix_post': gain((DEPTH, D_MODEL)),
        'n_f2_pre': gain((DEPTH, D_MODEL)),
        'n_f2_post': gain((DEPTH, D_MODEL)),
    }

def reference(x_prompt, x_sample, cache_mla_ckv, cache_mla_krope, cache_swa_k, cache_swa_v,
              state_rwkv_wkv, state_rwkv_shift, page_table,
              w_in, b_gate, w_branch_a, w_branch_b, w_branch_c, w_out,
              a_mu, a_w0, a_w2, a_a0, a_a2, a_g2, a_kk, a_ka, a_rk, a_ln_w, a_ln_b,
              c_q_norm, c_q_up, c_kv_norm, c_kv_up,
              f1_wg, f1_wu, f1_wd, f2_wg, f2_wu, f2_wd,
              n_f1_pre, n_f1_post, n_mix_pre, n_mix_post, n_f2_pre, n_f2_post):
    P = dict(w_in=w_in, b_gate=b_gate, w_branch_a=w_branch_a, w_branch_b=w_branch_b,
             w_branch_c=w_branch_c, w_out=w_out, a_mu=a_mu, a_w0=a_w0, a_w2=a_w2, a_a0=a_a0,
             a_a2=a_a2, a_g2=a_g2, a_kk=a_kk, a_ka=a_ka, a_rk=a_rk, a_ln_w=a_ln_w, a_ln_b=a_ln_b,
             c_q_norm=c_q_norm, c_q_up=c_q_up, c_kv_norm=c_kv_norm, c_kv_up=c_kv_up,
             f1_wg=f1_wg, f1_wu=f1_wu, f1_wd=f1_wd, f2_wg=f2_wg, f2_wu=f2_wu, f2_wd=f2_wd,
             n_f1_pre=n_f1_pre, n_f1_post=n_f1_post, n_mix_pre=n_mix_pre,
             n_mix_post=n_mix_post, n_f2_pre=n_f2_pre, n_f2_post=n_f2_post)
    bp, tp = x_prompt.shape[:2]
    db, n_pages = page_table.shape
    past_len = n_pages * cache_mla_ckv.shape[2]
    dt = x_prompt.dtype
    pos_p = jnp.arange(tp, dtype=jnp.int32)
    pos_s = past_len + jnp.arange(x_sample.shape[1], dtype=jnp.int32)
    keep_p = min(WIN_MAX, tp)
    keep_s = cache_swa_k.shape[2]
    names = ('ckv', 'krope', 'swa_k', 'swa_v', 'wkv', 'shift')
    new_p = {n: [] for n in names}
    new_s = {n: [] for n in names}
    yp, ys = x_prompt, x_sample
    for l in range(DEPTH):
        past_p = dict(shift=jnp.zeros((bp, A_COLS), dt), wkv=jnp.zeros((bp, H_A, DH_A, DH_A), dt),
                      swa_k=jnp.zeros((bp, 0, H_B, DH_B), dt), swa_v=jnp.zeros((bp, 0, H_B, DH_B), dt),
                      ckv=jnp.zeros((bp, 0, KV_LORA), dt), krope=jnp.zeros((bp, 0, DROPE), dt))
        yp, st_p = trunk_layer(yp, pos_p, past_p, keep_p, l, P)
        past_s = dict(shift=state_rwkv_shift[l], wkv=state_rwkv_wkv[l],
                      swa_k=cache_swa_k[l], swa_v=cache_swa_v[l],
                      ckv=cache_mla_ckv[l][page_table].reshape(db, past_len, KV_LORA),
                      krope=cache_mla_krope[l][page_table].reshape(db, past_len, DROPE))
        ys, st_s = trunk_layer(ys, pos_s, past_s, keep_s, l, P)
        for n in names:
            new_p[n].append(st_p[n])
            new_s[n].append(st_s[n])
    stk = lambda d, n: jnp.stack(d[n], axis=0)
    return (yp, ys,
            stk(new_p, 'ckv'), stk(new_s, 'ckv'),
            stk(new_p, 'krope'), stk(new_s, 'krope'),
            stk(new_p, 'swa_k'), stk(new_s, 'swa_k'),
            stk(new_p, 'swa_v'), stk(new_s, 'swa_v'),
            stk(new_p, 'wkv'), stk(new_s, 'wkv'),
            stk(new_p, 'shift'), stk(new_s, 'shift'))


_drawn_inputs = setup_inputs


def setup_inputs(seed=0):
    import zlib

    import numpy as np

    out = dict(_drawn_inputs(seed))
    spreads = {}
    factors = {}
    for name, (base, spread) in spreads.items():
        noise = np.random.default_rng([zlib.crc32(name.encode()), seed]).standard_normal(out[name].shape)
        drawn = base * np.exp(spread * noise) if base else spread * noise
        out[name] = jnp.asarray(drawn.astype(out[name].dtype))
    for name, factor in factors.items():
        out[name] = (out[name] * factor).astype(out[name].dtype)
    return out
```

```python
from contextlib import ExitStack

import numpy as np
import concourse.bass as bass
from concourse import mybir

F32 = mybir.dt.float32
I32 = mybir.dt.int32
ALU = mybir.AluOpType
ACT = mybir.ActivationFunctionType
AX = mybir.AxisListType.X

P = 128
D_MODEL, DEPTH, D_FF = 1024, 2, 2816
SEQ, NB, TS, PAST, PAGE, N_POOL = 256, 8, 8, 2048, 128, 160
NS = NB * TS
T = SEQ + NS
KD, KF = D_MODEL // P, D_FF // P
H, DH = 8, 64
W_A = H * DH
A_COLS, B_COLS, C_COLS = 3 * W_A + 160, 5 * W_A, 672
Q_LORA, KV_LORA, DROPE, DNOPE = 384, 256, 32, 64
CB, CC, CG = A_COLS, A_COLS + B_COLS, A_COLS + B_COLS + C_COLS
ROT, N_PAGES = 8, PAST // PAGE
A_TILES = [(m * P, P) for m in range(12)] + [(3 * W_A, 64), (3 * W_A + 64, 96)]
NAT = len(A_TILES)
PADT = 1 + SEQ + NB * (TS + 1)
TOK_TILES = [(0, 0, P), (1, P, P), (2, SEQ, NS)]
GROUPS_B = ((128, 1), (512, 4), (2048, 16))
CHUNK = 64
SW_TILES = 8 + 4 + 1
SW_COLS = SW_TILES * P + 3 * TS
NEG = -1.0e30

PAR = {}
_at = 0
for _n, _w in [("f1_pre", 8), ("f1_post", 8), ("mix_pre", 8), ("mix_post", 8), ("f2_pre", 8), ("f2_post", 8),
               ("b_gate", 24), ("a_mu", NAT), ("a_w0", 4), ("a_a0", 4), ("a_kk", 4), ("a_ka", 4), ("a_rk", 4),
               ("a_ln_w", 4), ("a_ln_b", 4), ("c_q_norm", 3)]:
    PAR[_n] = (_at, _w)
    _at += _w
NPAR = _at

CONST = {}
_at = 0
for _n, _w in [("ident", P), ("ones", P), ("onesblk", P), ("reset", T), ("cosb", 24), ("sinb", 24), ("cosc", 48),
               ("sinc", 48), ("bmask", 8), ("m8p", 64), ("m8Tp", 64), ("o16T", 64), ("o32T", 64), ("o64T", 64),
               ("sTp", 64), ("iTp", 64), ("sTs", 64), ("iTs", 64), ("swp", 2 * 3 * SEQ),
               ("mlp", 2 * SEQ), ("sws", SW_COLS), ("mls", TS)]:
    CONST[_n] = (_at, _w)
    _at += _w
NCONST = _at


def constants():
    c = np.zeros((P, NCONST), np.float32)

    def put(name, a):
        at, w = CONST[name]
        c[:a.shape[0], at:at + w] = a.reshape(a.shape[0], w)

    put("ident", np.eye(P))
    put("ones", np.ones((P, P)))
    blk = np.arange(P) // DH
    put("onesblk", (blk[:, None] == blk[None, :]) * 1.0)
    reset = np.ones(T)
    reset[0:SEQ:CHUNK] = 0
    reset[SEQ::TS] = 0
    put("reset", np.broadcast_to(reset, (P, T)))
    pos = np.zeros((P, 3), np.float32)
    pos[:, 0], pos[:, 1] = np.arange(P), P + np.arange(P)
    pos[:, 2] = PAST + np.arange(P) % TS
    for tag, half in (("b", ROT), ("c", DROPE // 2)):
        inv = np.float32(500000.0) ** (-(np.arange(half, dtype=np.float32) * np.float32(2.0) / np.float32(2 * half)))
        ang = pos[:, :, None] * inv.astype(np.float32)[None, None, :]
        put("cos" + tag, np.cos(ang))
        put("sin" + tag, np.sin(ang))
    t = np.arange(CHUNK)
    put("bmask", (t[:, None] // TS == np.arange(NB)[None, :]) * 1.0)
    low = t[None, :] < t[:, None]
    same = lambda n: t[:, None] // n == t[None, :] // n
    put("m8p", (low & same(8)) * -1.0)
    put("m8Tp", (low & same(8)).T * -1.0)
    for n in (16, 32, 64):
        put(f"o{n}T", (low & same(n) & ~same(n // 2)).T * -1.0)
    put("sTp", low.T * 1.0)
    put("iTp", (low | same(1)).T * 1.0)
    put("sTs", (low & same(8)).T * 1.0)
    put("iTs", ((low & same(8)) | same(1)).T * 1.0)
    q = np.arange(SEQ)[:, None]
    k = np.arange(SEQ)[None, :]
    swp = np.stack([np.where((q >= k) & ((q - k) % d == 0) & (q - k <= w), 0.0, NEG) for w, d in GROUPS_B], 1)
    put("swp", swp.reshape(2, P, 3, SEQ).transpose(1, 0, 2, 3))
    put("mlp", np.where(q >= k, 0.0, NEG).reshape(2, P, SEQ).transpose(1, 0, 2))
    j = np.arange(NS) % TS
    m = np.full((NS, SW_COLS), NEG)
    a = np.arange(P)
    for r in range(8):
        m[:, r * P:(r + 1) * P] = np.where(j[:, None] == r, 0.0, NEG)
    for r in range(4):
        ok = (j[:, None] % 4 == r) & ((j[:, None] < 4) | (a[None, :] >= 1))
        m[:, (8 + r) * P:(9 + r) * P] = np.where(ok, 0.0, NEG)
    m[:, 12 * P:13 * P] = np.where(a[None, :] >= j[:, None], 0.0, NEG)
    n = np.arange(TS)[None, :]
    for g, (w, d) in enumerate(GROUPS_B):
        ok = (j[:, None] >= n) & ((j[:, None] - n) % d == 0)
        m[:, SW_TILES * P + g * TS:SW_TILES * P + (g + 1) * TS] = np.where(ok, 0.0, NEG)
    put("sws", m)
    put("mls", np.where(j[:, None] >= n, 0.0, NEG))
    return c


ROOTS = {t: i + 1 for i, t in enumerate(("f1_pre", "f1_post", "mix_pre", "kk", "y", "mix_post", "f2_pre", "f2_post"))}
NORMS = {t: i + 1 for i, t in enumerate(("f1_pre", "f1_post", "mix_pre", "mix_post", "f2_pre", "f2_post"))}
PRES = {t: i + 1 for i, t in enumerate(("f1_pre", "mix_pre", "f2_pre"))}
FFN0, DOWN0, PROMPT0 = {"f1": 0, "f2": KF}, {"f1": 0, "mix": KD, "f2": 2 * KD}, {"swp": 0, "mlp": 2 * H}
NSLOT = 3
N_ROWS_OUT = 16 * (4 + 2 * NB + 2)
SLOT = 4096
SWK, SWV = SW_TILES * W_A, SW_TILES * W_A


def weight_units(io):
    out = []

    def cols(w, k, c0, c1):
        return lambda l: w[bass.ds(l, 1), :, c0:c1].rearrange("a (k p) n -> p (a k) n", p=P), k, c1 - c0

    def ffn(f):
        for u in range(KF // 2):
            out.append(((f, "gu", u), [cols(io[f + "_wg"], KD, u * 256, u * 256 + 256),
                                       cols(io[f + "_wu"], KD, u * 256, u * 256 + 256)]))
        for u in range(KD):
            out.append(((f, "d", u), [cols(io[f + "_wd"], KF, u * P, (u + 1) * P)]))

    ffn("f1")
    for u, (c0, c1) in enumerate([(0, 512), (512, 1024), (1024, 1536), (1536, 1696)]):
        out.append((("pa", u), [cols(io["w_in"], KD, c0, c1)]))
    for u, (c0, c1) in enumerate([(CC, CC + 512), (CC + 512, CG)] + [(CB + 512 * i, CB + 512 * i + 512) for i in range(5)]):
        out.append((("pbc", u), [cols(io["w_in"], KD, c0, c1)]))
    for u in range(6):
        out.append((("pg", u), [cols(io["w_in"], KD, CG + 512 * u, CG + 512 * u + 512)]))
    for br in "abc":
        out.append((("br", br), [cols(io["w_branch_" + br], 4, 0, D_MODEL)]))
    for u in range(2):
        out.append((("wo", u), [cols(io["w_out"], KD, 512 * u, 512 * u + 512)]))
    ffn("f2")
    return out


STEPS = (
    "G", "L", "RK", "TT", "X2T", "X4", "X6", "XP", "a_ready", "bonus_in", "bonus_ss", "br_ev", "brm", "ckvT",
    "ckvT_ev", "cqT", "dTT", "down_d", "down_y", "exps", "ffn_a", "ffn_gu", "ffn_sg", "g_level", "g_ready", "gate",
    "group", "h", "hs", "kk0", "kk_sq", "kk_ss", "kt_T", "kt_ev", "kvT", "kvT_ev", "last_rows", "latent_ms",
    "latent_root", "lora_g", "lora_wa", "lt_T", "lt_even", "lt_odd", "masked", "mean_squares", "mixed", "ml_PT", "ml_done",
    "ml_exp", "ml_mm", "ml_nm", "ml_oT", "ml_olT", "ml_osb", "ml_p", "ml_prep", "ml_pt", "ml_pv", "ml_s", "ml_yc",
    "norm_sums", "normed", "odd", "pa", "pa_zeroed", "pam", "pbc_ev", "pbc_mm", "pgm", "pm", "prompt_T", "prompt_e",
    "prompt_mm", "prompt_nm", "prompt_o", "prompt_ol", "prompt_olev", "prompt_p", "prompt_pt", "prompt_s",
    "prompt_y", "q_rope", "q_rows", "qbd", "qcT", "qcT_ev", "qkT", "qk_ev", "ql", "ql_ev", "qrow_ev", "rhs",
    "rhs_ev", "roots", "rows", "rows_ready", "rwkv_done", "squared", "streams", "sw_PT", "sw_e", "sw_masked",
    "sw_mm", "sw_nm", "sw_p", "sw_pt", "sw_pv", "sw_s", "sws_done", "t", "t_level", "tanh", "tt", "u", "u_ev", "ue",
    "x2", "x4", "x_f1", "x_f2", "x_mix", "y", "y_centred", "y_mean", "y_sq", "y_var", "zh", "zh_mm",
)


def build(nc, io):
    SCB, SCC = DH ** -0.5, (DNOPE + DROPE) ** -0.5
    with ExitStack() as ctx:
        def sb(name, cols):
            return ctx.enter_context(nc.sbuf_tensor(name, [P, cols], F32))

        def sem(name):
            return ctx.enter_context(nc.semaphore(name))

        x = sb("x", KD * T)[:, :].rearrange("p (k t) -> p k t", k=KD)
        h = sb("h", KD * T)[:, :].rearrange("p (k t) -> p k t", k=KD)
        cst = sb("cst", NCONST)
        par = sb("par", NPAR)
        kvn = sb("kvn", KV_LORA)
        ya, yb, yc = [sb(n, 4 * T)[:, :].rearrange("p (k t) -> p k t", k=4) for n in ("ya", "yb", "yc")]
        lora = sb("lora", 2 * W_A)
        sml = sb("sml", 16)
        big = sb("big", 7680)
        ring = sb("ring", NSLOT * SLOT)
        reg = sb("reg", 17408)
        ptab = ctx.enter_context(nc.sbuf_tensor("ptab", [1, NB * N_PAGES], I32))
        ps = ctx.enter_context(nc.psum_tensor("ps", [P, 8, 512], F32))

        def C(name, rows=P):
            at, w = CONST[name]
            return cst[0:rows, at:at + w]

        def pp(name, m, rows=P):
            return par[0:rows, PAR[name][0] + m:PAR[name][0] + m + 1]

        def cut(buf, at, a, b, rows=P):
            return buf[0:rows, at:at + a * b].rearrange("p (a b) -> p a b", a=a)

        ident, ones, onesblk = C("ident"), C("ones"), C("onesblk")
        act_t = cut(big, 0, KF, T)
        sqb = cut(big, 0, KD, T)
        yt = cut(reg, 0, KD, T)
        sg2 = cut(reg, 2560, 2, T)
        rstd = reg[:, 3200:3200 + T]
        gates = cut(big, 0, 24, T)
        mt = cut(reg, 4096, KD, T)
        pa = cut(reg, 0, NAT, PADT)
        xs = cut(big, 0, NAT, T)
        S_ = [cut(reg, NAT * PADT + 1280 * i, 4, T) for i in range(10)]
        th, sgd = reg[:, 0:T], reg[:, T:2 * T]
        Hp = cut(reg, 640, H, DH, 64)
        Ue, Ve, Tm = [cut(reg, 1152 + 512 * i, NB, DH, CHUNK) for i in range(3)]
        Odd = [cut(reg, 2688 + 256 * i, 4, CHUNK, 64) for i in range(5)]
        MX = [cut(ring, 512 * i, H, CHUNK, CHUNK) for i in range(20)]
        (X8, X8T, Xo16, Xo32, Xo64, KK, RB, RK, X2, X2T, X4, Pm, Tt, TT, G, RHS, U, Vr, bdr, kdr) = MX
        Hse, Hso = cut(ring, 10240, 4, NB * DH, 64), cut(big, NAT * T, 4, NB * DH, 64)
        Hs = lambda hd: (Hso if hd % 2 else Hse)[:, hd // 2, :]
        lastT = cut(reg, 16126, NAT, 9)
        shin = cut(reg, 16326, NAT, NB)
        PBc = cut(reg, 0, 3, C_COLS)
        PBq = cut(reg, 2016, 3, 2048)
        PBv = cut(reg, 8160, 3, W_A)
        qT = cut(reg, 9696, 12, T)
        kT = cut(reg, 13536, 4, T)
        rt = reg[:, 14816:14816 + 1024]
        Sp = [big[:, 768 * i:768 * i + 768].rearrange("p (g k) -> p g k", g=3) for i in range(2)]
        Pc = [big[:, 1536 + 256 * i:1792 + 256 * i] for i in range(2)]
        PTp = [cut(big, 2048 + 256 * i, 2, P) for i in range(2)]
        OLp = [cut(big, 2560 + 256 * i, 2, P) for i in range(2)]
        Kw = cut(big, 0, SW_TILES, W_A)
        Qbd = big[:, 6656:6656 + 768].rearrange("p (c g n) -> p c g n", c=4, g=3)
        Vw = cut(ring, 0, SW_TILES, W_A)
        Sw = ring[0:NS, 6656:6656 + SW_COLS]
        KTw = cut(ring, 8344, 4, 512)
        PTw = cut(ring, 10392, SW_TILES, NS)
        PTn = ring[0:NS, 11224:11224 + NS]
        PnF = ring[0:NS, 11288:11288 + NS]
        cqT = cut(reg, 2016, 3, T)
        cup = cut(reg, 2976, 3, H * 96)
        kvup = cut(reg, 5280, 2, 1024)
        qrow = cut(reg, 7328, 3, H * 96)
        qcT = cut(reg, 9632, H, T)
        kvT = cut(reg, 12192, H, KV_LORA, DNOPE)
        ckvT = cut(reg, 16448, 3, T)
        rt2 = reg[:, 14240:14240 + 1024]
        olT = rt2.rearrange("p (c h t) -> p c h t", c=2, h=H)
        QR = reg[:, 15264:15264 + 512].rearrange("p (b h j) -> p b h j", b=NB, h=H)
        Osb = reg[0:NS, 15776:15776 + 256]
        PnL = reg[0:NS, 16032:16032 + NS]
        PTl = reg[0:NS, 16096:16096 + NS]
        KR = cut(big, 0, N_PAGES, 288)
        qlT = ring[:, 0:4096].rearrange("p (h c t) -> p h c t", h=H, c=2)
        QL = ring[:, 4096:5120].rearrange("p (c b n) -> p c b n", c=2, b=NB)
        KTl = [cut(ring, 5120 + 1536 * i, 3, 512) for i in range(2)]
        Pl = ring[0:NS, 8192:8192 + PAST + TS]
        PTL = cut(ring, 10304, N_PAGES, NS)

        s_dve = sem("vector_step")
        s_par, s_sml, s_out = sem("params_in"), sem("small_in"), sem("rows_out")
        s_slot = [sem(f"weights_in_{i}") for i in range(NSLOT)]
        s_kw, s_vw, s_kr, s_copy = sem("window_keys_in"), sem("window_values_in"), sem("pages_in"), sem("window_copied")
        s_shin, s_shout, s_state, s_wkv = sem("shift_in"), sem("shift_out"), sem("states_in"), sem("states_out")
        s_once, s_arrive, s_go, s_pad = sem("constants_in"), sem("engines_at_layer_end"), sem("layer_begun"), sem("pad")
        S = {n: sem(n) for n in STEPS}
        per_layer = [s_dve, s_par, s_sml, s_out, s_kw, s_vw, s_kr, s_state, s_wkv, s_shin, s_shout] + s_slot + list(S.values())
        units = weight_units(io)
        uidx = {name: i for i, (name, _) in enumerate(units)}

        def landed(name):
            i = uidx[name]
            return s_slot[i % NSLOT], 16 * sum(len(units[j][1]) for j in range(i % NSLOT, i + 1, NSLOT))

        def used(name):
            kind, u = name[0], name[-1]
            if kind in ("f1", "f2"):
                return (S["ffn_gu"], FFN0[kind] + 2 * u + 2) if name[1] == "gu" else (S["down_d"], DOWN0[kind] + u + 1)
            return {"pa": lambda: (S["pam"], min(4 * u + 4, NAT)), "pbc": lambda: (S["pbc_mm"], 3 * u + 3),
                    "pg": lambda: (S["pgm"], 4 * u + 4), "br": lambda: (S["brm"], KD * "abc".index(str(u)) + KD),
                    "wo": lambda: (S["down_d"], DOWN0["mix"] + 4 * u + 4)}[kind]()

        def wslot(name, k, n, at=0):
            o = (uidx[name] % NSLOT) * SLOT + at
            return ring[:, o:o + k * n].rearrange("p (k n) -> p k n", k=k)

        def layer_end(eng, l):
            eng.sem_inc(s_arrive, 1)
            eng.wait_ge(s_go, l + 1)
            eng.sem_inc(s_pad, 1)

        def lay(ap, l):
            return ap[bass.ds(l, 1)]

        block = ctx.enter_context(nc.Block())

        def rwkv_sync(sp, l):
            sp.wait_ge(S["pa_zeroed"], 1)
            sp.dma_start(shin, lay(io["shiftT"], l).rearrange("a p n b -> p (a n) b")).then_inc(s_shin, 16)
            sp.wait_ge(*used(("pa", 3)))
            for r, buf in ((0, Hse), (1, Hso)):
                sp.dma_start(buf, lay(io["wkvT"], l)[:, r].rearrange("a p n v -> p (a n) v")).then_inc(s_state, 16)
            sp.wait_ge(S["last_rows"], 1)
            sp.dma_start(lay(io["o_shift"], l).rearrange("a p n b -> p (a n) b"), lastT).then_inc(s_shout, 16)
            sp.wait_ge(S["group"], 5)
            sp.dma_start(lay(io["o_wkv_p"], l).rearrange("a p n v -> p (a n) v"), Hp).then_inc(s_wkv, 16)
            for r, buf in ((0, Hse), (1, Hso)):
                sp.dma_start(lay(io["o_wkv_s"], l)[:, r].rearrange("a p n v -> p (a n) v"), buf).then_inc(s_wkv, 16)
            sp.wait_ge(S["rwkv_done"], 1)
            sp.wait_ge(s_wkv, 16 * 3)

        def attention_sync(sp, l):
            sp.wait_ge(S["rows_ready"], 3)
            for name, src in (("swa_k", PBq[:, :, 1536:2048]), ("swa_v", PBv), ("ckv", PBc[:, :, Q_LORA:Q_LORA + KV_LORA]),
                              ("krope", PBc[:, :, Q_LORA + KV_LORA:C_COLS])):
                sp.dma_start(lay(io[f"o_{name}_p"], l).rearrange("a b (t p) n -> p (a b t) n", p=P), src[:, 0:2, :]).then_inc(s_out, 16)
                if name.startswith("swa"):
                    for b in range(NB):
                        dst = lay(io[f"o_{name}_s"], l)[:, b, PAST - TS:PAST, :].rearrange("a r n -> (a r) n")
                        sp.dma_start(dst, src[TS * b:TS * b + TS, 2, :]).then_inc(s_out, 16)
                else:
                    dst = lay(io[f"o_{name}_s"], l).rearrange("a b t n -> (a b t) n")
                    sp.dma_start(dst, src[0:NS, 2, :]).then_inc(s_out, 16)
            sp.wait_ge(S["prompt_y"], 16)
            for b in range(NB):
                for cache, sem_in, buf, tag in ((io["cache_swa_k"], s_kw, Kw, "K"), (io["cache_swa_v"], s_vw, Vw, "V")):
                    src = lay(cache, l)[:, b]
                    if b:
                        if tag == "K":
                            sp.wait_ge(S["kt_T"], 16 * b)
                        else:
                            sp.wait_ge(S["sw_pv"], b)
                    sp.dma_start(buf[:, 0:8, :], src.rearrange("a (p r) n -> p (a r) n", r=16)[:, 0:8, :]).then_inc(sem_in, 16)
                    sp.dma_start(buf[:, 8:12, :], src[:, PAST - 512:PAST].rearrange("a (p r) n -> p (a r) n", r=4)).then_inc(sem_in, 16)
                    sp.dma_start(buf[:, 12:13, :], src[:, PAST - P:PAST].rearrange("a p n -> p a n")).then_inc(sem_in, 16)
            sp.wait_ge(S["sws_done"], NB)
            sp.wait_ge(s_out, N_ROWS_OUT)
            sp.dma_start(cup, lay(io["c_q_up"], l).rearrange("a (k p) n -> p (a k) n", p=P)).then_inc(s_sml, 16)
            sp.dma_start(kvup, lay(io["c_kv_up"], l).rearrange("a (k p) n -> p (a k) n", p=P)).then_inc(s_sml, 16)
            for b in range(NB):
                if b == 0:
                    sp.wait_ge(S["prompt_y"], 2 * H + 16)
                else:
                    sp.wait_ge(S["ml_pv"], b)
                for n in range(N_PAGES):
                    i = b * N_PAGES + n
                    page = sp.value_load(ptab[0:1, i:i + 1], min_val=0, max_val=N_POOL - 1)
                    for c0, cache, w in ((0, "ckv", KV_LORA), (KV_LORA, "krope", DROPE)):
                        src = lay(io["cache_mla_" + cache], l)[:, bass.ds(page, 1)].rearrange("a b p n -> p (a b n)")
                        sp.dma_start(KR[:, n, c0:c0 + w], src).then_inc(s_kr, 16)
            sp.wait_ge(S["ml_done"], 1)

        @block.sync
        def _(sp):
            sp.dma_start(cst[:, :], io["consts"]).then_inc(s_once, 16)
            sp.dma_start(x, io["xT"]).then_inc(s_once, 16)
            sp.dma_start(ptab[:, :], io["page_table"].rearrange("b n -> (b n)").unsqueeze(0)).then_inc(s_once, 16)
            sp.wait_ge(s_once, 48)
            with sp.Fori(0, DEPTH) as l:
                sp.dma_start(par[:, :], lay(io["params"], l).rearrange("a p n -> p (a n)")).then_inc(s_par, 16)
                sp.dma_start(kvn[:, :], lay(io["c_kv_norm"], l).rearrange("a n -> (a n)").partition_broadcast(P)).then_inc(s_par, 16)
                for lo, hi, name in ((0, 32, "a_w2"), (32, 64, "a_a2")):
                    sp.dma_start(lora[lo:hi, 0:W_A], lay(io[name], l).rearrange("a p n -> p (a n)")).then_inc(s_par, 16)
                sp.dma_start(lora[0:96, W_A:2 * W_A], lay(io["a_g2"], l).rearrange("a p n -> p (a n)")).then_inc(s_par, 16)
                for i, (name, srcs) in enumerate(units):
                    if name == ("pbc", 0):
                        rwkv_sync(sp, l)
                    if name == ("pg", 0):
                        attention_sync(sp, l)
                    if i >= NSLOT:
                        sp.wait_ge(*used(units[i - NSLOT][0]))
                    at = (i % NSLOT) * SLOT
                    for src, k, n in srcs:
                        sp.dma_start(ring[:, at:at + k * n].rearrange("p (k n) -> p k n", k=k), src(l)).then_inc(s_slot[i % NSLOT], 16)
                        at += k * n
                sp.wait_ge(S["x_f2"], 1)
                sp.wait_ge(S["roots"], ROOTS["f2_post"])
                sp.wait_ge(S["norm_sums"], NORMS["f2_post"])
                sp.wait_ge(s_out, N_ROWS_OUT)
                sp.wait_ge(s_wkv, 16 * 3)
                sp.wait_ge(s_shout, 16)
                sp.wait_ge(s_arrive, 4 * (l + 1))
                sp.sem_inc(s_pad, 1)
                for s in per_layer:
                    sp.sem_clear(s)
                sp.sem_inc(s_go, 1)
            sp.dma_start(io["yT"], x).then_inc(s_once, 16)
            sp.wait_ge(s_once, 64)

        @block.gpsimd
        def _(pool):
            with pool.Fori(0, DEPTH) as l:
                rows = PAST - TS
                for b in range(NB):
                    for n in ("k", "v"):
                        src = lay(io["cache_swa_" + n], l)[:, b, TS:PAST].rearrange("a r n -> (a r n)")
                        dst = lay(io[f"o_swa_{n}_s"], l)[:, b, 0:rows].rearrange("a r n -> (a r n)")
                        pool.dma_start(dst.rearrange("(q n) -> q n", q=240),
                                       src.rearrange("(q n) -> q n", q=240)).then_inc(s_copy, 16)
                pool.wait_ge(s_copy, (l + 1) * (16 * 2 * NB))
                layer_end(pool, l)

        @block.tensor
        def _(pe):
            pe.wait_ge(s_once, 48)

            def mm(out, lhsT, rhs, first=True, last=True):
                return pe.matmul(out, lhsT, rhs, start=first, stop=last, skip_group_check=True)

            def tr(out, in_, rows=P):
                return pe.transpose(out, in_, ident[0:rows, 0:rows])


            def norm_sum(tag, src):
                for k in range(KD):
                    m = mm(ps[:, 7, 0:T], ones, src[:, k, :], k == 0, k == KD - 1)
                m.then_inc(S["norm_sums"], 1)

            def ffn(f):
                pe.wait_ge(S["squared"], PRES[f + "_pre"])
                norm_sum(f + "_pre", sqb)
                pe.wait_ge(S["normed"], PRES[f + "_pre"])
                for m in range(KF):
                    u = (f, "gu", m // 2)
                    pe.wait_ge(*landed(u))
                    if m >= 3:
                        pe.wait_ge(S["ffn_a"], FFN0[f] + m - 2)
                    for bank, at in ((m % 3, 0), (3 + m % 3, 2048)):
                        w = wslot(u, KD, 256, at)
                        for k in range(KD):
                            q = mm(ps[:, bank, 0:T], w[:, k, (m % 2) * P:(m % 2) * P + P], h[:, k, :], k == 0, k == KD - 1)
                    q.then_inc(S["ffn_gu"], 1)
                pe.wait_ge(S["ffn_a"], FFN0[f] + KF)
                for m in range(KD):
                    u = (f, "d", m)
                    pe.wait_ge(*landed(u))
                    if m >= 4:
                        pe.wait_ge(S["down_y"], DOWN0[f] + m - 3)
                    w = wslot(u, KF, P)
                    for k in range(KF):
                        q = mm(ps[:, m % 4, 0:T], w[:, k, :], act_t[:, k, :], k == 0, k == KF - 1)
                    q.then_inc(S["down_d"], 1)
                pe.wait_ge(S["down_y"], DOWN0[f] + KD)
                norm_sum(f + "_post", h)

            def a_proj():
                pe.wait_ge(S["squared"], PRES["mix_pre"])
                norm_sum("mix_pre", sqb)
                pe.wait_ge(S["normed"], PRES["mix_pre"])
                for m, (c0, rows) in enumerate(A_TILES):
                    u = ("pa", min(c0 // 512, 3))
                    pe.wait_ge(*landed(u))
                    if m >= 6:
                        pe.wait_ge(S["pa"], m - 5)
                    n = 512 if c0 < 1536 else 160
                    w, at = wslot(u, KD, n), c0 - 512 * (c0 // 512)
                    for k in range(KD):
                        q = mm(ps[0:rows, m % 6, 0:T], w[:, k, at:at + rows], h[:, k, :], k == 0, k == KD - 1)
                    q.then_inc(S["pam"], 1)

            def rwkv():
                pe.wait_ge(S["tanh"], 1)
                for m in range(4):
                    mm(ps[:, m, 0:T], lora[0:32, m * P:m * P + P], th[0:32, :])
                    q = mm(ps[:, 4 + m, 0:T], lora[32:64, m * P:m * P + P], xs[32:64, 12, :])
                q.then_inc(S["lora_wa"], 1)
                pe.wait_ge(S["a_ready"], 4)
                for m in range(4):
                    q = mm(ps[:, m, 0:T], lora[0:96, W_A + m * P:W_A + m * P + P], sgd[0:96, :])
                q.then_inc(S["lora_g"], 1)
                pe.wait_ge(S["kk_sq"], 1)
                for m in range(4):
                    q = mm(ps[:, 4 + m, 0:T], onesblk, S_[9][:, m, :])
                q.then_inc(S["kk_ss"], 1)
                pe.wait_ge(S["bonus_in"], 1)
                pe.wait_ge(S["g_ready"], 1)
                for m in range(4):
                    q = mm(ps[:, m, 0:T], onesblk, S_[9][:, m, :])
                q.then_inc(S["bonus_ss"], 1)
                pe.wait_ge(S["streams"], 1)
                ZT, bdT, kdT, RqT, vT = S_[6], S_[0], S_[7], S_[3], xs[:, 8:12]
                for g in range(5):
                    t0, sample = g * CHUNK, g == 4
                    odd = {id(ZT): Odd[0], id(bdT): Odd[1], id(kdT): Odd[2], id(RqT): Odd[3]}
                    at = lambda a, hd: odd[id(a)][:, hd // 2, :] if hd % 2 else a[0:64, hd // 2, t0:t0 + CHUNK]
                    bank = lambda b, hd: ps[0:64, b, 64 * hd:64 * hd + 64]

                    def each(b, name, f):
                        for hd in range(H):
                            q = f(bank(b, hd), hd)
                        if name is not None:
                            q.then_inc(S[name], 1)

                    if g:
                        pe.wait_ge(S["group"], g)
                    for b, a in ((0, vT), (1, bdT), (2, kdT)):
                        for m in range(4):
                            q = tr(ps[0:64, b, m * P:m * P + P], a[:, m, t0:t0 + CHUNK])
                    q.then_inc(S["rows"], 1)
                    pe.wait_ge(S["odd"], 5 * g + 5)
                    each(3, None, lambda o, hd: mm(o, at(ZT, hd), at(bdT, hd)))
                    each(4, None, lambda o, hd: mm(o, at(bdT, hd), at(ZT, hd)))
                    each(5, None, lambda o, hd: mm(o, at(kdT, hd), at(ZT, hd)))
                    each(6, None, lambda o, hd: mm(o, at(bdT, hd), at(RqT, hd)))
                    each(7, "RK", lambda o, hd: mm(o, at(kdT, hd), at(RqT, hd)))
                    pe.wait_ge(S["masked"], g + 1)
                    each(0, None, lambda o, hd: mm(o, X8T[:, hd], X8[:, hd]))
                    each(1, "X2T", lambda o, hd: mm(o, X8[:, hd], X8T[:, hd]))
                    pe.wait_ge(S["x2"], g + 1)
                    each(2, "X4", lambda o, hd: mm(o, X2T[:, hd], X2[:, hd]))
                    pe.wait_ge(S["x4"], g + 1)
                    each(3, "X6", lambda o, hd: mm(o, X2T[:, hd], X4[:, hd]))
                    pe.wait_ge(S["pm"], g + 1)
                    each(4, "XP", lambda o, hd: mm(o, X8T[:, hd], Pm[:, hd]))
                    pe.wait_ge(S["t"], g + 1)
                    each(5, "TT", lambda o, hd: tr(o, Tt[:, hd], 64))
                    pe.wait_ge(S["tt"], g + 1)
                    if not sample:
                        for i, xo in enumerate((Xo16, Xo32, Xo64)):
                            each(0, "G", lambda o, hd: mm(o, xo[:, hd], Tt[:, hd]))
                            pe.wait_ge(S["g_level" ], 3 * g + i + 1)
                            each(1, None, lambda o, hd: mm(o, TT[:, hd], G[:, hd]))
                            each(2, "dTT", lambda o, hd: mm(o, G[:, hd], TT[:, hd]))
                            pe.wait_ge(S["t_level" ], 3 * g + i + 1)
                        for hd in range(H):
                            mm(bank(3, hd), at(ZT, hd), Hp[:, hd, :], True, False)
                            q = mm(bank(3, hd), KK[:, hd], Vr[:, hd], False, True)
                        q.then_inc(S["rhs"], 1)
                    else:
                        pe.wait_ge(s_state, 32)
                        for hd in range(H):
                            if hd >= 2:
                                pe.wait_ge(S["zh"], hd - 1)
                            mm(ps[0:64, hd % 2, :], at(ZT, hd), Hs(hd)).then_inc(S["zh_mm"], 1)
                        each(3, "rhs", lambda o, hd: mm(o, KK[:, hd], Vr[:, hd]))
                    pe.wait_ge(S["rhs_ev"], g + 1)
                    each(4, "u", lambda o, hd: mm(o, TT[:, hd], RHS[:, hd]))
                    pe.wait_ge(S["u_ev"], g + 1)
                    for hd in range(H):
                        r0 = 64 * (hd % 2)
                        o = ps[r0:r0 + 64, 5, 64 * (hd // 2):64 * (hd // 2) + 64]
                        mm(o, U[:, hd], RB[:, hd], True, False)
                        q = mm(o, Vr[:, hd], RK[:, hd], False, False)
                        if not sample:
                            q = mm(o, Hp[:, hd, :], at(RqT, hd), False, True)
                        else:
                            for b in range(NB):
                                q = mm(o[:, TS * b:TS * b + TS], Hs(hd)[:, DH * b:DH * b + DH],
                                       at(RqT, hd)[:, TS * b:TS * b + TS], False, b == NB - 1)
                    q.then_inc(S["y"], 1)
                    if not sample:
                        for hd in range(H):
                            o = bank(6, hd)
                            mm(o, bdr[:, hd], U[:, hd], True, False)
                            q = mm(o, kdr[:, hd], Vr[:, hd], False, True)
                        q.then_inc(S["h"], 1)
                    else:
                        for hd in range(H):
                            pe.wait_ge(S["ue"], hd + 1)
                            mm(ps[0:64, 6 + hd % 2, :], bdr[:, hd], Ue.rearrange("p b v -> p (b v)"), True, False)
                            q = mm(ps[0:64, 6 + hd % 2, :], kdr[:, hd], Ve.rearrange("p b v -> p (b v)"), False, True)
                            q.then_inc(S["hs"], 1)
                Y = S_[8]
                pe.wait_ge(S["group"], 5)
                for m in range(4):
                    q = mm(ps[:, m, 0:T], onesblk, Y[:, m, :])
                q.then_inc(S["y_mean"], 1)
                pe.wait_ge(S["y_sq"], 1)
                for m in range(4):
                    q = mm(ps[:, 4 + m, 0:T], onesblk, S_[0][:, m, :])
                q.then_inc(S["y_var"], 1)

            def bc_proj():
                pe.wait_ge(S["rwkv_done"], 1)
                n = 0
                for u in range(7):
                    pe.wait_ge(*landed(("pbc", u)))
                    cols = 160 if u == 1 else 512
                    w = wslot(("pbc", u), KD, cols)
                    for i, t0, rows in TOK_TILES:
                        if n >= 6:
                            pe.wait_ge(S["pbc_ev"], n - 5)
                        for k in range(KD):
                            q = mm(ps[0:rows, n % 6, 0:cols], h[:, k, t0:t0 + rows], w[:, k, :], k == 0, k == KD - 1)
                        q.then_inc(S["pbc_mm"], 1)
                        n += 1
                pe.wait_ge(S["rows_ready"], 3)
                n = 0
                for c in range(16):
                    if c >= 4:
                        pe.wait_ge(S["qk_ev"], c - 3)
                    for i, t0, rows in TOK_TILES:
                        q = tr(ps[:, c % 4, t0:t0 + rows], PBq[0:rows, i, c * P:c * P + P], rows)
                    q.then_inc(S["qkT"], 1)
                pe.wait_ge(S["qk_ev"], 16)
                for j, c0 in enumerate((Q_LORA, Q_LORA + P, C_COLS - 96)):
                    w = 96 if j == 2 else P
                    for i, t0, rows in TOK_TILES:
                        q = tr(ps[0:w, j, t0:t0 + rows], PBc[0:rows, i, c0:c0 + w], rows)
                q.then_inc(S["ckvT"], 1)

            def sw_prompt():
                pe.wait_ge(S["ckvT_ev"], 1)

                def scores(n):
                    t, hd = n // H, n % H
                    r0 = 64 * (hd % 2)
                    if n >= 2:
                        pe.wait_ge(S["prompt_s"], n - 1)
                    for g in range(3):
                        col = (n % 2) * 1024 + g * 256
                        o = ps[:, col // 512, col % 512:col % 512 + 256]
                        q = mm(o, qT[r0:r0 + 64, 4 * g + hd // 2, t * P:t * P + P], kT[r0:r0 + 64, hd // 2, 0:SEQ])
                    q.then_inc(S["prompt_mm"], 1)

                scores(0)
                for n in range(16):
                    if n + 1 < 16:
                        scores(n + 1)
                    hd = n % H
                    pe.wait_ge(S["prompt_p"], n + 1)
                    for i in range(2):
                        q = tr(ps[:, 4 + n % 2, i * P:i * P + P], Pc[n % 2][:, i * P:i * P + P])
                    q.then_inc(S["prompt_T"], 1)
                    pe.wait_ge(S["prompt_pt"], n + 1)
                    r0 = 64 * (hd % 2)
                    for i in range(2):
                        q = mm(ps[r0:r0 + 64, 6 + n % 2, 0:P], PBv[:, i, hd * 64:hd * 64 + 64], PTp[n % 2][:, i, :], i == 0, i == 1)
                    q.then_inc(S["prompt_o"], 1)

            def sw_sample():
                pe.wait_ge(S["prompt_y"], 16)
                for b in range(NB):
                    pe.wait_ge(s_kw, 48 * (b + 1))
                    pe.wait_ge(S["qbd"], 8 * b + 8)
                    for q4 in range(4):
                        nt = 4 if q4 < 3 else 1
                        g = 2 if q4 < 2 else 1 if q4 == 2 else 0
                        for c in range(4):
                            n = 16 * b + 4 * q4 + c
                            if n >= 2:
                                pe.wait_ge(S["kt_ev"], n - 1)
                            for t in range(nt):
                                q = tr(ps[:, 4 + n % 2, t * P:t * P + P], Kw[:, 4 * q4 + t, c * P:c * P + P])
                            q.then_inc(S["kt_T"], 1)
                        if b and q4 == 0:
                            pe.wait_ge(S["sw_masked"], b)
                        for c in range(4):
                            pe.wait_ge(S["kt_ev"], 16 * b + 4 * q4 + c + 1)
                            q = mm(ps[0:NS, q4, 0:nt * P], Qbd[:, c, g, :], KTw[:, c, 0:nt * P], c == 0, c == 3)
                        q.then_inc(S["sw_mm"], 1)
                    for g in range(3):
                        for c in range(4):
                            q = mm(ps[0:NS, 3, P + g * TS:P + g * TS + TS], Qbd[:, c, g, :],
                                   kT[:, c, SEQ + TS * b:SEQ + TS * b + TS], c == 0, c == 3)
                    q.then_inc(S["sw_s"], 1)
                    pe.wait_ge(S["sw_p"], b + 1)
                    for t in range(SW_TILES):
                        q = tr(ps[:, 6 + t // 8, (t % 8) * NS:(t % 8) * NS + NS], Sw[:, t * P:t * P + P], NS)
                    q = tr(ps[0:NS, 7, 320:384], PnF, NS)
                    q.then_inc(S["sw_PT"], 1)
                    pe.wait_ge(S["sw_pt"], b + 1)
                    pe.wait_ge(s_vw, 48 * (b + 1))
                    for c in range(4):
                        o = ps[:, 7, 448 + 16 * c:464 + 16 * c]
                        for t in range(SW_TILES):
                            mm(o, Vw[:, t, c * P:c * P + P], PTw[:, t, 16 * c:16 * c + 16], t == 0, False)
                        q = mm(o, PBv[0:NS, 2, c * P:c * P + P], PTn[:, 16 * c:16 * c + 16], False, True)
                    q.then_inc(S["sw_pv"], 1)

            def latent_prep():
                pe.wait_ge(S["sws_done"], NB)
                for k in range(3):
                    for i, t0, rows in TOK_TILES:
                        q = tr(ps[:, k, t0:t0 + rows], PBc[0:rows, i, k * P:k * P + P], rows)
                q.then_inc(S["cqT"], 1)
                pe.wait_ge(s_sml, 32)
                for hd in range(H):
                    for c in range(2):
                        q = tr(ps[:, 3 + hd // 2, (hd % 2) * 256 + c * P:(hd % 2) * 256 + c * P + P], kvup[:, c, hd * P:hd * P + P])
                q.then_inc(S["kvT"], 1)
                pe.wait_ge(S["kvT_ev"], 1)
                n = 0
                for i, t0, rows in TOK_TILES:
                    for j in range(2):
                        for k in range(3):
                            q = mm(ps[0:rows, n, 0:384], cqT[:, k, t0:t0 + rows], cup[:, k, j * 384:j * 384 + 384], k == 0, k == 2)
                        n += 1
                q.then_inc(S["q_rows"], 1)
                pe.wait_ge(S["q_rope"], 3)
                for hd in range(H):
                    if hd >= 4:
                        pe.wait_ge(S["qcT_ev"], hd - 3)
                    for i, t0, rows in TOK_TILES:
                        q = tr(ps[0:96, hd % 4, t0:t0 + rows], qrow[0:rows, i, hd * 96:hd * 96 + 96], rows)
                    q.then_inc(S["qcT"], 1)
                for n in range(16):
                    pe.wait_ge(S["qcT_ev"], max(n // 2, 7) + 1)
                    if n >= 4:
                        pe.wait_ge(S["ql_ev"], n - 3)
                    mm(ps[:, 4 + n % 4, 0:T], kvT[:, n // 2, (n % 2) * P:(n % 2) * P + P], qcT[0:64, n // 2, :]).then_inc(S["ql"], 1)

            def ml_prompt():
                pe.wait_ge(S["ml_prep"], 1)

                def scores(n):
                    t, hd = n // H, n % H
                    if n >= 2:
                        pe.wait_ge(S["prompt_s"], 2 * H + n - 1)
                    o = ps[:, n % 2, 0:SEQ]
                    for c in range(2):
                        mm(o, qlT[:, hd, c, t * P:t * P + P], ckvT[:, c, 0:SEQ], c == 0, False)
                    mm(o, qcT[64:96, hd, t * P:t * P + P], ckvT[64:96, 2, 0:SEQ], False, True).then_inc(S["prompt_mm"], 1)

                scores(0)
                for n in range(16):
                    if n + 1 < 16:
                        scores(n + 1)
                    hd = n % H
                    pe.wait_ge(S["prompt_p"], 2 * H + n + 1)
                    for i in range(2):
                        q = tr(ps[:, 2 + n % 2, i * P:i * P + P], Pc[n % 2][:, i * P:i * P + P])
                    q.then_inc(S["prompt_T"], 1)
                    pe.wait_ge(S["prompt_pt"], 2 * H + n + 1)
                    for c in range(2):
                        for i in range(2):
                            q = mm(ps[:, 4 + n % 2, c * P:c * P + P], PBc[:, i, Q_LORA + c * P:Q_LORA + c * P + P],
                                   PTp[n % 2][:, i, :], i == 0, i == 1)
                    q.then_inc(S["prompt_ol"], 1)
                    pe.wait_ge(S["prompt_olev"], n + 1)
                    r0 = 64 * (hd % 2)
                    for c in range(2):
                        q = mm(ps[r0:r0 + 64, 6 + n % 2, 0:P], kvup[:, c, hd * P + 64:hd * P + P], OLp[n % 2][:, c, :], c == 0, c == 1)
                    q.then_inc(S["prompt_o"], 1)

            def ml_sample():
                pe.wait_ge(S["prompt_y"], 2 * H + 16)
                for b in range(NB):
                    pe.wait_ge(s_kr, 16 * 2 * N_PAGES * (b + 1))
                    for t in range(N_PAGES):
                        n = 16 * b + t
                        if n >= 2:
                            pe.wait_ge(S["lt_odd" if n % 2 else "lt_even"], n // 2)
                        o = ps[:, 5 + n % 2, :]
                        tr(o[:, 0:P], KR[:, t, 0:P])
                        tr(o[:, P:2 * P], KR[:, t, P:2 * P])
                        tr(o[0:96, 2 * P:3 * P], KR[:, t, 192:288]).then_inc(S["lt_T"], 1)
                        if t % 4 == 3:
                            q4 = t // 4
                            if b and q4 == 0:
                                pe.wait_ge(S["ml_exp"], b)
                            pe.wait_ge(S["lt_even"], n // 2 + 1)
                            pe.wait_ge(S["lt_odd"], n // 2 + 1)
                            kt = KTl[(n // 4) % 2]
                            for c in range(2):
                                mm(ps[0:NS, q4, :], QL[:, c, b, :], kt[:, c, :], c == 0, False)
                            mm(ps[0:NS, q4, :], QR[64:96, b].rearrange("p h j -> p (h j)"), kt[64:96, 2, :], False, True).then_inc(S["ml_mm"], 1)
                    o = ps[0:NS, 4, 0:TS]
                    tk = slice(SEQ + TS * b, SEQ + TS * b + TS)
                    for c in range(2):
                        mm(o, QL[:, c, b, :], ckvT[:, c, tk], c == 0, False)
                    mm(o, QR[64:96, b].rearrange("p h j -> p (h j)"), ckvT[64:96, 2, tk], False, True).then_inc(S["ml_s"], 1)
                    pe.wait_ge(S["ml_p"], b + 1)
                    for half in range(2):
                        if half:
                            pe.wait_ge(S["ml_pt"], 3 * b + 1)
                        for t in range(8):
                            tt = 8 * half + t
                            q = tr(ps[:, 7, t * NS:t * NS + NS], Pl[:, tt * P:tt * P + P], NS)
                        q.then_inc(S["ml_PT"], 1)
                    pe.wait_ge(S["ml_pt"], 3 * b + 2)
                    tr(ps[0:NS, 7, 0:NS], PnL, NS).then_inc(S["ml_PT"], 1)
                    pe.wait_ge(S["ml_pt"], 3 * b + 3)
                    o = ps[0:NS, 4, 256:512]
                    for t in range(N_PAGES):
                        mm(o, PTL[:, t, :], KR[:, t, 0:KV_LORA], t == 0, False)
                    mm(o, PTl, PBc[0:NS, 2, Q_LORA:Q_LORA + KV_LORA], False, True).then_inc(S["ml_pv"], 1)
                    pe.wait_ge(S["ml_osb"], b + 1)
                    for c in range(2):
                        q = tr(ps[:, 7, c * NS:c * NS + NS], Osb[:, c * P:c * P + P], NS)
                    q.then_inc(S["ml_oT"], 1)
                pe.wait_ge(S["ml_olT"], NB)
                for hd in range(H):
                    r0 = 64 * (hd % 2)
                    for c in range(2):
                        q = mm(ps[r0:r0 + 64, 0, (hd // 2) * NS:(hd // 2) * NS + NS], kvup[:, c, hd * P + 64:hd * P + P], olT[:, c, hd, :], c == 0, c == 1)
                q.then_inc(S["ml_yc"], 1)

            def mix():
                pe.wait_ge(S["ml_done"], 1)
                for m in range(24):
                    u = ("pg", m // 4)
                    pe.wait_ge(*landed(u))
                    if m >= 8:
                        pe.wait_ge(S["gate"], m - 7)
                    w = wslot(u, KD, 512)
                    for k in range(KD):
                        q = mm(ps[:, m % 8, 0:T], w[:, k, (m % 4) * P:(m % 4) * P + P], h[:, k, :], k == 0, k == KD - 1)
                    q.then_inc(S["pgm"], 1)
                pe.wait_ge(S["gate"], 24)
                for i, (br, y) in enumerate((("a", ya), ("b", yb), ("c", yc))):
                    u = ("br", br)
                    pe.wait_ge(*landed(u))
                    w = wslot(u, 4, D_MODEL)
                    for m in range(KD):
                        if 8 * i + m >= 8:
                            pe.wait_ge(S["br_ev"], 8 * i + m - 7)
                        for k in range(4):
                            q = mm(ps[:, m, 0:T], w[:, k, m * P:m * P + P], y[:, k, :], k == 0, k == 3)
                        q.then_inc(S["brm"], 1)
                pe.wait_ge(S["br_ev"], 24)
                for m in range(KD):
                    u = ("wo", m // 4)
                    pe.wait_ge(*landed(u))
                    if m >= 4:
                        pe.wait_ge(S["down_y"], DOWN0["mix"] + m - 3)
                    w = wslot(u, KD, 512)
                    for k in range(KD):
                        q = mm(ps[:, m % 4, 0:T], w[:, k, (m % 4) * P:(m % 4) * P + P], mt[:, k, :], k == 0, k == KD - 1)
                    q.then_inc(S["down_d"], 1)
                pe.wait_ge(S["down_y"], DOWN0["mix"] + KD)
                norm_sum("mix_post", h)

            with pe.Fori(0, DEPTH) as l:
                ffn("f1")
                a_proj()
                rwkv()
                bc_proj()
                sw_prompt()
                sw_sample()
                latent_prep()
                ml_prompt()
                ml_sample()
                mix()
                ffn("f2")
                layer_end(pe, l)

        @block.scalar
        def _(act):
            act.wait_ge(s_once, 48)

            def root(tag, v):
                act.wait_ge(S["mean_squares"], ROOTS[tag])
                act.activation(v, v, ACT.Sqrt).then_inc(S["roots"], 1)

            def square_x(tag):
                act.activation(sqb, x, ACT.Square).then_inc(S["squared"], 1)
                root(tag, rstd)

            def down(f):
                for m in range(KD):
                    act.wait_ge(S["down_d"], DOWN0[f] + m + 1)
                    act.activation(yt[:, m, :], ps[:, m % 4, 0:T], ACT.Copy)
                    act.activation(h[:, m, :], ps[:, m % 4, 0:T], ACT.Square).then_inc(S["down_y"], 1)
                root(f + "_post", rstd)

            def ffn(f):
                for m in range(KF):
                    act.wait_ge(S["ffn_gu"], FFN0[f] + m + 1)
                    if m >= 2:
                        act.wait_ge(S["ffn_a"], FFN0[f] + m - 1)
                    act.activation(sg2[:, m % 2, :], ps[:, m % 3, 0:T], ACT.Sigmoid).then_inc(S["ffn_sg"], 1)
                down(f)

            def rwkv():
                act.wait_ge(s_par, 16 * 5)
                act.wait_ge(S["pa_zeroed"], 1)
                for m, (_, rows) in enumerate(A_TILES):
                    act.wait_ge(S["pam"], m + 1)
                    act.activation(pa[0:rows, m, 1:1 + SEQ], ps[0:rows, m % 6, 0:SEQ], ACT.Copy)
                    act.activation(pa[0:rows, m, 1 + SEQ:].rearrange("p (b j) -> p b j", b=NB)[:, :, 1:], ps[0:rows, m % 6, SEQ:T].rearrange("p (b j) -> p b j", b=NB), ACT.Copy).then_inc(S["pa"], 1)
                act.wait_ge(S["mixed"], 1)
                act.activation(th[0:32, :], xs[0:32, 12, :], ACT.Tanh)
                act.activation(sgd[0:96, :], xs[0:96, 13, :], ACT.Sigmoid).then_inc(S["tanh"], 1)
                act.wait_ge(S["lora_wa"], 1)
                for m in range(4):
                    act.activation(S_[0][:, m, :], ps[:, m, 0:T], ACT.Sigmoid, bias=pp("a_w0", m))
                    act.activation(S_[1][:, m, :], ps[:, 4 + m, 0:T], ACT.Sigmoid, bias=pp("a_a0", m)).then_inc(S["a_ready"], 1)
                act.wait_ge(S["lora_g"], 1)
                act.activation(S_[2], ps[:, 0:4, 0:T], ACT.Copy).then_inc(S["g_ready"], 1)
                act.wait_ge(S["kk0"], 1)
                act.wait_ge(s_shout, 16)
                act.activation(S_[9], S_[8], ACT.Square).then_inc(S["kk_sq"], 1)
                act.wait_ge(S["L"], 1)
                act.activation(S_[5], S_[3], ACT.Exp)
                act.activation(S_[6], S_[4], ACT.Exp)
                act.activation(S_[7], S_[3], ACT.Exp, scale=-1.0).then_inc(S["exps"], 1)
                root("kk", S_[9])
                for g in range(5):
                    if g:
                        act.wait_ge(S["group"], g)
                    else:
                        act.wait_ge(S["streams"], 1)
                    for o, a in zip(Odd, (S_[6], S_[0], S_[7], S_[3], S_[5])):
                        act.activation(o, a[64:128, :, g * CHUNK:(g + 1) * CHUNK], ACT.Copy).then_inc(S["odd"], 1)
                act.wait_ge(S["y_centred"], 1)
                act.activation(S_[0], S_[8], ACT.Square).then_inc(S["y_sq"], 1)
                root("y", S_[1])

            def bc_proj():
                n = 0
                for u in range(7):
                    for i, _, rows in TOK_TILES:
                        act.wait_ge(S["pbc_mm"], n + 1)
                        dst = (PBc[0:rows, i, 0:512] if u == 0 else PBc[0:rows, i, 512:672] if u == 1 else
                               PBv[0:rows, i, :] if u == 6 else PBq[0:rows, i, (u - 2) * 512:(u - 1) * 512])
                        act.activation(dst, ps[0:rows, n % 6, 0:160 if u == 1 else 512], ACT.Copy).then_inc(S["pbc_ev"], 1)
                        n += 1
                act.wait_ge(S["latent_ms"], 6)
                act.activation(sml[:, 8:14], sml[:, 8:14], ACT.Sqrt).then_inc(S["latent_root"], 1)
                for c in range(16):
                    act.wait_ge(S["qkT"], c + 1)
                    act.activation(qT[:, c, :] if c < 12 else kT[:, c - 12, :], ps[:, c % 4, 0:T], ACT.Copy).then_inc(S["qk_ev"], 1)
                act.wait_ge(S["ckvT"], 1)
                act.activation(ckvT[:, 0:2, :], ps[:, 0:2, 0:T], ACT.Copy)
                act.activation(ckvT[0:96, 2, :], ps[0:96, 2, 0:T], ACT.Copy).then_inc(S["ckvT_ev"], 1)

            def sw_prompt():
                for n in range(16):
                    act.wait_ge(S["prompt_nm"], n + 1)
                    act.activation(Sp[n % 2], Sp[n % 2], ACT.Exp, scale=SCB, bias=sml[:, 2 + n % 2:3 + n % 2], accum_out=sml[:, 4 + n % 2:5 + n % 2]).then_inc(S["prompt_e"], 1)

            def sw_sample():
                for b in range(NB):
                    for n in range(16 * b, 16 * b + 16):
                        c, q4 = n % 4, (n // 4) % 4
                        w = P if q4 == 3 else 512
                        act.wait_ge(S["kt_T"], n + 1)
                        if n >= 4:
                            act.wait_ge(S["sw_mm"], n // 4)
                        act.activation(KTw[:, c, 0:w], ps[:, 4 + n % 2, 0:w], ACT.Copy).then_inc(S["kt_ev"], 1)
                    act.wait_ge(S["sw_nm"], b + 1)
                    act.activation(Sw, Sw, ACT.Exp, scale=SCB, bias=sml[0:NS, 2:3], accum_out=sml[0:NS, 4:5]).then_inc(S["sw_e"], 1)

            def latent_prep():
                act.wait_ge(S["q_rows"], 1)
                n = 0
                for i, _, rows in TOK_TILES:
                    for j in range(2):
                        act.activation(qrow[0:rows, i, j * 384:j * 384 + 384], ps[0:rows, n, 0:384], ACT.Copy).then_inc(S["qrow_ev"], 1)
                        n += 1
                for hd in range(H):
                    act.wait_ge(S["qcT"], hd + 1)
                    act.activation(qcT[0:96, hd, :], ps[0:96, hd % 4, 0:T], ACT.Copy).then_inc(S["qcT_ev"], 1)
                for n in range(16):
                    hd, c = n // 2, n % 2
                    act.wait_ge(S["ql"], n + 1)
                    act.activation(qlT[:, hd, c, :], ps[:, 4 + n % 4, 0:SEQ], ACT.Copy)
                    act.activation(QL[:, c, :, TS * hd:TS * hd + TS], ps[:, 4 + n % 4, SEQ:T].rearrange("p (b j) -> p b j", b=NB), ACT.Copy).then_inc(S["ql_ev"], 1)

            def ml_prompt():
                for n in range(16):
                    act.wait_ge(S["prompt_nm"], 2 * H + n + 1)
                    act.activation(Sp[n % 2][:, 0, :], Sp[n % 2][:, 0, :], ACT.Exp, scale=SCC, bias=sml[:, 2 + n % 2:3 + n % 2], accum_out=sml[:, 4 + n % 2:5 + n % 2]).then_inc(S["prompt_e"], 1)

            def ml_sample():
                for b in range(NB):
                    for n in range(16 * b, 16 * b + 16, 2):
                        act.wait_ge(S["lt_T"], n + 1)
                        if n >= 8:
                            act.wait_ge(S["ml_mm"], n // 4 - 1)
                        kt = KTl[(n // 4) % 2][:, :, (n % 4) * P:(n % 4) * P + P]
                        act.activation(kt[:, 0:2, :], ps[:, 5 + n % 2, 0:2 * P].rearrange("p (c k) -> p c k", c=2), ACT.Copy)
                        act.activation(kt[64:96, 2, :], ps[64:96, 5 + n % 2, 2 * P:3 * P], ACT.Copy).then_inc(S["lt_even"], 1)
                    act.wait_ge(S["ml_nm"], b + 1)
                    act.activation(Pl[:, 0:PAST].rearrange("p (a k) -> p a k", a=4), ps[0:NS, 0:4, :], ACT.Exp, scale=SCC, bias=sml[0:NS, 2:3], accum_out=sml[0:NS, 4:5])
                    act.activation(Pl[:, PAST:], Pl[:, PAST:], ACT.Exp, scale=SCC, bias=sml[0:NS, 2:3], accum_out=sml[0:NS, 5:6]).then_inc(S["ml_exp"], 1)

            def mix():
                for m in range(24):
                    act.wait_ge(S["pgm"], m + 1)
                    act.activation(gates[:, m, :], ps[:, m % 8, 0:T], ACT.Sigmoid, bias=pp("b_gate", m)).then_inc(S["gate"], 1)
                down("mix")

            with act.Fori(0, DEPTH) as l:
                square_x("f1_pre")
                ffn("f1")
                act.wait_ge(S["x_f1"], 1)
                square_x("mix_pre")
                rwkv()
                bc_proj()
                sw_prompt()
                sw_sample()
                latent_prep()
                ml_prompt()
                ml_sample()
                mix()
                act.wait_ge(S["x_mix"], 1)
                square_x("f2_pre")
                ffn("f2")
                layer_end(act, l)

        @block.vector
        def _(dve):
            dve.wait_ge(s_once, 48)

            chain = [0]

            def link(ins):
                chain[0] += 1
                ins.then_inc(s_dve, 1)
                dve.wait_ge(s_dve, chain[0])

            def root(tag, half=None):
                dve.wait_ge(S["norm_sums"], NORMS[tag])
                dve.tensor_scalar(rstd, ps[:, 7, 0:T], 1.0 / D_MODEL, 1e-6, ALU.mult, ALU.add).then_inc(S["mean_squares"], 1)
                dve.wait_ge(S["mean_squares"], ROOTS[tag])
                dve.wait_ge(S["roots"], ROOTS[tag])
                link(dve.reciprocal(rstd, rstd))
                if half:
                    link(dve.tensor_scalar(rstd, rstd, half, None, ALU.mult))

            def pre(tag):
                root(tag)
                for k in range(KD):
                    q = dve.scalar_tensor_tensor(out=h[:, k, :], in0=x[:, k, :], scalar=pp(tag, k), in1=rstd, op0=ALU.mult, op1=ALU.mult)

                q.then_inc(S["normed"], 1)
                dve.wait_ge(S["normed"], PRES[tag])
            def post(tag, f, half=None):
                root(tag, half)
                for k in range(KD):
                    q = dve.scalar_tensor_tensor(out=yt[:, k, :], in0=yt[:, k, :], scalar=pp(tag, k), in1=rstd, op0=ALU.mult, op1=ALU.mult)
                link(q)
                dve.tensor_tensor(x, x, yt, ALU.add).then_inc(S["x_" + f], 1)
                dve.wait_ge(S["x_" + f], 1)

            def ffn(f):
                pre(f + "_pre")
                for m in range(KF):
                    dve.wait_ge(S["ffn_sg"], FFN0[f] + m + 1)
                    link(dve.tensor_tensor(act_t[:, m, :], ps[:, m % 3, 0:T], sg2[:, m % 2, :], ALU.mult))
                    dve.tensor_tensor(act_t[:, m, :], ps[:, 3 + m % 3, 0:T], act_t[:, m, :], ALU.mult).then_inc(S["ffn_a"], 1)
                dve.wait_ge(S["ffn_a"], FFN0[f] + KF)
                post(f + "_post", f, 0.5)

            def rwkv():
                pre("mix_pre")
                dve.memset(pa, 0.0).then_inc(S["pa_zeroed"], 1)
                dve.wait_ge(S["pa_zeroed"], 1)
                link(dve.memset(xs, 0.0))
                pas = pa[:, :, 1 + SEQ:].rearrange("p m (b j) -> p m b j", b=NB)
                dve.wait_ge(s_shin, 16)
                dve.wait_ge(S["pa"], NAT)
                link(dve.tensor_copy(pas[:, :, :, 0], shin))
                dve.tensor_copy(lastT[:, :, 0], pa[:, :, SEQ])
                dve.tensor_copy(lastT[:, :, 1:9], pas[:, :, :, TS]).then_inc(S["last_rows"], 1)
                dve.wait_ge(S["last_rows"], 1)
                dve.tensor_tensor(xs[:, :, 0:SEQ], pa[:, :, 0:SEQ], pa[:, :, 1:1 + SEQ], ALU.subtract)
                for m in range(NAT):
                    q = dve.tensor_tensor(xs[:, m, SEQ:T].rearrange("p (b j) -> p b j", b=NB), pas[:, m, :, 0:TS], pas[:, m, :, 1:], ALU.subtract)
                link(q)
                for m in range(NAT):
                    mu = pp("a_mu", m)
                    xm = xs[:, m, SEQ:T].rearrange("p (b j) -> p b j", b=NB)
                    dve.scalar_tensor_tensor(out=xs[:, m, 0:SEQ], in0=xs[:, m, 0:SEQ], scalar=mu, in1=pa[:, m, 1:1 + SEQ], op0=ALU.mult, op1=ALU.add)
                    q = dve.scalar_tensor_tensor(out=xm, in0=xm, scalar=mu, in1=pas[:, m, :, 1:], op0=ALU.mult, op1=ALU.add)
                q.then_inc(S["mixed"], 1)
                dve.wait_ge(S["mixed"], 1)
                r, k, v = xs[:, 0:4], xs[:, 4:8], xs[:, 8:12]
                link(dve.memset(Hp, 0.0))
                for m in range(4):
                    q = dve.tensor_scalar(S_[8][:, m, :], k[:, m, :], pp("a_kk", m), None, ALU.mult)
                q.then_inc(S["kk0"], 1)
                dve.wait_ge(S["kk0"], 1)
                link(dve.tensor_scalar(sml[:, 8:12], par[:, PAR["a_ka"][0]:PAR["a_ka"][0] + 4], -1.0, 1.0, ALU.mult, ALU.add))
                dve.wait_ge(S["a_ready"], 4)
                link(dve.tensor_scalar(S_[0], S_[0], -float(np.exp(-0.5)), None, ALU.mult))
                for m in range(4):
                    q = dve.tensor_tensor_scan(S_[3][:, m, :], C("reset"), S_[0][:, m, :], 0.0, ALU.mult, ALU.add)
                link(q)
                dve.tensor_tensor(S_[4], S_[3], S_[0], ALU.subtract).then_inc(S["L"], 1)
                dve.wait_ge(S["L"], 1)
                dve.wait_ge(S["kk_ss"], 1)
                dve.tensor_scalar(S_[9], ps[:, 4:8, 0:T], 1e-24, None, ALU.max).then_inc(S["mean_squares"], 1)
                dve.wait_ge(S["mean_squares"], ROOTS["kk"])
                dve.wait_ge(S["roots"], ROOTS["kk"])
                link(dve.reciprocal(S_[9], S_[9]))
                link(dve.tensor_tensor(S_[8], S_[8], S_[9], ALU.mult))
                dve.wait_ge(S["exps"], 1)
                for m in range(4):
                    q = dve.tensor_scalar(S_[4][:, m, :], S_[1][:, m, :], pp("a_ka", m), sml[:, 8 + m:9 + m], ALU.mult, ALU.add)
                link(q)
                link(dve.tensor_tensor(S_[4], S_[4], k, ALU.mult))
                link(dve.tensor_tensor(S_[9], r, S_[4], ALU.mult))
                for m in range(4):
                    q = dve.tensor_scalar(S_[9][:, m, :], S_[9][:, m, :], pp("a_rk", m), None, ALU.mult)
                q.then_inc(S["bonus_in"], 1)
                dve.wait_ge(S["bonus_in"], 1)
                link(dve.tensor_tensor(S_[1], S_[8], S_[1], ALU.mult))
                dve.tensor_tensor(S_[0], S_[1], S_[7], ALU.mult)
                link(dve.tensor_tensor(S_[6], S_[8], S_[6], ALU.mult))
                dve.tensor_tensor(S_[7], S_[4], S_[7], ALU.mult)
                link(dve.tensor_tensor(S_[3], r, S_[5], ALU.mult))
                dve.wait_ge(S["bonus_ss"], 1)
                dve.tensor_tensor(S_[9], ps[:, 0:4, 0:T], v, ALU.mult).then_inc(S["streams"], 1)
                dve.wait_ge(S["streams"], 1)
                for g in range(5):
                    rwkv_group(g)
                Y = S_[8]
                dve.wait_ge(S["y_mean"], 1)
                dve.scalar_tensor_tensor(out=Y, in0=ps[:, 0:4, 0:T], scalar=-1.0 / DH, in1=Y, op0=ALU.mult, op1=ALU.add).then_inc(S["y_centred"], 1)
                dve.wait_ge(S["y_centred"], 1)
                dve.wait_ge(S["y_var"], 1)
                dve.tensor_scalar(S_[1], ps[:, 4:8, 0:T], 1.0 / DH, 64e-5, ALU.mult, ALU.add).then_inc(S["mean_squares"], 1)
                dve.wait_ge(S["mean_squares"], ROOTS["y"])
                dve.wait_ge(S["roots"], ROOTS["y"])
                link(dve.reciprocal(S_[1], S_[1]))
                link(dve.tensor_tensor(Y, Y, S_[1], ALU.mult))
                for m in range(4):
                    q = dve.tensor_scalar(Y[:, m, :], Y[:, m, :], pp("a_ln_w", m), pp("a_ln_b", m), ALU.mult, ALU.add)
                link(q)
                link(dve.tensor_tensor(Y, Y, S_[9], ALU.add))
                dve.tensor_tensor(ya, Y, S_[2], ALU.mult).then_inc(S["rwkv_done"], 1)
                dve.wait_ge(S["rwkv_done"], 1)

            def rwkv_group(g):
                sample = g == 4
                t0 = g * CHUNK
                bank = lambda b: ps[0:64, b, :].rearrange("p (h s) -> p h s", h=H)
                msk = lambda n: C(n, 64).unsqueeze(1).to_broadcast([64, H, CHUNK])
                dve.wait_ge(S["rows"], g + 1)
                for i, o in enumerate((Vr, bdr, kdr)):
                    dve.tensor_copy(o, bank(i))
                dve.wait_ge(S["RK"], g + 1)
                dve.tensor_tensor(X8, bank(3), msk("m8p"), ALU.mult)
                dve.tensor_tensor(X8T, bank(4), msk("m8Tp"), ALU.mult)
                if not sample:
                    for o, n in ((Xo16, "o16T"), (Xo32, "o32T"), (Xo64, "o64T")):
                        dve.tensor_tensor(o, bank(4), msk(n), ALU.mult)
                dve.tensor_tensor(KK, bank(5), msk("sTs" if sample else "sTp"), ALU.mult)
                dve.tensor_tensor(RB, bank(6), msk("iTs" if sample else "iTp"), ALU.mult)
                dve.tensor_tensor(RK, bank(7), msk("iTs" if sample else "iTp"), ALU.mult).then_inc(S["masked"], 1)
                dve.wait_ge(S["masked"], g + 1)
                dve.wait_ge(S["X2T"], g + 1)
                dve.tensor_copy(X2, bank(0))
                dve.tensor_copy(X2T, bank(1)).then_inc(S["x2"], 1)
                dve.wait_ge(S["x2"], g + 1)
                dve.wait_ge(S["X4"], g + 1)
                dve.tensor_copy(X4, bank(2)).then_inc(S["x4"], 1)
                dve.wait_ge(S["x4"], g + 1)
                link(dve.tensor_tensor(Pm, X2, X4, ALU.add))
                link(dve.tensor_tensor(Pm, Pm, msk_id(), ALU.add))
                dve.wait_ge(S["X6"], g + 1)
                dve.tensor_tensor(Pm, bank(3), Pm, ALU.add).then_inc(S["pm"], 1)
                dve.wait_ge(S["pm"], g + 1)
                dve.wait_ge(S["XP"], g + 1)
                dve.tensor_tensor(Tt, bank(4), Pm, ALU.add).then_inc(S["t"], 1)
                dve.wait_ge(S["t"], g + 1)
                dve.wait_ge(S["TT"], g + 1)
                dve.tensor_copy(TT, bank(5)).then_inc(S["tt"], 1)
                dve.wait_ge(S["tt"], g + 1)
                if not sample:
                    for i in range(3):
                        dve.wait_ge(S["G"], 3 * g + i + 1)
                        dve.tensor_copy(G, bank(0)).then_inc(S["g_level" ], 1)
                        dve.wait_ge(S["g_level" ], 3 * g + i + 1)
                        dve.wait_ge(S["dTT"], 3 * g + i + 1)
                        dve.tensor_tensor(Tt, bank(1), Tt, ALU.add)
                        dve.tensor_tensor(TT, bank(2), TT, ALU.add).then_inc(S["t_level" ], 1)
                        dve.wait_ge(S["t_level" ], 3 * g + i + 1)
                    dve.wait_ge(S["rhs"], g + 1)
                    dve.tensor_copy(RHS, bank(3)).then_inc(S["rhs_ev"], 1)
                    dve.wait_ge(S["rhs_ev"], g + 1)
                else:
                    bm = C("bmask", 64).unsqueeze(2).to_broadcast([64, NB, DH])
                    for hd in range(H):
                        dve.wait_ge(S["zh_mm"], hd + 1)
                        dve.tensor_tensor(Tm, ps[0:64, hd % 2, :].rearrange("p (b v) -> p b v", b=NB), bm, ALU.mult).then_inc(S["zh"], 1)
                        dve.wait_ge(S["zh"], hd + 1)
                        link(dve.tensor_reduce(RHS[:, hd], Tm.rearrange("p b v -> p v b"), AX, ALU.add))
                    dve.wait_ge(S["rhs"], g + 1)
                    dve.tensor_tensor(RHS, bank(3), RHS, ALU.add).then_inc(S["rhs_ev"], 1)
                    dve.wait_ge(S["rhs_ev"], g + 1)
                dve.wait_ge(S["u"], g + 1)
                dve.tensor_scalar(U, bank(4), -1.0, None, ALU.mult).then_inc(S["u_ev"], 1)
                dve.wait_ge(S["u_ev"], g + 1)
                dve.wait_ge(S["y"], g + 1)
                dve.tensor_copy(S_[8][:, :, t0:t0 + CHUNK], ps[:, 5, 0:256].rearrange("p (m t) -> p m t", m=4))
                EL = S_[5]
                if not sample:
                    dve.wait_ge(S["h"], g + 1)
                    link(dve.tensor_tensor(Hp, bank(6), Hp, ALU.add))
                    pairs = Hp.rearrange("p (m r) v -> p r m v", r=2)
                    dve.wait_ge(S["odd"], 5 * g + 5)
                    for r, el in ((0, EL[0:64, :, t0 + CHUNK - 1:t0 + CHUNK]), (1, Odd[4][:, :, CHUNK - 1:CHUNK])):
                        q = dve.tensor_tensor(pairs[:, r], pairs[:, r], el.to_broadcast([64, 4, DH]), ALU.mult)
                    q.then_inc(S["group"], 1)
                    dve.wait_ge(S["group"], g + 1)
                else:
                    for hd in range(H):
                        if hd:
                            dve.wait_ge(S["hs"], hd)
                        dve.tensor_tensor(Ue, U[:, hd].unsqueeze(1).to_broadcast([64, NB, DH]), bm, ALU.mult)
                        dve.tensor_tensor(Ve, Vr[:, hd].unsqueeze(1).to_broadcast([64, NB, DH]), bm, ALU.mult).then_inc(S["ue"], 1)
                        dve.wait_ge(S["ue"], hd + 1)
                        dve.wait_ge(S["hs"], hd + 1)
                        Hh = Hs(hd)
                        link(dve.tensor_tensor(Hh, ps[0:64, 6 + hd % 2, :], Hh, ALU.add))
                        Hh = Hh.rearrange("p (b v) -> p b v", b=NB)
                        el = Odd[4][:, hd // 2, :] if hd % 2 else EL[0:64, hd // 2, SEQ:T]
                        el = el.rearrange("p (b j) -> p b j", b=NB)[:, :, TS - 1:TS]
                        q = dve.tensor_tensor(Hh, Hh, el.to_broadcast([64, NB, DH]), ALU.mult)
                    q.then_inc(S["group"], 1)
                    dve.wait_ge(S["group"], g + 1)

            def msk_id():
                return cst[0:64, CONST["ident"][0]:CONST["ident"][0] + 64].unsqueeze(1).to_broadcast([64, H, CHUNK])

            def rope(v, heads, half, cos, sin, tmp):
                rows = v.shape[0]
                a, b = v[:, :, 0:half], v[:, :, half:2 * half]
                cos, sin = [c.unsqueeze(1).to_broadcast([rows, heads, half]) for c in (cos, sin)]
                n = heads * half
                t = [tmp[0:rows, i * n:i * n + n].rearrange("p (h d) -> p h d", h=heads) for i in range(4)]
                dve.tensor_tensor(t[0], a, cos, ALU.mult)
                dve.tensor_tensor(t[1], b, sin, ALU.mult)
                dve.tensor_tensor(t[2], b, cos, ALU.mult)
                link(dve.tensor_tensor(t[3], a, sin, ALU.mult))
                dve.tensor_tensor(a, t[0], t[1], ALU.subtract)
                return dve.tensor_tensor(b, t[2], t[3], ALU.add)

            def bc_rows():
                link(dve.memset(sml[:, 8:14], 1.0))
                parts = ((0, Q_LORA), (Q_LORA, KV_LORA))
                for i, _, rows in TOK_TILES:
                    dve.wait_ge(S["pbc_ev"], 3 + i + 1)
                    for j, (c0, w) in enumerate(parts):
                        part, ms = PBc[0:rows, i, c0:c0 + w], sml[0:rows, 8 + 2 * i + j:9 + 2 * i + j]
                        link(dve.tensor_tensor_reduce(rt[0:rows, 0:w], part, part, 1.0, 0.0, ALU.mult, ALU.add, ms))
                        dve.tensor_scalar(ms, ms, 1.0 / w, 1e-6, ALU.mult, ALU.add).then_inc(S["latent_ms"], 1)
                        dve.wait_ge(S["latent_ms"], 2 * i + j + 1)
                dve.wait_ge(S["latent_root"], 1)
                link(dve.reciprocal(sml[:, 8:14], sml[:, 8:14]))
                for i, _, rows in TOK_TILES:
                    q_part, kv_part = [PBc[0:rows, i, c0:c0 + w] for c0, w in parts]
                    link(dve.tensor_scalar(q_part, q_part, sml[0:rows, 8 + 2 * i:9 + 2 * i], None, ALU.mult))
                    link(dve.scalar_tensor_tensor(out=kv_part, in0=kv_part, scalar=sml[0:rows, 9 + 2 * i:10 + 2 * i], in1=kvn[0:rows, :], op0=ALU.mult, op1=ALU.mult))
                    link(rope(PBc[0:rows, i:i + 1, Q_LORA + KV_LORA:], 1, DROPE // 2, C("cosc")[0:rows, 16 * i:16 * i + 16],
                              C("sinc")[0:rows, 16 * i:16 * i + 16], rt))
                dve.wait_ge(S["pbc_ev"], 21)
                for i, _, rows in TOK_TILES:
                    rope(PBq[0:rows, i, :].rearrange("p (h d) -> p h d", h=32), 32, ROT, C("cosb")[0:rows, 8 * i:8 * i + 8],
                         C("sinb")[0:rows, 8 * i:8 * i + 8], rt).then_inc(S["rows_ready"], 1)
                    dve.wait_ge(S["rows_ready"], i + 1)

            def softmax_in(tag, n, src, mask, scores):
                i, base = n % 2, PROMPT0[tag]
                dve.tensor_tensor(scores, src, mask, ALU.add).then_inc(S["prompt_s"], 1)
                dve.wait_ge(S["prompt_s"], base + n + 1)
                link(dve.tensor_reduce(sml[:, i:i + 1], scores, mybir.AxisListType.XY if len(scores.shape) == 3 else AX, ALU.max))
                dve.tensor_scalar(sml[:, 2 + i:3 + i], sml[:, i:i + 1], -(SCB if tag == "swp" else SCC), None, ALU.mult).then_inc(S["prompt_nm"], 1)
                dve.wait_ge(S["prompt_nm"], base + n + 1)

            def prompt_attention(tag, y, one_group):
                base = PROMPT0[tag]
                src = lambda n: (ps[:, n % 2, 0:SEQ] if one_group else
                                 ps[:, 2 * (n % 2):2 * (n % 2) + 2, :].rearrange("p b k -> p (b k)")[:, 0:768].rearrange("p (g k) -> p g k", g=3))

                def finish(n):
                    r0, m, t = 64 * (n % 2), (n % H) // 2, n // H
                    dve.wait_ge(S["prompt_o"], base + n + 1)
                    dve.tensor_copy(y[r0:r0 + 64, m, t * P:t * P + P], ps[r0:r0 + 64, 6 + n % 2, 0:P]).then_inc(S["prompt_y"], 1)
                    dve.wait_ge(S["prompt_y"], base + n + 1)

                for i in range(17):
                    if i < 16:
                        t = i // H
                        dve.wait_ge(S["prompt_mm"], base + i + 1)
                        scores = Sp[i % 2][:, 0, :] if one_group else Sp[i % 2]
                        mask = (C("mlp")[:, t * SEQ:t * SEQ + SEQ] if one_group else
                                C("swp")[:, t * 768:t * 768 + 768].rearrange("p (g k) -> p g k", g=3))
                        softmax_in(tag, i, src(i), mask, scores)
                    if i >= 2:
                        finish(i - 2)
                    if i >= 1:
                        n = i - 1
                        dve.wait_ge(S["prompt_e"], base + n + 1)
                        probs, rs = Sp[n % 2], sml[:, 4 + n % 2:5 + n % 2]
                        link(dve.reciprocal(rs, rs))
                        if one_group:
                            dve.tensor_scalar(Pc[n % 2], probs[:, 0, :], rs, None, ALU.mult).then_inc(S["prompt_p"], 1)
                            dve.wait_ge(S["prompt_p"], base + n + 1)
                        else:
                            link(dve.tensor_tensor(Pc[n % 2], probs[:, 0, :], probs[:, 1, :], ALU.add))
                            link(dve.tensor_tensor(Pc[n % 2], Pc[n % 2], probs[:, 2, :], ALU.add))
                            dve.tensor_scalar(Pc[n % 2], Pc[n % 2], rs, None, ALU.mult).then_inc(S["prompt_p"], 1)
                            dve.wait_ge(S["prompt_p"], base + n + 1)
                        dve.wait_ge(S["prompt_T"], base + n + 1)
                        dve.tensor_copy(PTp[n % 2], ps[:, (2 if one_group else 4) + n % 2, 0:256].rearrange("p (c k) -> p c k", c=2)).then_inc(S["prompt_pt"], 1)
                        dve.wait_ge(S["prompt_pt"], base + n + 1)
                        if one_group:
                            dve.wait_ge(S["prompt_ol"], n + 1)
                            dve.tensor_copy(OLp[n % 2], ps[:, 4 + n % 2, 0:256].rearrange("p (c k) -> p c k", c=2)).then_inc(S["prompt_olev"], 1)
                            dve.wait_ge(S["prompt_olev"], n + 1)
                finish(15)

            def sw_sample():
                dve.memset(Qbd, 0.0)
                link(dve.memset(PnF, 0.0))
                q4 = qT.rearrange("p (g c) t -> p g c t", g=3)
                for b in range(NB):
                    tk = slice(SEQ + TS * b, SEQ + TS * b + TS)
                    if b:
                        dve.wait_ge(S["sw_s"], b)
                    for c in range(4):
                        for r in range(2):
                            o = Qbd[64 * r:64 * r + 64, c, :, 16 * c + 8 * r:16 * c + 8 * r + 8]
                            dve.tensor_copy(o, q4[64 * r:64 * r + 64, :, c, tk]).then_inc(S["qbd"], 1)
                    dve.wait_ge(S["sw_s"], b + 1)
                    dve.tensor_tensor(Sw, ps[0:NS, 0:4, :].rearrange("p b k -> p (b k)")[:, 0:SW_COLS], C("sws", NS), ALU.add).then_inc(S["sw_masked"], 1)
                    dve.wait_ge(S["sw_masked"], b + 1)
                    link(dve.tensor_reduce(sml[0:NS, 0:1], Sw, AX, ALU.max))
                    dve.tensor_scalar(sml[0:NS, 2:3], sml[0:NS, 0:1], -SCB, None, ALU.mult).then_inc(S["sw_nm"], 1)
                    dve.wait_ge(S["sw_nm"], b + 1)
                    dve.wait_ge(S["sw_e"], b + 1)
                    link(dve.reciprocal(sml[0:NS, 6:7], sml[0:NS, 4:5]))
                    link(dve.tensor_scalar(Sw, Sw, sml[0:NS, 6:7], None, ALU.mult))
                    n0 = SW_TILES * P
                    if b:
                        dve.memset(PnF[:, TS * (b - 1):TS * b], 0.0)
                    o = PnF[:, TS * b:TS * b + TS]
                    link(dve.tensor_tensor(o, Sw[:, n0:n0 + TS], Sw[:, n0 + TS:n0 + 2 * TS], ALU.add))
                    dve.tensor_tensor(o, o, Sw[:, n0 + 2 * TS:n0 + 3 * TS], ALU.add).then_inc(S["sw_p"], 1)
                    dve.wait_ge(S["sw_p"], b + 1)
                    dve.wait_ge(S["sw_PT"], b + 1)
                    dve.tensor_copy(PTw[:, 0:8, :], ps[:, 6, :].rearrange("p (t n) -> p t n", t=8))
                    dve.tensor_copy(PTw[:, 8:13, :], ps[:, 7, 0:320].rearrange("p (t n) -> p t n", t=5))
                    dve.tensor_copy(PTn, ps[0:NS, 7, 320:384]).then_inc(S["sw_pt"], 1)
                    dve.wait_ge(S["sw_pt"], b + 1)
                    dve.wait_ge(S["sw_pv"], b + 1)
                    o = ps[:, 7, 448:512].rearrange("p (c r j) -> p c r j", c=4, r=2)
                    dve.tensor_copy(yb[0:64, :, tk], o[0:64, :, 0, :])
                    dve.tensor_copy(yb[64:128, :, tk], o[64:128, :, 1, :]).then_inc(S["sws_done"], 1)
                    dve.wait_ge(S["sws_done"], b + 1)

            def latent_prep():
                dve.wait_ge(s_out, N_ROWS_OUT)
                dve.wait_ge(S["cqT"], 1)
                for k in range(3):
                    dve.tensor_scalar(cqT[:, k, :], ps[:, k, 0:T], pp("c_q_norm", k), None, ALU.mult)
                dve.wait_ge(S["kvT"], 1)
                dve.tensor_copy(kvT[0:64].rearrange("p (a b) k -> p a (b k)", b=2), ps[0:64, 3:7, :]).then_inc(S["kvT_ev"], 1)
                dve.wait_ge(S["kvT_ev"], 1)
                dve.wait_ge(S["qrow_ev"], 6)
                for i, _, rows in TOK_TILES:
                    v = qrow[0:rows, i, :].rearrange("p (h d) -> p h d", h=H)[:, :, DNOPE:]
                    rope(v, H, DROPE // 2, C("cosc")[0:rows, 16 * i:16 * i + 16], C("sinc")[0:rows, 16 * i:16 * i + 16], rt2).then_inc(S["q_rope"], 1)
                    dve.wait_ge(S["q_rope"], i + 1)
                dve.wait_ge(S["qcT_ev"], H)
                dve.tensor_copy(QR[64:96], qcT[64:96, :, SEQ:T].rearrange("p h (b j) -> p b h j", b=NB))
                dve.wait_ge(S["ql_ev"], 16)
                dve.memset(PnL, 0.0).then_inc(S["ml_prep"], 1)
                dve.wait_ge(S["ml_prep"], 1)

            def ml_sample():
                for b in range(NB):
                    for n in range(16 * b + 1, 16 * b + 16, 2):
                        dve.wait_ge(S["lt_T"], n + 1)
                        if n >= 8:
                            dve.wait_ge(S["ml_mm"], n // 4 - 1)
                        kt = KTl[(n // 4) % 2][:, :, (n % 4) * P:(n % 4) * P + P]
                        dve.tensor_copy(kt[:, 0:2, :], ps[:, 5 + n % 2, 0:2 * P].rearrange("p (c k) -> p c k", c=2))
                        dve.tensor_copy(kt[64:96, 2, :], ps[64:96, 5 + n % 2, 2 * P:3 * P]).then_inc(S["lt_odd"], 1)
                    dve.wait_ge(S["ml_s"], b + 1)
                    link(dve.tensor_tensor(Pl[:, PAST:], ps[0:NS, 4, 0:TS], C("mls", NS), ALU.add))
                    dve.tensor_reduce(sml[0:NS, 0:1], ps[0:NS, 0:4, :], mybir.AxisListType.XY, ALU.max)
                    link(dve.tensor_reduce(sml[0:NS, 1:2], Pl[:, PAST:], AX, ALU.max))
                    link(dve.tensor_tensor(sml[0:NS, 0:1], sml[0:NS, 0:1], sml[0:NS, 1:2], ALU.max))
                    dve.tensor_scalar(sml[0:NS, 2:3], sml[0:NS, 0:1], -SCC, None, ALU.mult).then_inc(S["ml_nm"], 1)
                    dve.wait_ge(S["ml_nm"], b + 1)
                    dve.wait_ge(S["ml_exp"], b + 1)
                    link(dve.tensor_tensor(sml[0:NS, 6:7], sml[0:NS, 4:5], sml[0:NS, 5:6], ALU.add))
                    dve.reciprocal(sml[0:NS, 7:8], sml[0:NS, 6:7])
                    if b:
                        dve.memset(PnL[:, TS * (b - 1):TS * b], 0.0)
                    dve.tensor_copy(PnL[:, TS * b:TS * b + TS], Pl[:, PAST:]).then_inc(S["ml_p"], 1)
                    dve.wait_ge(S["ml_p"], b + 1)
                    for half in range(2):
                        dve.wait_ge(S["ml_PT"], 3 * b + half + 1)
                        dve.tensor_copy(PTL[:, 8 * half:8 * half + 8, :], ps[:, 7, :].rearrange("p (t n) -> p t n", t=8)).then_inc(S["ml_pt"], 1)
                        dve.wait_ge(S["ml_pt"], 3 * b + half + 1)
                    dve.wait_ge(S["ml_PT"], 3 * b + 3)
                    dve.tensor_copy(PTl, ps[0:NS, 7, 0:NS]).then_inc(S["ml_pt"], 1)
                    dve.wait_ge(S["ml_pt"], 3 * b + 3)
                    dve.wait_ge(S["ml_pv"], b + 1)
                    dve.tensor_scalar(Osb, ps[0:NS, 4, 256:512], sml[0:NS, 7:8], None, ALU.mult).then_inc(S["ml_osb"], 1)
                    dve.wait_ge(S["ml_osb"], b + 1)
                    dve.wait_ge(S["ml_oT"], b + 1)
                    dve.tensor_copy(olT[:, :, :, TS * b:TS * b + TS], ps[:, 7, 0:2 * NS].rearrange("p (c h j) -> p c h j", c=2, h=H)).then_inc(S["ml_olT"], 1)
                    dve.wait_ge(S["ml_olT"], b + 1)
                dve.wait_ge(S["ml_yc"], 1)
                dve.tensor_copy(yc[:, :, SEQ:T], ps[:, 0, 0:4 * NS].rearrange("p (m t) -> p m t", m=4)).then_inc(S["ml_done"], 1)
                dve.wait_ge(S["ml_done"], 1)

            def mix():
                for n in range(24):
                    m = n % KD
                    dve.wait_ge(S["brm"], n + 1)
                    if n < KD:
                        dve.tensor_tensor(mt[:, m, :], ps[:, m, 0:T], gates[:, n, :], ALU.mult).then_inc(S["br_ev"], 1)
                        dve.wait_ge(S["br_ev"], n + 1)
                    else:
                        link(dve.tensor_tensor(gates[:, n, :], ps[:, m, 0:T], gates[:, n, :], ALU.mult))
                        dve.tensor_tensor(mt[:, m, :], gates[:, n, :], mt[:, m, :], ALU.add).then_inc(S["br_ev"], 1)
                        dve.wait_ge(S["br_ev"], n + 1)
                post("mix_post", "mix")

            with dve.Fori(0, DEPTH) as l:
                dve.wait_ge(s_par, 16 * 5)
                ffn("f1")
                rwkv()
                bc_rows()
                prompt_attention("swp", yb, False)
                sw_sample()
                latent_prep()
                prompt_attention("mlp", yc, True)
                ml_sample()
                mix()
                ffn("f2")
                layer_end(dve, l)


_IN = ["consts", "params", "xT", "shiftT", "wkvT", "page_table", "cache_mla_ckv", "cache_mla_krope", "cache_swa_k",
       "cache_swa_v", "c_kv_norm", "a_w2", "a_a2", "a_g2", "w_in", "w_branch_a", "w_branch_b", "w_branch_c", "w_out",
       "c_q_up", "c_kv_up", "f1_wg", "f1_wu", "f1_wd", "f2_wg", "f2_wu", "f2_wd"]
_OUT = {"yT": (P, KD, T), "o_ckv_p": (DEPTH, 1, SEQ, KV_LORA), "o_ckv_s": (DEPTH, NB, TS, KV_LORA),
        "o_krope_p": (DEPTH, 1, SEQ, DROPE), "o_krope_s": (DEPTH, NB, TS, DROPE),
        "o_swa_k_p": (DEPTH, 1, SEQ, W_A), "o_swa_k_s": (DEPTH, NB, PAST, W_A),
        "o_swa_v_p": (DEPTH, 1, SEQ, W_A), "o_swa_v_s": (DEPTH, NB, PAST, W_A),
        "o_wkv_p": (DEPTH, DH, H, DH), "o_wkv_s": (DEPTH, 2, DH, 4, NB * DH), "o_shift": (DEPTH, P, NAT, 9)}


def kernel(**inputs):
    import concourse.bacc as bacc
    from concourse.bass_utils import run_bass_kernel_spmd

    a = {k: np.ascontiguousarray(v) for k, v in inputs.items()}

    def by_channel(v, tiles):
        out = np.zeros((v.shape[0], P, len(tiles)) + v.shape[2:], v.dtype)
        for m, (c0, rows) in enumerate(tiles):
            out[:, :rows, m] = v[:, c0:c0 + rows]
        return out

    full = lambda n: [(i * P, P) for i in range(n)]
    names = {"f1_pre": "n_f1_pre", "f1_post": "n_f1_post", "mix_pre": "n_mix_pre", "mix_post": "n_mix_post",
             "f2_pre": "n_f2_pre", "f2_post": "n_f2_post"}
    params = [by_channel(a[names.get(n, n)].reshape(DEPTH, -1), A_TILES if n == "a_mu" else full(w))
              for n, (_, w) in PAR.items()]
    tokens = np.concatenate([a["x_prompt"].reshape(SEQ, D_MODEL), a["x_sample"].reshape(NS, D_MODEL)])
    states = a["state_rwkv_wkv"].reshape(DEPTH, NB, 4, 2, DH, DH).transpose(0, 3, 5, 2, 1, 4).reshape(DEPTH, 2, DH, 4, NB * DH)
    arrays = {
        "consts": constants(), "params": np.concatenate(params, axis=2),
        "xT": np.ascontiguousarray(tokens.T.reshape(KD, P, T).transpose(1, 0, 2)),
        "shiftT": by_channel(a["state_rwkv_shift"].transpose(0, 2, 1), A_TILES),
        "wkvT": np.ascontiguousarray(states),
        "cache_swa_k": a["cache_swa_k"].reshape(DEPTH, NB, PAST, W_A),
        "cache_swa_v": a["cache_swa_v"].reshape(DEPTH, NB, PAST, W_A),
    }
    for n in _IN:
        if n not in arrays:
            arrays[n] = a[n]

    nc = bacc.Bacc("TRN2", target_bir_lowering=False, num_devices=1)
    io = {n: nc.dram_tensor(f"in_{n}_dram", arrays[n].shape, mybir.dt.from_np(arrays[n].dtype), kind="ExternalInput").ap()
          for n in _IN}
    for n, shape in _OUT.items():
        io[n] = nc.dram_tensor(f"out_{n}_dram", shape, F32, kind="ExternalOutput").ap()
    build(nc, io)
    r = run_bass_kernel_spmd(nc, [{f"in_{n}_dram": arrays[n] for n in _IN}], core_ids=[0]).results[0]
    o = {n: r[f"out_{n}_dram"] for n in _OUT}

    tokens = o["yT"].transpose(1, 0, 2).reshape(D_MODEL, T).T
    rows = np.concatenate([o["o_shift"][:, :n, m] for m, (_, n) in enumerate(A_TILES)], axis=1)
    wkv_p = o["o_wkv_p"].transpose(0, 2, 3, 1)[:, None]
    wkv_s = o["o_wkv_s"].reshape(DEPTH, 2, DH, 4, NB, DH).transpose(0, 4, 3, 1, 5, 2).reshape(DEPTH, NB, H, DH, DH)
    heads = lambda v: v.reshape(v.shape[:3] + (H, DH))
    c = np.ascontiguousarray
    return (c(tokens[:SEQ].reshape(1, SEQ, D_MODEL)), c(tokens[SEQ:].reshape(NB, TS, D_MODEL)),
            o["o_ckv_p"], o["o_ckv_s"], o["o_krope_p"], o["o_krope_s"],
            heads(o["o_swa_k_p"]), heads(o["o_swa_k_s"]), heads(o["o_swa_v_p"]), heads(o["o_swa_v_s"]),
            c(wkv_p), c(wkv_s), c(rows[:, None, :, 0]), c(rows[:, :, 1:].transpose(0, 2, 1)))
```

```python
from contextlib import ExitStack

import numpy as np
import concourse.bass as bass
from concourse import mybir

F32 = mybir.dt.float32
I32 = mybir.dt.int32
ALU = mybir.AluOpType
ACT = mybir.ActivationFunctionType
AX = mybir.AxisListType.X

P = 128
D_MODEL, DEPTH, D_FF = 1024, 2, 2816
SEQ, NB, TS, PAST, PAGE, N_POOL = 256, 8, 8, 2048, 128, 160
NS = NB * TS
T = SEQ + NS
KD, KF = D_MODEL // P, D_FF // P
H, DH = 8, 64
W_A = H * DH
A_COLS, B_COLS, C_COLS = 3 * W_A + 160, 5 * W_A, 672
Q_LORA, KV_LORA, DROPE, DNOPE = 384, 256, 32, 64
CB, CC, CG = A_COLS, A_COLS + B_COLS, A_COLS + B_COLS + C_COLS
ROT, N_PAGES = 8, PAST // PAGE
A_TILES = [(m * P, P) for m in range(12)] + [(3 * W_A, 64), (3 * W_A + 64, 96)]
NAT = len(A_TILES)
PADT = 1 + SEQ + NB * (TS + 1)
TOK_TILES = [(0, 0, P), (1, P, P), (2, SEQ, NS)]
GROUPS_B = ((128, 1), (512, 4), (2048, 16))
CHUNK = 64
SW_TILES = 8 + 4 + 1
SW_COLS = SW_TILES * P + 3 * TS
NEG = -1.0e30

PAR = {}
_at = 0
for _n, _w in [("f1_pre", 8), ("f1_post", 8), ("mix_pre", 8), ("mix_post", 8), ("f2_pre", 8), ("f2_post", 8),
               ("b_gate", 24), ("a_mu", NAT), ("a_w0", 4), ("a_a0", 4), ("a_kk", 4), ("a_ka", 4), ("a_rk", 4),
               ("a_ln_w", 4), ("a_ln_b", 4), ("c_q_norm", 3)]:
    PAR[_n] = (_at, _w)
    _at += _w
NPAR = _at

CONST = {}
_at = 0
for _n, _w in [("ident", P), ("ones", P), ("onesblk", P), ("reset", T), ("cosb", 24), ("sinb", 24), ("cosc", 48),
               ("sinc", 48), ("bmask", 8), ("tsel", 8), ("m8p", 64), ("m8Tp", 64), ("o16T", 64), ("o32T", 64), ("o64T", 64),
               ("sTp", 64), ("iTp", 64), ("sTs", 64), ("iTs", 64), ("swp", 2 * 3 * SEQ),
               ("mlp", 2 * SEQ), ("sws", SW_COLS), ("mls", TS)]:
    CONST[_n] = (_at, _w)
    _at += _w
NCONST = _at


def constants():
    c = np.zeros((P, NCONST), np.float32)

    def put(name, a):
        at, w = CONST[name]
        c[:a.shape[0], at:at + w] = a.reshape(a.shape[0], w)

    put("ident", np.eye(P))
    put("ones", np.ones((P, P)))
    blk = np.arange(P) // DH
    put("onesblk", (blk[:, None] == blk[None, :]) * 1.0)
    reset = np.ones(T)
    reset[0:SEQ:CHUNK] = 0
    reset[SEQ::TS] = 0
    put("reset", np.broadcast_to(reset, (P, T)))
    pos = np.zeros((P, 3), np.float32)
    pos[:, 0], pos[:, 1] = np.arange(P), P + np.arange(P)
    pos[:, 2] = PAST + np.arange(P) % TS
    for tag, half in (("b", ROT), ("c", DROPE // 2)):
        inv = np.float32(500000.0) ** (-(np.arange(half, dtype=np.float32) * np.float32(2.0) / np.float32(2 * half)))
        ang = pos[:, :, None] * inv.astype(np.float32)[None, None, :]
        put("cos" + tag, np.cos(ang))
        put("sin" + tag, np.sin(ang))
    t = np.arange(CHUNK)
    put("bmask", (t[:, None] // TS == np.arange(NB)[None, :]) * 1.0)
    put("tsel", (t[:, None] % TS == np.arange(TS)[None, :]) * 1.0)
    low = t[None, :] < t[:, None]
    same = lambda n: t[:, None] // n == t[None, :] // n
    put("m8p", (low & same(8)) * -1.0)
    put("m8Tp", (low & same(8)).T * -1.0)
    for n in (16, 32, 64):
        put(f"o{n}T", (low & same(n) & ~same(n // 2)).T * -1.0)
    put("sTp", low.T * 1.0)
    put("iTp", (low | same(1)).T * 1.0)
    put("sTs", (low & same(8)).T * 1.0)
    put("iTs", ((low & same(8)) | same(1)).T * 1.0)
    q = np.arange(SEQ)[:, None]
    k = np.arange(SEQ)[None, :]
    swp = np.stack([np.where((q >= k) & ((q - k) % d == 0) & (q - k <= w), 0.0, NEG) for w, d in GROUPS_B], 1)
    put("swp", swp.reshape(2, P, 3, SEQ).transpose(1, 0, 2, 3))
    put("mlp", np.where(q >= k, 0.0, NEG).reshape(2, P, SEQ).transpose(1, 0, 2))
    j = np.arange(NS) % TS
    m = np.full((NS, SW_COLS), NEG)
    a = np.arange(P)
    for r in range(8):
        m[:, r * P:(r + 1) * P] = np.where(j[:, None] == r, 0.0, NEG)
    for r in range(4):
        ok = (j[:, None] % 4 == r) & ((j[:, None] < 4) | (a[None, :] >= 1))
        m[:, (8 + r) * P:(9 + r) * P] = np.where(ok, 0.0, NEG)
    m[:, 12 * P:13 * P] = np.where(a[None, :] >= j[:, None], 0.0, NEG)
    n = np.arange(TS)[None, :]
    for g, (w, d) in enumerate(GROUPS_B):
        ok = (j[:, None] >= n) & ((j[:, None] - n) % d == 0)
        m[:, SW_TILES * P + g * TS:SW_TILES * P + (g + 1) * TS] = np.where(ok, 0.0, NEG)
    put("sws", m)
    put("mls", np.where(j[:, None] >= n, 0.0, NEG))
    return c


ROOTS = {t: i + 1 for i, t in enumerate(("f1_pre", "f1_post", "mix_pre", "kk", "y", "mix_post", "f2_pre", "f2_post"))}
NORMS = {t: i + 1 for i, t in enumerate(("f1_pre", "f1_post", "mix_pre", "mix_post", "f2_pre", "f2_post"))}
PRES = {t: i + 1 for i, t in enumerate(("f1_pre", "mix_pre", "f2_pre"))}
FFN0, DOWN0, PROMPT0 = {"f1": 0, "f2": KF}, {"f1": 0, "mix": KD, "f2": 2 * KD}, {"swp": 0, "mlp": 2 * H}
NSLOT = 3
N_ROWS_OUT = 16 * (4 + 2 * NB + 2)
SLOT = 4096
SWK, SWV = SW_TILES * W_A, SW_TILES * W_A


def weight_units(io):
    out = []

    def cols(w, k, c0, c1):
        return lambda l: w[bass.ds(l, 1), :, c0:c1].rearrange("a (k p) n -> p (a k) n", p=P), k, c1 - c0

    def ffn(f):
        for u in range(KF // 2):
            out.append(((f, "gu", u), [cols(io[f + "_wg"], KD, u * 256, u * 256 + 256),
                                       cols(io[f + "_wu"], KD, u * 256, u * 256 + 256)]))
        for u in range(KD):
            out.append(((f, "d", u), [cols(io[f + "_wd"], KF, u * P, (u + 1) * P)]))

    ffn("f1")
    for u, (c0, c1) in enumerate([(0, 512), (512, 1024), (1024, 1536), (1536, 1696)]):
        out.append((("pa", u), [cols(io["w_in"], KD, c0, c1)]))
    for u, (c0, c1) in enumerate([(CC, CC + 512), (CC + 512, CG)] + [(CB + 512 * i, CB + 512 * i + 512) for i in range(5)]):
        out.append((("pbc", u), [cols(io["w_in"], KD, c0, c1)]))
    for u in range(6):
        out.append((("pg", u), [cols(io["w_in"], KD, CG + 512 * u, CG + 512 * u + 512)]))
    for br in "abc":
        out.append((("br", br), [cols(io["w_branch_" + br], 4, 0, D_MODEL)]))
    for u in range(2):
        out.append((("wo", u), [cols(io["w_out"], KD, 512 * u, 512 * u + 512)]))
    ffn("f2")
    return out


STEPS = (
    "G", "L", "RK", "TT", "X2T", "X4", "X6", "XP", "a_ready", "bonus_in", "bonus_ss", "br_ev", "brm", "ckvT",
    "ckvT_ev", "cqT", "dTT", "down_d", "down_y", "exps", "ffn_a", "ffn_gu", "ffn_sg", "g_level", "g_ready", "gate",
    "group", "h", "hs", "kk0", "kk_sq", "kk_ss", "kt_T", "kt_ev", "kvT", "kvT_ev", "last_rows", "latent_ms",
    "latent_root", "lora_g", "lora_wa", "lt_T", "lt_even", "lt_odd", "masked", "mean_squares", "mixed", "ml_PT", "ml_done",
    "ml_exp", "ml_mm", "ml_nm", "ml_oT", "ml_olT", "ml_osb", "ml_p", "ml_prep", "ml_pt", "ml_pv", "ml_s", "ml_yc",
    "norm_sums", "normed", "odd", "pa", "pa_zeroed", "pam", "pbc_ev", "pbc_mm", "pgm", "pm", "prompt_T", "prompt_e",
    "prompt_mm", "prompt_nm", "prompt_o", "prompt_ol", "prompt_olev", "prompt_p", "prompt_pt", "prompt_s",
    "prompt_y", "q_rope", "q_rows", "qbd", "qcT", "qcT_ev", "qkT", "qk_ev", "ql", "ql_ev", "qrow_ev", "rhs",
    "rhs_ev", "roots", "rows", "rows_ready", "rwkv_done", "squared", "streams", "sw_PT", "sw_e", "sw_masked",
    "sw_mm", "sw_nm", "sw_p", "sw_pt", "sw_pv", "sw_own", "sw_y", "sw_s", "sws_done", "t", "t_level", "tanh", "tt", "u", "u_ev", "ue",
    "x2", "x4", "x_f1", "x_f2", "x_mix", "y", "y_centred", "y_mean", "y_sq", "y_var", "zh", "zh_mm",
)


def build(nc, io):
    SCB, SCC = DH ** -0.5, (DNOPE + DROPE) ** -0.5
    with ExitStack() as ctx:
        def sb(name, cols):
            return ctx.enter_context(nc.sbuf_tensor(name, [P, cols], F32))

        def sem(name):
            return ctx.enter_context(nc.semaphore(name))

        x = sb("x", KD * T)[:, :].rearrange("p (k t) -> p k t", k=KD)
        h = sb("h", KD * T)[:, :].rearrange("p (k t) -> p k t", k=KD)
        cst = sb("cst", NCONST)
        par = sb("par", NPAR)
        kvn = sb("kvn", KV_LORA)
        ya, yb, yc = [sb(n, 4 * T)[:, :].rearrange("p (k t) -> p k t", k=4) for n in ("ya", "yb", "yc")]
        lora = sb("lora", 2 * W_A)
        sml = sb("sml", 16)
        big = sb("big", 7680)
        ring = sb("ring", NSLOT * SLOT)
        reg = sb("reg", 17408)
        ptab = ctx.enter_context(nc.sbuf_tensor("ptab", [1, NB * N_PAGES], I32))
        ps = ctx.enter_context(nc.psum_tensor("ps", [P, 8, 512], F32))

        def C(name, rows=P):
            at, w = CONST[name]
            return cst[0:rows, at:at + w]

        def pp(name, m, rows=P):
            return par[0:rows, PAR[name][0] + m:PAR[name][0] + m + 1]

        def cut(buf, at, a, b, rows=P):
            return buf[0:rows, at:at + a * b].rearrange("p (a b) -> p a b", a=a)

        ident, ones, onesblk = C("ident"), C("ones"), C("onesblk")
        act_t = cut(big, 0, KF, T)
        sqb = cut(big, 0, KD, T)
        yt = cut(reg, 0, KD, T)
        sg2 = cut(reg, 2560, 2, T)
        rstd = reg[:, 3200:3200 + T]
        gates = cut(big, 0, 24, T)
        mt = cut(reg, 4096, KD, T)
        pa = cut(reg, 0, NAT, PADT)
        xs = cut(big, 0, NAT, T)
        S_ = [cut(reg, NAT * PADT + 1280 * i, 4, T) for i in range(10)]
        th, sgd = reg[:, 0:T], reg[:, T:2 * T]
        Hp = cut(reg, 640, H, DH, 64)
        Ue, Ve, Tm = [cut(reg, 1152 + 512 * i, NB, DH, CHUNK) for i in range(3)]
        Odd = [cut(reg, 2688 + 256 * i, 4, CHUNK, 64) for i in range(5)]
        MX = [cut(ring, 512 * i, H, CHUNK, CHUNK) for i in range(20)]
        (X8, X8T, Xo16, Xo32, Xo64, KK, RB, RK, X2, X2T, X4, Pm, Tt, TT, G, RHS, U, Vr, bdr, kdr) = MX
        Hse, Hso = cut(ring, 10240, 4, NB * DH, 64), cut(big, NAT * T, 4, NB * DH, 64)
        Hs = lambda hd: (Hso if hd % 2 else Hse)[:, hd // 2, :]
        lastT = cut(reg, 16126, NAT, 9)
        shin = cut(reg, 16326, NAT, NB)
        PBc = cut(reg, 0, 3, C_COLS)
        PBq = cut(reg, 2016, 3, 2048)
        PBv = cut(reg, 8160, 3, W_A)
        qT = cut(reg, 9696, 12, T)
        kT = cut(reg, 13536, 4, T)
        rt = reg[:, 14816:14816 + 1024]
        Sp = [big[:, 768 * i:768 * i + 768].rearrange("p (g k) -> p g k", g=3) for i in range(2)]
        Pc = [big[:, 1536 + 256 * i:1792 + 256 * i] for i in range(2)]
        PTp = [cut(big, 2048 + 256 * i, 2, P) for i in range(2)]
        OLp = [cut(big, 2560 + 256 * i, 2, P) for i in range(2)]
        Kw = cut(big, 0, SW_TILES, W_A)
        Qbd = big[:, 6656:6656 + 768].rearrange("p (c g n) -> p c g n", c=4, g=3)
        Vw = cut(ring, 0, SW_TILES, W_A)
        Sw = [ring[0:NS, 6656:6656 + SW_COLS], reg[0:NS, 4064:4064 + SW_COLS]]
        KTw = [cut(ring, 8344, 4, 512), cut(reg, 2016, 4, 512)]
        PTw = cut(ring, 10392, SW_TILES, NS)
        Ow = cut(reg, 5752, H, DH, NS)
        PTn = ring[0:NS, 11224:11224 + NS]
        PnF = ring[0:NS, 11288:11288 + NS]
        cqT = cut(reg, 2016, 3, T)
        cup = cut(reg, 2976, 3, H * 96)
        kvup = cut(reg, 5280, 2, 1024)
        qrow = cut(reg, 7328, 3, H * 96)
        qcT = cut(reg, 9632, H, T)
        kvT = cut(reg, 12192, H, KV_LORA, DNOPE)
        ckvT = cut(reg, 16448, 3, T)
        rt2 = reg[:, 14240:14240 + 1024]
        olT = rt2.rearrange("p (c h t) -> p c h t", c=2, h=H)
        QR = reg[:, 15264:15264 + 512].rearrange("p (b h j) -> p b h j", b=NB, h=H)
        Osb = reg[0:NS, 15776:15776 + 256]
        PnL = reg[0:NS, 16032:16032 + NS]
        PTl = reg[0:NS, 16096:16096 + NS]
        KR = [cut(big, 3072, N_PAGES, 288), cut(ring, 0, N_PAGES, 288), cut(reg, 7328, N_PAGES, 288)]
        qlT = ring[:, 0:4096].rearrange("p (h c t) -> p h c t", h=H, c=2)
        QL = ring[:, 4608:5632].rearrange("p (c b n) -> p c b n", c=2, b=NB)
        KTl = [cut(ring, 5632 + 1536 * i, 3, 512) for i in range(2)]
        Pl = ring[0:NS, 8704:8704 + PAST + TS]
        PTL = cut(ring, 10760, N_PAGES, NS)

        s_dve = sem("vector_step")
        s_par, s_sml, s_out = sem("params_in"), sem("small_in"), sem("rows_out")
        s_slot = [sem(f"weights_in_{i}") for i in range(NSLOT)]
        s_kw = [sem(f"window_keys_in_{i}") for i in range(4)]
        s_vw, s_copy = sem("window_values_in"), sem("window_copied")
        s_kr = [sem(f"pages_in_{i}") for i in range(3)]
        s_shin, s_shout, s_state, s_wkv = sem("shift_in"), sem("shift_out"), sem("states_in"), sem("states_out")
        s_once, s_arrive, s_go, s_pad = sem("constants_in"), sem("engines_at_layer_end"), sem("layer_begun"), sem("pad")
        S = {n: sem(n) for n in STEPS}
        per_layer = [s_dve, s_par, s_sml, s_out, s_vw, s_state, s_wkv, s_shin, s_shout] + s_kw + s_kr + s_slot + list(S.values())
        units = weight_units(io)
        uidx = {name: i for i, (name, _) in enumerate(units)}

        def landed(name):
            i = uidx[name]
            return s_slot[i % NSLOT], 16 * sum(len(units[j][1]) for j in range(i % NSLOT, i + 1, NSLOT))

        def used(name):
            kind, u = name[0], name[-1]
            if kind in ("f1", "f2"):
                return (S["ffn_gu"], FFN0[kind] + 2 * u + 2) if name[1] == "gu" else (S["down_d"], DOWN0[kind] + u + 1)
            return {"pa": lambda: (S["pam"], min(4 * u + 4, NAT)), "pbc": lambda: (S["pbc_mm"], 3 * u + 3),
                    "pg": lambda: (S["pgm"], 4 * u + 4), "br": lambda: (S["brm"], KD * "abc".index(str(u)) + KD),
                    "wo": lambda: (S["down_d"], DOWN0["mix"] + 4 * u + 4)}[kind]()

        def wslot(name, k, n, at=0):
            o = (uidx[name] % NSLOT) * SLOT + at
            return ring[:, o:o + k * n].rearrange("p (k n) -> p k n", k=k)

        def layer_end(eng, l):
            eng.sem_inc(s_arrive, 1)
            eng.wait_ge(s_go, l + 1)
            eng.sem_inc(s_pad, 1)

        def lay(ap, l):
            return ap[bass.ds(l, 1)]

        block = ctx.enter_context(nc.Block())

        def rwkv_sync(sp, l):
            sp.wait_ge(S["pa_zeroed"], 1)
            sp.dma_start(shin, lay(io["shiftT"], l).rearrange("a p n b -> p (a n) b")).then_inc(s_shin, 16)
            sp.wait_ge(*used(("pa", 3)))
            for r, buf in ((0, Hse), (1, Hso)):
                sp.dma_start(buf, lay(io["wkvT"], l)[:, r].rearrange("a p n v -> p (a n) v")).then_inc(s_state, 16)
            sp.wait_ge(S["last_rows"], 1)
            sp.dma_start(lay(io["o_shift"], l).rearrange("a p n b -> p (a n) b"), lastT).then_inc(s_shout, 16)
            sp.wait_ge(S["group"], 5)
            sp.dma_start(lay(io["o_wkv_p"], l).rearrange("a p n v -> p (a n) v"), Hp).then_inc(s_wkv, 16)
            for r, buf in ((0, Hse), (1, Hso)):
                sp.dma_start(lay(io["o_wkv_s"], l)[:, r].rearrange("a p n v -> p (a n) v"), buf).then_inc(s_wkv, 16)
            sp.wait_ge(S["rwkv_done"], 1)
            sp.wait_ge(s_wkv, 16 * 3)

        def attention_sync(sp, l):
            sp.wait_ge(S["rows_ready"], 3)
            for name, src in (("swa_k", PBq[:, :, 1536:2048]), ("swa_v", PBv), ("ckv", PBc[:, :, Q_LORA:Q_LORA + KV_LORA]),
                              ("krope", PBc[:, :, Q_LORA + KV_LORA:C_COLS])):
                sp.dma_start(lay(io[f"o_{name}_p"], l).rearrange("a b (t p) n -> p (a b t) n", p=P), src[:, 0:2, :]).then_inc(s_out, 16)
                if name.startswith("swa"):
                    for b in range(NB):
                        dst = lay(io[f"o_{name}_s"], l)[:, b, PAST - TS:PAST, :].rearrange("a r n -> (a r) n")
                        sp.dma_start(dst, src[TS * b:TS * b + TS, 2, :]).then_inc(s_out, 16)
                else:
                    dst = lay(io[f"o_{name}_s"], l).rearrange("a b t n -> (a b t) n")
                    sp.dma_start(dst, src[0:NS, 2, :]).then_inc(s_out, 16)

            def window(cache, b, part):
                src = lay(cache, l)[:, b]
                if part < 2:
                    return src.rearrange("a (p r) n -> p (a r) n", r=16)[:, 4 * part:4 * part + 4, :]
                if part == 2:
                    return src[:, PAST - 512:PAST].rearrange("a (p r) n -> p (a r) n", r=4)
                return src[:, PAST - P:PAST].rearrange("a p n -> p a n")

            def keys(b, parts):
                for i in parts:
                    if b:
                        sp.wait_ge(S["kt_T"], 16 * (b - 1) + 4 * i + 4)
                    sp.dma_start(Kw[:, 4 * i:min(4 * i + 4, SW_TILES), :], window(io["cache_swa_k"], b, i)).then_inc(s_kw[i], 16)

            keys(0, (2, 3))
            for b in range(NB):
                if b:
                    sp.wait_ge(S["sw_pv"], b)
                for i in range(4):
                    sp.dma_start(Vw[:, 4 * i:min(4 * i + 4, SW_TILES), :], window(io["cache_swa_v"], b, i)).then_inc(s_vw, 16)
                if b == 0:
                    sp.wait_ge(S["prompt_y"], 16)
                    keys(0, (0, 1))
                    keys(1, range(4))
                if b + 2 < NB:
                    keys(b + 2, range(4))
            sp.wait_ge(S["sws_done"], NB)
            sp.wait_ge(s_out, N_ROWS_OUT)
            sp.dma_start(cup, lay(io["c_q_up"], l).rearrange("a (k p) n -> p (a k) n", p=P)).then_inc(s_sml, 16)
            sp.dma_start(kvup, lay(io["c_kv_up"], l).rearrange("a (k p) n -> p (a k) n", p=P)).then_inc(s_sml, 16)
            for b in range(NB):
                if b in (1, 2):
                    sp.wait_ge(S["prompt_y"], 2 * H + 16)
                elif b:
                    sp.wait_ge(S["ml_pv"], b - 2)
                for n in range(N_PAGES):
                    i = b * N_PAGES + n
                    page = sp.value_load(ptab[0:1, i:i + 1], min_val=0, max_val=N_POOL - 1)
                    for c0, cache, w in ((0, "ckv", KV_LORA), (KV_LORA, "krope", DROPE)):
                        src = lay(io["cache_mla_" + cache], l)[:, bass.ds(page, 1)].rearrange("a b p n -> p (a b n)")
                        sp.dma_start(KR[b % 3][:, n, c0:c0 + w], src).then_inc(s_kr[b % 3], 16)
            sp.wait_ge(S["ml_done"], 1)

        @block.sync
        def _(sp):
            sp.dma_start(cst[:, :], io["consts"]).then_inc(s_once, 16)
            sp.dma_start(x, io["xT"]).then_inc(s_once, 16)
            sp.dma_start(ptab[:, :], io["page_table"].rearrange("b n -> (b n)").unsqueeze(0)).then_inc(s_once, 16)
            sp.wait_ge(s_once, 48)
            with sp.Fori(0, DEPTH) as l:
                sp.dma_start(par[:, :], lay(io["params"], l).rearrange("a p n -> p (a n)")).then_inc(s_par, 16)
                sp.dma_start(kvn[:, :], lay(io["c_kv_norm"], l).rearrange("a n -> (a n)").partition_broadcast(P)).then_inc(s_par, 16)
                for lo, hi, name in ((0, 32, "a_w2"), (32, 64, "a_a2")):
                    sp.dma_start(lora[lo:hi, 0:W_A], lay(io[name], l).rearrange("a p n -> p (a n)")).then_inc(s_par, 16)
                sp.dma_start(lora[0:96, W_A:2 * W_A], lay(io["a_g2"], l).rearrange("a p n -> p (a n)")).then_inc(s_par, 16)
                for i, (name, srcs) in enumerate(units):
                    if name == ("pbc", 0):
                        rwkv_sync(sp, l)
                    if name == ("pg", 0):
                        attention_sync(sp, l)
                    if i >= NSLOT:
                        sp.wait_ge(*used(units[i - NSLOT][0]))
                    at = (i % NSLOT) * SLOT
                    for src, k, n in srcs:
                        sp.dma_start(ring[:, at:at + k * n].rearrange("p (k n) -> p k n", k=k), src(l)).then_inc(s_slot[i % NSLOT], 16)
                        at += k * n
                sp.wait_ge(S["x_f2"], 1)
                sp.wait_ge(S["roots"], ROOTS["f2_post"])
                sp.wait_ge(S["norm_sums"], NORMS["f2_post"])
                sp.wait_ge(s_out, N_ROWS_OUT)
                sp.wait_ge(s_wkv, 16 * 3)
                sp.wait_ge(s_shout, 16)
                sp.wait_ge(s_arrive, 4 * (l + 1))
                sp.sem_inc(s_pad, 1)
                for s in per_layer:
                    sp.sem_clear(s)
                sp.sem_inc(s_go, 1)
            sp.dma_start(io["yT"], x).then_inc(s_once, 16)
            sp.wait_ge(s_once, 64)

        @block.gpsimd
        def _(pool):
            with pool.Fori(0, DEPTH) as l:
                rows = PAST - TS
                copies = 0
                pool.wait_ge(S["ffn_gu"], 2)
                for b in range(NB):
                    for n in ("k", "v"):
                        if copies:
                            pool.wait_ge(s_copy, l * (16 * 2 * NB) + 16 * copies)
                            pool.sem_inc(s_pad, 1)
                        copies += 1
                        src = lay(io["cache_swa_" + n], l)[:, b, TS:PAST].rearrange("a r n -> (a r n)")
                        dst = lay(io[f"o_swa_{n}_s"], l)[:, b, 0:rows].rearrange("a r n -> (a r n)")
                        pool.dma_start(dst.rearrange("(q n) -> q n", q=240),
                                       src.rearrange("(q n) -> q n", q=240)).then_inc(s_copy, 16)
                pool.wait_ge(s_copy, (l + 1) * (16 * 2 * NB))
                layer_end(pool, l)

        @block.tensor
        def _(pe):
            pe.wait_ge(s_once, 48)

            def mm(out, lhsT, rhs, first=True, last=True):
                return pe.matmul(out, lhsT, rhs, start=first, stop=last, skip_group_check=True)

            def tr(out, in_, rows=P):
                return pe.transpose(out, in_, ident[0:rows, 0:rows])


            def norm_sum(tag, src):
                for k in range(KD):
                    m = mm(ps[:, 7, 0:T], ones, src[:, k, :], k == 0, k == KD - 1)
                m.then_inc(S["norm_sums"], 1)

            def ffn(f):
                pe.wait_ge(S["squared"], PRES[f + "_pre"])
                norm_sum(f + "_pre", sqb)
                pe.wait_ge(S["normed"], PRES[f + "_pre"])
                for m in range(KF):
                    u = (f, "gu", m // 2)
                    pe.wait_ge(*landed(u))
                    if m >= 3:
                        pe.wait_ge(S["ffn_a"], FFN0[f] + m - 2)
                    for bank, at in ((m % 3, 0), (3 + m % 3, 2048)):
                        w = wslot(u, KD, 256, at)
                        for k in range(KD):
                            q = mm(ps[:, bank, 0:T], w[:, k, (m % 2) * P:(m % 2) * P + P], h[:, k, :], k == 0, k == KD - 1)
                    q.then_inc(S["ffn_gu"], 1)
                pe.wait_ge(S["ffn_a"], FFN0[f] + KF)
                for m in range(KD):
                    u = (f, "d", m)
                    pe.wait_ge(*landed(u))
                    if m >= 4:
                        pe.wait_ge(S["down_y"], DOWN0[f] + m - 3)
                    w = wslot(u, KF, P)
                    for k in range(KF):
                        q = mm(ps[:, m % 4, 0:T], w[:, k, :], act_t[:, k, :], k == 0, k == KF - 1)
                    q.then_inc(S["down_d"], 1)
                pe.wait_ge(S["down_y"], DOWN0[f] + KD)
                norm_sum(f + "_post", h)

            def a_proj():
                pe.wait_ge(S["squared"], PRES["mix_pre"])
                norm_sum("mix_pre", sqb)
                pe.wait_ge(S["normed"], PRES["mix_pre"])
                for m, (c0, rows) in enumerate(A_TILES):
                    u = ("pa", min(c0 // 512, 3))
                    pe.wait_ge(*landed(u))
                    if m >= 6:
                        pe.wait_ge(S["pa"], m - 5)
                    n = 512 if c0 < 1536 else 160
                    w, at = wslot(u, KD, n), c0 - 512 * (c0 // 512)
                    for k in range(KD):
                        q = mm(ps[0:rows, m % 6, 0:T], w[:, k, at:at + rows], h[:, k, :], k == 0, k == KD - 1)
                    q.then_inc(S["pam"], 1)

            def rwkv():
                pe.wait_ge(S["tanh"], 1)
                for m in range(4):
                    mm(ps[:, m, 0:T], lora[0:32, m * P:m * P + P], th[0:32, :])
                    q = mm(ps[:, 4 + m, 0:T], lora[32:64, m * P:m * P + P], xs[32:64, 12, :])
                q.then_inc(S["lora_wa"], 1)
                pe.wait_ge(S["a_ready"], 4)
                for m in range(4):
                    q = mm(ps[:, m, 0:T], lora[0:96, W_A + m * P:W_A + m * P + P], sgd[0:96, :])
                q.then_inc(S["lora_g"], 1)
                pe.wait_ge(S["kk_sq"], 1)
                for m in range(4):
                    q = mm(ps[:, 4 + m, 0:T], onesblk, S_[9][:, m, :])
                q.then_inc(S["kk_ss"], 1)
                pe.wait_ge(S["bonus_in"], 1)
                pe.wait_ge(S["g_ready"], 1)
                for m in range(4):
                    q = mm(ps[:, m, 0:T], onesblk, S_[9][:, m, :])
                q.then_inc(S["bonus_ss"], 1)
                pe.wait_ge(S["streams"], 1)
                ZT, bdT, kdT, RqT, vT = S_[6], S_[0], S_[7], S_[3], xs[:, 8:12]
                for g in range(5):
                    t0, sample = g * CHUNK, g == 4
                    odd = {id(ZT): Odd[0], id(bdT): Odd[1], id(kdT): Odd[2], id(RqT): Odd[3]}
                    at = lambda a, hd: odd[id(a)][:, hd // 2, :] if hd % 2 else a[0:64, hd // 2, t0:t0 + CHUNK]
                    bank = lambda b, hd: ps[0:64, b, 64 * hd:64 * hd + 64]

                    def each(b, name, f):
                        for hd in range(H):
                            q = f(bank(b, hd), hd)
                        if name is not None:
                            q.then_inc(S[name], 1)

                    if g:
                        pe.wait_ge(S["group"], g)
                    for b, a in ((0, vT), (1, bdT), (2, kdT)):
                        for m in range(4):
                            q = tr(ps[0:64, b, m * P:m * P + P], a[:, m, t0:t0 + CHUNK])
                    q.then_inc(S["rows"], 1)
                    pe.wait_ge(S["odd"], 5 * g + 5)
                    each(3, None, lambda o, hd: mm(o, at(ZT, hd), at(bdT, hd)))
                    each(4, None, lambda o, hd: mm(o, at(bdT, hd), at(ZT, hd)))
                    each(5, None, lambda o, hd: mm(o, at(kdT, hd), at(ZT, hd)))
                    each(6, None, lambda o, hd: mm(o, at(bdT, hd), at(RqT, hd)))
                    each(7, "RK", lambda o, hd: mm(o, at(kdT, hd), at(RqT, hd)))
                    pe.wait_ge(S["masked"], g + 1)
                    each(0, None, lambda o, hd: mm(o, X8T[:, hd], X8[:, hd]))
                    each(1, "X2T", lambda o, hd: mm(o, X8[:, hd], X8T[:, hd]))
                    pe.wait_ge(S["x2"], g + 1)
                    each(2, "X4", lambda o, hd: mm(o, X2T[:, hd], X2[:, hd]))
                    pe.wait_ge(S["x4"], g + 1)
                    each(3, "X6", lambda o, hd: mm(o, X2T[:, hd], X4[:, hd]))
                    pe.wait_ge(S["pm"], g + 1)
                    each(4, "XP", lambda o, hd: mm(o, X8T[:, hd], Pm[:, hd]))
                    pe.wait_ge(S["t"], g + 1)
                    each(5, "TT", lambda o, hd: tr(o, Tt[:, hd], 64))
                    pe.wait_ge(S["tt"], g + 1)
                    if not sample:
                        for i, xo in enumerate((Xo16, Xo32, Xo64)):
                            each(0, "G", lambda o, hd: mm(o, xo[:, hd], Tt[:, hd]))
                            pe.wait_ge(S["g_level" ], 3 * g + i + 1)
                            each(1, None, lambda o, hd: mm(o, TT[:, hd], G[:, hd]))
                            each(2, "dTT", lambda o, hd: mm(o, G[:, hd], TT[:, hd]))
                            pe.wait_ge(S["t_level" ], 3 * g + i + 1)
                        for hd in range(H):
                            mm(bank(3, hd), at(ZT, hd), Hp[:, hd, :], True, False)
                            q = mm(bank(3, hd), KK[:, hd], Vr[:, hd], False, True)
                        q.then_inc(S["rhs"], 1)
                    else:
                        pe.wait_ge(s_state, 32)
                        for hd in range(H):
                            if hd >= 2:
                                pe.wait_ge(S["zh"], hd - 1)
                            mm(ps[0:64, hd % 2, :], at(ZT, hd), Hs(hd)).then_inc(S["zh_mm"], 1)
                        each(3, "rhs", lambda o, hd: mm(o, KK[:, hd], Vr[:, hd]))
                    pe.wait_ge(S["rhs_ev"], g + 1)
                    each(4, "u", lambda o, hd: mm(o, TT[:, hd], RHS[:, hd]))
                    pe.wait_ge(S["u_ev"], g + 1)
                    for hd in range(H):
                        r0 = 64 * (hd % 2)
                        o = ps[r0:r0 + 64, 5, 64 * (hd // 2):64 * (hd // 2) + 64]
                        mm(o, U[:, hd], RB[:, hd], True, False)
                        q = mm(o, Vr[:, hd], RK[:, hd], False, False)
                        if not sample:
                            q = mm(o, Hp[:, hd, :], at(RqT, hd), False, True)
                        else:
                            for b in range(NB):
                                q = mm(o[:, TS * b:TS * b + TS], Hs(hd)[:, DH * b:DH * b + DH],
                                       at(RqT, hd)[:, TS * b:TS * b + TS], False, b == NB - 1)
                    q.then_inc(S["y"], 1)
                    if not sample:
                        for hd in range(H):
                            o = bank(6, hd)
                            mm(o, bdr[:, hd], U[:, hd], True, False)
                            q = mm(o, kdr[:, hd], Vr[:, hd], False, True)
                        q.then_inc(S["h"], 1)
                    else:
                        for hd in range(H):
                            pe.wait_ge(S["ue"], hd + 1)
                            mm(ps[0:64, 6 + hd % 2, :], bdr[:, hd], Ue.rearrange("p b v -> p (b v)"), True, False)
                            q = mm(ps[0:64, 6 + hd % 2, :], kdr[:, hd], Ve.rearrange("p b v -> p (b v)"), False, True)
                            q.then_inc(S["hs"], 1)
                Y = S_[8]
                pe.wait_ge(S["group"], 5)
                for m in range(4):
                    q = mm(ps[:, m, 0:T], onesblk, Y[:, m, :])
                q.then_inc(S["y_mean"], 1)
                pe.wait_ge(S["y_sq"], 1)
                for m in range(4):
                    q = mm(ps[:, 4 + m, 0:T], onesblk, S_[0][:, m, :])
                q.then_inc(S["y_var"], 1)

            def bc_proj():
                pe.wait_ge(S["rwkv_done"], 1)
                n = 0
                for u in range(7):
                    pe.wait_ge(*landed(("pbc", u)))
                    cols = 160 if u == 1 else 512
                    w = wslot(("pbc", u), KD, cols)
                    for i, t0, rows in TOK_TILES:
                        if n >= 6:
                            pe.wait_ge(S["pbc_ev"], n - 5)
                        for k in range(KD):
                            q = mm(ps[0:rows, n % 6, 0:cols], h[:, k, t0:t0 + rows], w[:, k, :], k == 0, k == KD - 1)
                        q.then_inc(S["pbc_mm"], 1)
                        n += 1
                pe.wait_ge(S["rows_ready"], 3)
                n = 0
                for c in range(16):
                    if c >= 4:
                        pe.wait_ge(S["qk_ev"], c - 3)
                    for i, t0, rows in TOK_TILES:
                        q = tr(ps[:, c % 4, t0:t0 + rows], PBq[0:rows, i, c * P:c * P + P], rows)
                    q.then_inc(S["qkT"], 1)
                pe.wait_ge(S["qk_ev"], 16)
                for j, c0 in enumerate((Q_LORA, Q_LORA + P, C_COLS - 96)):
                    w = 96 if j == 2 else P
                    for i, t0, rows in TOK_TILES:
                        q = tr(ps[0:w, j, t0:t0 + rows], PBc[0:rows, i, c0:c0 + w], rows)
                q.then_inc(S["ckvT"], 1)

            def sw_prompt():
                pe.wait_ge(S["ckvT_ev"], 1)

                def scores(n):
                    t, hd = n // H, n % H
                    r0 = 64 * (hd % 2)
                    if n >= 2:
                        pe.wait_ge(S["prompt_s"], n - 1)
                    for g in range(3):
                        col = (n % 2) * 1024 + g * 256
                        o = ps[:, col // 512, col % 512:col % 512 + 256]
                        q = mm(o, qT[r0:r0 + 64, 4 * g + hd // 2, t * P:t * P + P], kT[r0:r0 + 64, hd // 2, 0:SEQ])
                    q.then_inc(S["prompt_mm"], 1)

                scores(0)
                for n in range(16):
                    if n + 1 < 16:
                        scores(n + 1)
                    hd = n % H
                    pe.wait_ge(S["prompt_p"], n + 1)
                    for i in range(2):
                        q = tr(ps[:, 4 + n % 2, i * P:i * P + P], Pc[n % 2][:, i * P:i * P + P])
                    q.then_inc(S["prompt_T"], 1)
                    pe.wait_ge(S["prompt_pt"], n + 1)
                    r0 = 64 * (hd % 2)
                    for i in range(2):
                        q = mm(ps[r0:r0 + 64, 6 + n % 2, 0:P], PBv[:, i, hd * 64:hd * 64 + 64], PTp[n % 2][:, i, :], i == 0, i == 1)
                    q.then_inc(S["prompt_o"], 1)

            def sw_sample():
                pe.wait_ge(S["prompt_y"], 16)

                def transposes(part):
                    b, q4 = part // 4, part % 4
                    pe.wait_ge(s_kw[q4], 16 * (b + 1))
                    for c in range(4):
                        n = 4 * part + c
                        if n >= 2:
                            pe.wait_ge(S["kt_ev"], n - 1)
                        for t in range(4 if q4 < 3 else 1):
                            q = tr(ps[:, 4 + n % 2, t * P:t * P + P], Kw[:, 4 * q4 + t, c * P:c * P + P])
                        q.then_inc(S["kt_T"], 1)

                def scores(part):
                    b, q4 = part // 4, part % 4
                    nt = 4 if q4 < 3 else 1
                    g = 2 if q4 < 2 else 1 if q4 == 2 else 0
                    if q4 == 0:
                        pe.wait_ge(S["qbd"], 8 * b + 8)
                        if b:
                            pe.wait_ge(S["sw_masked"], b)
                    for c in range(4):
                        pe.wait_ge(S["kt_ev"], 4 * part + c + 1)
                        q = mm(ps[0:NS, q4, 0:nt * P], Qbd[:, c, g, :], KTw[part % 2][:, c, 0:nt * P], c == 0, c == 3)
                    q.then_inc(S["sw_mm"], 1)
                    if q4 == 3:
                        for g in range(3):
                            for c in range(4):
                                q = mm(ps[0:NS, 3, P + g * TS:P + g * TS + TS], Qbd[:, c, g, :],
                                       kT[:, c, SEQ + TS * b:SEQ + TS * b + TS], c == 0, c == 3)
                        q.then_inc(S["sw_s"], 1)

                def values(b):
                    pe.wait_ge(S["sw_p"], b + 1)
                    if b:
                        pe.wait_ge(S["sws_done"], b)
                    for t in range(SW_TILES):
                        q = tr(ps[:, 6 + t // 8, (t % 8) * NS:(t % 8) * NS + NS], Sw[b % 2][:, t * P:t * P + P], NS)
                    q = tr(ps[0:NS, 7, 320:384], PnF, NS)
                    q.then_inc(S["sw_PT"], 1)
                    pe.wait_ge(S["sw_pt"], b + 1)
                    pe.wait_ge(s_vw, 64 * (b + 1))
                    for t in range(SW_TILES):
                        mm(ps[0:NS, 7, :], PTw[:, t, :], Vw[:, t, :], t == 0, False)
                    mm(ps[0:NS, 7, :], PTn, PBv[0:NS, 2, :], False, True).then_inc(S["sw_pv"], 1)

                def by_channel(b):
                    pe.wait_ge(S["sw_own"], b + 1)
                    for c in range(4):
                        q = mm(ps[:, 6, c * TS:c * TS + TS], Ow.rearrange("p h v -> p (h v)")[:, c * P:c * P + P], C("tsel", NS))
                    q.then_inc(S["sw_y"], 1)

                transposes(0)
                for part in range(4 * NB):
                    if part + 1 < 4 * NB:
                        transposes(part + 1)
                    if part % 4 == 0 and part >= 8:
                        by_channel(part // 4 - 2)
                    scores(part)
                    if part % 4 == 3 and part > 4:
                        values(part // 4 - 1)
                by_channel(NB - 2)
                values(NB - 1)
                by_channel(NB - 1)

            def latent_prep():
                pe.wait_ge(S["sws_done"], NB)
                for k in range(3):
                    for i, t0, rows in TOK_TILES:
                        q = tr(ps[:, k, t0:t0 + rows], PBc[0:rows, i, k * P:k * P + P], rows)
                q.then_inc(S["cqT"], 1)
                pe.wait_ge(s_sml, 32)
                for hd in range(H):
                    for c in range(2):
                        q = tr(ps[:, 3 + hd // 2, (hd % 2) * 256 + c * P:(hd % 2) * 256 + c * P + P], kvup[:, c, hd * P:hd * P + P])
                q.then_inc(S["kvT"], 1)
                pe.wait_ge(S["kvT_ev"], 1)
                n = 0
                for i, t0, rows in TOK_TILES:
                    for j in range(2):
                        for k in range(3):
                            q = mm(ps[0:rows, n, 0:384], cqT[:, k, t0:t0 + rows], cup[:, k, j * 384:j * 384 + 384], k == 0, k == 2)
                        n += 1
                q.then_inc(S["q_rows"], 1)
                pe.wait_ge(S["q_rope"], 3)
                for hd in range(H):
                    if hd >= 4:
                        pe.wait_ge(S["qcT_ev"], hd - 3)
                    for i, t0, rows in TOK_TILES:
                        q = tr(ps[0:96, hd % 4, t0:t0 + rows], qrow[0:rows, i, hd * 96:hd * 96 + 96], rows)
                    q.then_inc(S["qcT"], 1)
                for n in range(16):
                    pe.wait_ge(S["qcT_ev"], max(n // 2, 7) + 1)
                    if n >= 4:
                        pe.wait_ge(S["ql_ev"], n - 3)
                    mm(ps[:, 4 + n % 4, 0:T], kvT[:, n // 2, (n % 2) * P:(n % 2) * P + P], qcT[0:64, n // 2, :]).then_inc(S["ql"], 1)

            def ml_prompt():
                pe.wait_ge(S["ml_prep"], 1)

                def scores(n):
                    t, hd = n // H, n % H
                    if n >= 2:
                        pe.wait_ge(S["prompt_s"], 2 * H + n - 1)
                    o = ps[:, n % 2, 0:SEQ]
                    for c in range(2):
                        mm(o, qlT[:, hd, c, t * P:t * P + P], ckvT[:, c, 0:SEQ], c == 0, False)
                    mm(o, qcT[64:96, hd, t * P:t * P + P], ckvT[64:96, 2, 0:SEQ], False, True).then_inc(S["prompt_mm"], 1)

                scores(0)
                for n in range(16):
                    if n + 1 < 16:
                        scores(n + 1)
                    hd = n % H
                    pe.wait_ge(S["prompt_p"], 2 * H + n + 1)
                    for i in range(2):
                        q = tr(ps[:, 2 + n % 2, i * P:i * P + P], Pc[n % 2][:, i * P:i * P + P])
                    q.then_inc(S["prompt_T"], 1)
                    pe.wait_ge(S["prompt_pt"], 2 * H + n + 1)
                    for c in range(2):
                        for i in range(2):
                            q = mm(ps[:, 4 + n % 2, c * P:c * P + P], PBc[:, i, Q_LORA + c * P:Q_LORA + c * P + P],
                                   PTp[n % 2][:, i, :], i == 0, i == 1)
                    q.then_inc(S["prompt_ol"], 1)
                    pe.wait_ge(S["prompt_olev"], n + 1)
                    r0 = 64 * (hd % 2)
                    for c in range(2):
                        q = mm(ps[r0:r0 + 64, 6 + n % 2, 0:P], kvup[:, c, hd * P + 64:hd * P + P], OLp[n % 2][:, c, :], c == 0, c == 1)
                    q.then_inc(S["prompt_o"], 1)

            def ml_sample():
                pe.wait_ge(S["prompt_y"], 2 * H + 16)

                def transposes(part):
                    b = part // 4
                    pe.wait_ge(s_kr[b % 3], 16 * 2 * N_PAGES * (b // 3 + 1))
                    for n in range(4 * part, 4 * part + 4):
                        if n >= 2:
                            pe.wait_ge(S["lt_odd" if n % 2 else "lt_even"], n // 2)
                        o, page = ps[:, 5 + n % 2, :], KR[b % 3][:, n % N_PAGES, :]
                        tr(o[:, 0:P], page[:, 0:P])
                        tr(o[:, P:2 * P], page[:, P:2 * P])
                        tr(o[0:96, 2 * P:3 * P], page[:, 192:288]).then_inc(S["lt_T"], 1)

                def scores(part):
                    b, q4 = part // 4, part % 4
                    if b and q4 == 0:
                        pe.wait_ge(S["ml_exp"], b)
                    pe.wait_ge(S["lt_even"], 2 * part + 2)
                    pe.wait_ge(S["lt_odd"], 2 * part + 2)
                    kt, qr = KTl[part % 2], QR[64:96, b].rearrange("p h j -> p (h j)")
                    for c in range(2):
                        mm(ps[0:NS, q4, :], QL[:, c, b, :], kt[:, c, :], c == 0, False)
                    mm(ps[0:NS, q4, :], qr, kt[64:96, 2, :], False, True).then_inc(S["ml_mm"], 1)
                    if q4 == 3:
                        o = ps[0:NS, 4, 0:TS]
                        tk = slice(SEQ + TS * b, SEQ + TS * b + TS)
                        for c in range(2):
                            mm(o, QL[:, c, b, :], ckvT[:, c, tk], c == 0, False)
                        mm(o, qr, ckvT[64:96, 2, tk], False, True).then_inc(S["ml_s"], 1)

                def values(b, tiles):
                    pe.wait_ge(S["ml_p"], b + 1)
                    if b:
                        pe.wait_ge(S["ml_olT"], b)
                    pe.wait_ge(S["lt_even"], tiles // 2)
                    pe.wait_ge(S["lt_odd"], tiles // 2)
                    for t in range(N_PAGES):
                        tr(ps[:, 5 + 2 * (t // 8), (t % 8) * NS:(t % 8) * NS + NS], Pl[:, t * P:t * P + P], NS)
                    tr(ps[0:NS, 6, 0:NS], PnL, NS).then_inc(S["ml_PT"], 1)
                    pe.wait_ge(S["ml_pt"], b + 1)
                    o = ps[0:NS, 4, 256:512]
                    for t in range(N_PAGES):
                        mm(o, PTL[:, t, :], KR[b % 3][:, t, 0:KV_LORA], t == 0, False)
                    mm(o, PTl, PBc[0:NS, 2, Q_LORA:Q_LORA + KV_LORA], False, True).then_inc(S["ml_pv"], 1)

                def by_channel(b):
                    pe.wait_ge(S["ml_osb"], b + 1)
                    for c in range(2):
                        q = tr(ps[:, 7, c * NS:c * NS + NS], Osb[:, c * P:c * P + P], NS)
                    q.then_inc(S["ml_oT"], 1)

                transposes(0)
                for part in range(4 * NB):
                    if part + 1 < 4 * NB:
                        transposes(part + 1)
                    if part % 4 == 0 and part >= 8:
                        by_channel(part // 4 - 2)
                    scores(part)
                    if part % 4 == 3 and part > 4:
                        values(part // 4 - 1, min(4 * part + 8, NB * N_PAGES))
                by_channel(NB - 2)
                values(NB - 1, NB * N_PAGES)
                by_channel(NB - 1)
                pe.wait_ge(S["ml_olT"], NB)
                for hd in range(H):
                    r0 = 64 * (hd % 2)
                    for c in range(2):
                        q = mm(ps[r0:r0 + 64, 0, (hd // 2) * NS:(hd // 2) * NS + NS], kvup[:, c, hd * P + 64:hd * P + P], olT[:, c, hd, :], c == 0, c == 1)
                q.then_inc(S["ml_yc"], 1)

            def mix():
                pe.wait_ge(S["ml_done"], 1)
                for m in range(24):
                    u = ("pg", m // 4)
                    pe.wait_ge(*landed(u))
                    if m >= 8:
                        pe.wait_ge(S["gate"], m - 7)
                    w = wslot(u, KD, 512)
                    for k in range(KD):
                        q = mm(ps[:, m % 8, 0:T], w[:, k, (m % 4) * P:(m % 4) * P + P], h[:, k, :], k == 0, k == KD - 1)
                    q.then_inc(S["pgm"], 1)
                pe.wait_ge(S["gate"], 24)
                for i, (br, y) in enumerate((("a", ya), ("b", yb), ("c", yc))):
                    u = ("br", br)
                    pe.wait_ge(*landed(u))
                    w = wslot(u, 4, D_MODEL)
                    for m in range(KD):
                        if 8 * i + m >= 8:
                            pe.wait_ge(S["br_ev"], 8 * i + m - 7)
                        for k in range(4):
                            q = mm(ps[:, m, 0:T], w[:, k, m * P:m * P + P], y[:, k, :], k == 0, k == 3)
                        q.then_inc(S["brm"], 1)
                pe.wait_ge(S["br_ev"], 24)
                for m in range(KD):
                    u = ("wo", m // 4)
                    pe.wait_ge(*landed(u))
                    if m >= 4:
                        pe.wait_ge(S["down_y"], DOWN0["mix"] + m - 3)
                    w = wslot(u, KD, 512)
                    for k in range(KD):
                        q = mm(ps[:, m % 4, 0:T], w[:, k, (m % 4) * P:(m % 4) * P + P], mt[:, k, :], k == 0, k == KD - 1)
                    q.then_inc(S["down_d"], 1)
                pe.wait_ge(S["down_y"], DOWN0["mix"] + KD)
                norm_sum("mix_post", h)

            with pe.Fori(0, DEPTH) as l:
                ffn("f1")
                a_proj()
                rwkv()
                bc_proj()
                sw_prompt()
                sw_sample()
                latent_prep()
                ml_prompt()
                ml_sample()
                mix()
                ffn("f2")
                layer_end(pe, l)

        @block.scalar
        def _(act):
            act.wait_ge(s_once, 48)

            def root(tag, v):
                act.wait_ge(S["mean_squares"], ROOTS[tag])
                act.activation(v, v, ACT.Sqrt).then_inc(S["roots"], 1)

            def square_x(tag):
                act.activation(sqb, x, ACT.Square).then_inc(S["squared"], 1)
                root(tag, rstd)

            def down(f):
                for m in range(KD):
                    act.wait_ge(S["down_d"], DOWN0[f] + m + 1)
                    act.activation(yt[:, m, :], ps[:, m % 4, 0:T], ACT.Copy)
                    act.activation(h[:, m, :], ps[:, m % 4, 0:T], ACT.Square).then_inc(S["down_y"], 1)
                root(f + "_post", rstd)

            def ffn(f):
                for m in range(KF):
                    act.wait_ge(S["ffn_gu"], FFN0[f] + m + 1)
                    if m >= 2:
                        act.wait_ge(S["ffn_a"], FFN0[f] + m - 1)
                    act.activation(sg2[:, m % 2, :], ps[:, m % 3, 0:T], ACT.Sigmoid).then_inc(S["ffn_sg"], 1)
                down(f)

            def rwkv():
                act.wait_ge(s_par, 16 * 5)
                act.wait_ge(S["pa_zeroed"], 1)
                for m, (_, rows) in enumerate(A_TILES):
                    act.wait_ge(S["pam"], m + 1)
                    act.activation(pa[0:rows, m, 1:1 + SEQ], ps[0:rows, m % 6, 0:SEQ], ACT.Copy)
                    act.activation(pa[0:rows, m, 1 + SEQ:].rearrange("p (b j) -> p b j", b=NB)[:, :, 1:], ps[0:rows, m % 6, SEQ:T].rearrange("p (b j) -> p b j", b=NB), ACT.Copy).then_inc(S["pa"], 1)
                act.wait_ge(S["mixed"], 1)
                act.activation(th[0:32, :], xs[0:32, 12, :], ACT.Tanh)
                act.activation(sgd[0:96, :], xs[0:96, 13, :], ACT.Sigmoid).then_inc(S["tanh"], 1)
                act.wait_ge(S["lora_wa"], 1)
                for m in range(4):
                    act.activation(S_[0][:, m, :], ps[:, m, 0:T], ACT.Sigmoid, bias=pp("a_w0", m))
                    act.activation(S_[1][:, m, :], ps[:, 4 + m, 0:T], ACT.Sigmoid, bias=pp("a_a0", m)).then_inc(S["a_ready"], 1)
                act.wait_ge(S["lora_g"], 1)
                act.activation(S_[2], ps[:, 0:4, 0:T], ACT.Copy).then_inc(S["g_ready"], 1)
                act.wait_ge(S["kk0"], 1)
                act.wait_ge(s_shout, 16)
                act.activation(S_[9], S_[8], ACT.Square).then_inc(S["kk_sq"], 1)
                act.wait_ge(S["L"], 1)
                act.activation(S_[5], S_[3], ACT.Exp)
                act.activation(S_[6], S_[4], ACT.Exp)
                act.activation(S_[7], S_[3], ACT.Exp, scale=-1.0).then_inc(S["exps"], 1)
                root("kk", S_[9])
                for g in range(5):
                    if g:
                        act.wait_ge(S["group"], g)
                    else:
                        act.wait_ge(S["streams"], 1)
                    for o, a in zip(Odd, (S_[6], S_[0], S_[7], S_[3], S_[5])):
                        act.activation(o, a[64:128, :, g * CHUNK:(g + 1) * CHUNK], ACT.Copy).then_inc(S["odd"], 1)
                act.wait_ge(S["y_centred"], 1)
                act.activation(S_[0], S_[8], ACT.Square).then_inc(S["y_sq"], 1)
                root("y", S_[1])

            def bc_proj():
                n = 0
                for u in range(7):
                    for i, _, rows in TOK_TILES:
                        act.wait_ge(S["pbc_mm"], n + 1)
                        dst = (PBc[0:rows, i, 0:512] if u == 0 else PBc[0:rows, i, 512:672] if u == 1 else
                               PBv[0:rows, i, :] if u == 6 else PBq[0:rows, i, (u - 2) * 512:(u - 1) * 512])
                        act.activation(dst, ps[0:rows, n % 6, 0:160 if u == 1 else 512], ACT.Copy).then_inc(S["pbc_ev"], 1)
                        n += 1
                act.wait_ge(S["latent_ms"], 6)
                act.activation(sml[:, 8:14], sml[:, 8:14], ACT.Sqrt).then_inc(S["latent_root"], 1)
                for c in range(16):
                    act.wait_ge(S["qkT"], c + 1)
                    act.activation(qT[:, c, :] if c < 12 else kT[:, c - 12, :], ps[:, c % 4, 0:T], ACT.Copy).then_inc(S["qk_ev"], 1)
                act.wait_ge(S["ckvT"], 1)
                act.activation(ckvT[:, 0:2, :], ps[:, 0:2, 0:T], ACT.Copy)
                act.activation(ckvT[0:96, 2, :], ps[0:96, 2, 0:T], ACT.Copy).then_inc(S["ckvT_ev"], 1)

            def sw_prompt():
                for n in range(16):
                    act.wait_ge(S["prompt_nm"], n + 1)
                    act.activation(Sp[n % 2], Sp[n % 2], ACT.Exp, scale=SCB, bias=sml[:, 2 + n % 2:3 + n % 2], accum_out=sml[:, 4 + n % 2:5 + n % 2]).then_inc(S["prompt_e"], 1)

            def sw_sample():

                def keys_out(part):
                    for c in range(4):
                        n = 4 * part + c
                        w = P if part % 4 == 3 else 512
                        act.wait_ge(S["kt_T"], n + 1)
                        if part >= 2:
                            act.wait_ge(S["sw_mm"], part - 1)
                        act.activation(KTw[part % 2][:, c, 0:w], ps[:, 4 + n % 2, 0:w], ACT.Copy).then_inc(S["kt_ev"], 1)

                act.wait_ge(s_out, N_ROWS_OUT)
                keys_out(0)
                for part in range(4 * NB):
                    if part + 1 < 4 * NB:
                        keys_out(part + 1)
                    if part % 4 == 3:
                        b = part // 4
                        act.wait_ge(S["sw_nm"], b + 1)
                        act.activation(Sw[b % 2], Sw[b % 2], ACT.Exp, scale=SCB, bias=sml[0:NS, 2:3], accum_out=sml[0:NS, 4:5]).then_inc(S["sw_e"], 1)

            def latent_prep():
                act.wait_ge(S["q_rows"], 1)
                n = 0
                for i, _, rows in TOK_TILES:
                    for j in range(2):
                        act.activation(qrow[0:rows, i, j * 384:j * 384 + 384], ps[0:rows, n, 0:384], ACT.Copy).then_inc(S["qrow_ev"], 1)
                        n += 1
                for hd in range(H):
                    act.wait_ge(S["qcT"], hd + 1)
                    act.activation(qcT[0:96, hd, :], ps[0:96, hd % 4, 0:T], ACT.Copy).then_inc(S["qcT_ev"], 1)
                for n in range(16):
                    hd, c = n // 2, n % 2
                    act.wait_ge(S["ql"], n + 1)
                    act.activation(qlT[:, hd, c, :], ps[:, 4 + n % 4, 0:SEQ], ACT.Copy)
                    act.activation(QL[:, c, :, TS * hd:TS * hd + TS], ps[:, 4 + n % 4, SEQ:T].rearrange("p (b j) -> p b j", b=NB), ACT.Copy).then_inc(S["ql_ev"], 1)

            def ml_prompt():
                for n in range(16):
                    act.wait_ge(S["prompt_nm"], 2 * H + n + 1)
                    act.activation(Sp[n % 2][:, 0, :], Sp[n % 2][:, 0, :], ACT.Exp, scale=SCC, bias=sml[:, 2 + n % 2:3 + n % 2], accum_out=sml[:, 4 + n % 2:5 + n % 2]).then_inc(S["prompt_e"], 1)

            def ml_sample():

                def pages_out(part):
                    for n in range(4 * part, 4 * part + 4, 2):
                        act.wait_ge(S["lt_T"], n + 1)
                        if part >= 2:
                            act.wait_ge(S["ml_mm"], part - 1)
                        kt = KTl[(n // 4) % 2][:, :, (n % 4) * P:(n % 4) * P + P]
                        act.activation(kt[:, 0:2, :], ps[:, 5 + n % 2, 0:2 * P].rearrange("p (c k) -> p c k", c=2), ACT.Copy)
                        act.activation(kt[64:96, 2, :], ps[64:96, 5 + n % 2, 2 * P:3 * P], ACT.Copy).then_inc(S["lt_even"], 1)

                pages_out(0)
                for part in range(4 * NB):
                    if part + 1 < 4 * NB:
                        pages_out(part + 1)
                    if part % 4 < 3:
                        continue
                    b = part // 4
                    act.wait_ge(S["ml_nm"], b + 1)
                    if b:
                        act.wait_ge(S["ml_PT"], b)
                    act.activation(Pl[:, 0:PAST].rearrange("p (a k) -> p a k", a=4), ps[0:NS, 0:4, :], ACT.Exp, scale=SCC, bias=sml[0:NS, 2:3], accum_out=sml[0:NS, 4:5])
                    act.activation(Pl[:, PAST:], Pl[:, PAST:], ACT.Exp, scale=SCC, bias=sml[0:NS, 2:3], accum_out=sml[0:NS, 5:6]).then_inc(S["ml_exp"], 1)

            def mix():
                for m in range(24):
                    act.wait_ge(S["pgm"], m + 1)
                    act.activation(gates[:, m, :], ps[:, m % 8, 0:T], ACT.Sigmoid, bias=pp("b_gate", m)).then_inc(S["gate"], 1)
                down("mix")

            with act.Fori(0, DEPTH) as l:
                square_x("f1_pre")
                ffn("f1")
                act.wait_ge(S["x_f1"], 1)
                square_x("mix_pre")
                rwkv()
                bc_proj()
                sw_prompt()
                sw_sample()
                latent_prep()
                ml_prompt()
                ml_sample()
                mix()
                act.wait_ge(S["x_mix"], 1)
                square_x("f2_pre")
                ffn("f2")
                layer_end(act, l)

        @block.vector
        def _(dve):
            dve.wait_ge(s_once, 48)

            chain = [0]

            def link(ins):
                chain[0] += 1
                ins.then_inc(s_dve, 1)
                dve.wait_ge(s_dve, chain[0])

            def root(tag, half=None):
                dve.wait_ge(S["norm_sums"], NORMS[tag])
                dve.tensor_scalar(rstd, ps[:, 7, 0:T], 1.0 / D_MODEL, 1e-6, ALU.mult, ALU.add).then_inc(S["mean_squares"], 1)
                dve.wait_ge(S["mean_squares"], ROOTS[tag])
                dve.wait_ge(S["roots"], ROOTS[tag])
                link(dve.reciprocal(rstd, rstd))
                if half:
                    link(dve.tensor_scalar(rstd, rstd, half, None, ALU.mult))

            def pre(tag):
                root(tag)
                for k in range(KD):
                    q = dve.scalar_tensor_tensor(out=h[:, k, :], in0=x[:, k, :], scalar=pp(tag, k), in1=rstd, op0=ALU.mult, op1=ALU.mult)

                q.then_inc(S["normed"], 1)
                dve.wait_ge(S["normed"], PRES[tag])
            def post(tag, f, half=None):
                root(tag, half)
                for k in range(KD):
                    q = dve.scalar_tensor_tensor(out=yt[:, k, :], in0=yt[:, k, :], scalar=pp(tag, k), in1=rstd, op0=ALU.mult, op1=ALU.mult)
                link(q)
                dve.tensor_tensor(x, x, yt, ALU.add).then_inc(S["x_" + f], 1)
                dve.wait_ge(S["x_" + f], 1)

            def ffn(f):
                pre(f + "_pre")
                for m in range(KF):
                    dve.wait_ge(S["ffn_sg"], FFN0[f] + m + 1)
                    link(dve.tensor_tensor(act_t[:, m, :], ps[:, m % 3, 0:T], sg2[:, m % 2, :], ALU.mult))
                    dve.tensor_tensor(act_t[:, m, :], ps[:, 3 + m % 3, 0:T], act_t[:, m, :], ALU.mult).then_inc(S["ffn_a"], 1)
                dve.wait_ge(S["ffn_a"], FFN0[f] + KF)
                post(f + "_post", f, 0.5)

            def rwkv():
                pre("mix_pre")
                dve.memset(pa, 0.0).then_inc(S["pa_zeroed"], 1)
                dve.wait_ge(S["pa_zeroed"], 1)
                link(dve.memset(xs, 0.0))
                pas = pa[:, :, 1 + SEQ:].rearrange("p m (b j) -> p m b j", b=NB)
                dve.wait_ge(s_shin, 16)
                dve.wait_ge(S["pa"], NAT)
                link(dve.tensor_copy(pas[:, :, :, 0], shin))
                dve.tensor_copy(lastT[:, :, 0], pa[:, :, SEQ])
                dve.tensor_copy(lastT[:, :, 1:9], pas[:, :, :, TS]).then_inc(S["last_rows"], 1)
                dve.wait_ge(S["last_rows"], 1)
                dve.tensor_tensor(xs[:, :, 0:SEQ], pa[:, :, 0:SEQ], pa[:, :, 1:1 + SEQ], ALU.subtract)
                for m in range(NAT):
                    q = dve.tensor_tensor(xs[:, m, SEQ:T].rearrange("p (b j) -> p b j", b=NB), pas[:, m, :, 0:TS], pas[:, m, :, 1:], ALU.subtract)
                link(q)
                for m in range(NAT):
                    mu = pp("a_mu", m)
                    xm = xs[:, m, SEQ:T].rearrange("p (b j) -> p b j", b=NB)
                    dve.scalar_tensor_tensor(out=xs[:, m, 0:SEQ], in0=xs[:, m, 0:SEQ], scalar=mu, in1=pa[:, m, 1:1 + SEQ], op0=ALU.mult, op1=ALU.add)
                    q = dve.scalar_tensor_tensor(out=xm, in0=xm, scalar=mu, in1=pas[:, m, :, 1:], op0=ALU.mult, op1=ALU.add)
                q.then_inc(S["mixed"], 1)
                dve.wait_ge(S["mixed"], 1)
                r, k, v = xs[:, 0:4], xs[:, 4:8], xs[:, 8:12]
                link(dve.memset(Hp, 0.0))
                for m in range(4):
                    q = dve.tensor_scalar(S_[8][:, m, :], k[:, m, :], pp("a_kk", m), None, ALU.mult)
                q.then_inc(S["kk0"], 1)
                dve.wait_ge(S["kk0"], 1)
                link(dve.tensor_scalar(sml[:, 8:12], par[:, PAR["a_ka"][0]:PAR["a_ka"][0] + 4], -1.0, 1.0, ALU.mult, ALU.add))
                dve.wait_ge(S["a_ready"], 4)
                link(dve.tensor_scalar(S_[0], S_[0], -float(np.exp(-0.5)), None, ALU.mult))
                for m in range(4):
                    q = dve.tensor_tensor_scan(S_[3][:, m, :], C("reset"), S_[0][:, m, :], 0.0, ALU.mult, ALU.add)
                link(q)
                dve.tensor_tensor(S_[4], S_[3], S_[0], ALU.subtract).then_inc(S["L"], 1)
                dve.wait_ge(S["L"], 1)
                dve.wait_ge(S["kk_ss"], 1)
                dve.tensor_scalar(S_[9], ps[:, 4:8, 0:T], 1e-24, None, ALU.max).then_inc(S["mean_squares"], 1)
                dve.wait_ge(S["mean_squares"], ROOTS["kk"])
                dve.wait_ge(S["roots"], ROOTS["kk"])
                link(dve.reciprocal(S_[9], S_[9]))
                link(dve.tensor_tensor(S_[8], S_[8], S_[9], ALU.mult))
                dve.wait_ge(S["exps"], 1)
                for m in range(4):
                    q = dve.tensor_scalar(S_[4][:, m, :], S_[1][:, m, :], pp("a_ka", m), sml[:, 8 + m:9 + m], ALU.mult, ALU.add)
                link(q)
                link(dve.tensor_tensor(S_[4], S_[4], k, ALU.mult))
                link(dve.tensor_tensor(S_[9], r, S_[4], ALU.mult))
                for m in range(4):
                    q = dve.tensor_scalar(S_[9][:, m, :], S_[9][:, m, :], pp("a_rk", m), None, ALU.mult)
                q.then_inc(S["bonus_in"], 1)
                dve.wait_ge(S["bonus_in"], 1)
                link(dve.tensor_tensor(S_[1], S_[8], S_[1], ALU.mult))
                dve.tensor_tensor(S_[0], S_[1], S_[7], ALU.mult)
                link(dve.tensor_tensor(S_[6], S_[8], S_[6], ALU.mult))
                dve.tensor_tensor(S_[7], S_[4], S_[7], ALU.mult)
                link(dve.tensor_tensor(S_[3], r, S_[5], ALU.mult))
                dve.wait_ge(S["bonus_ss"], 1)
                dve.tensor_tensor(S_[9], ps[:, 0:4, 0:T], v, ALU.mult).then_inc(S["streams"], 1)
                dve.wait_ge(S["streams"], 1)
                for g in range(5):
                    rwkv_group(g)
                Y = S_[8]
                dve.wait_ge(S["y_mean"], 1)
                dve.scalar_tensor_tensor(out=Y, in0=ps[:, 0:4, 0:T], scalar=-1.0 / DH, in1=Y, op0=ALU.mult, op1=ALU.add).then_inc(S["y_centred"], 1)
                dve.wait_ge(S["y_centred"], 1)
                dve.wait_ge(S["y_var"], 1)
                dve.tensor_scalar(S_[1], ps[:, 4:8, 0:T], 1.0 / DH, 64e-5, ALU.mult, ALU.add).then_inc(S["mean_squares"], 1)
                dve.wait_ge(S["mean_squares"], ROOTS["y"])
                dve.wait_ge(S["roots"], ROOTS["y"])
                link(dve.reciprocal(S_[1], S_[1]))
                link(dve.tensor_tensor(Y, Y, S_[1], ALU.mult))
                for m in range(4):
                    q = dve.tensor_scalar(Y[:, m, :], Y[:, m, :], pp("a_ln_w", m), pp("a_ln_b", m), ALU.mult, ALU.add)
                link(q)
                link(dve.tensor_tensor(Y, Y, S_[9], ALU.add))
                dve.tensor_tensor(ya, Y, S_[2], ALU.mult).then_inc(S["rwkv_done"], 1)
                dve.wait_ge(S["rwkv_done"], 1)

            def rwkv_group(g):
                sample = g == 4
                t0 = g * CHUNK
                bank = lambda b: ps[0:64, b, :].rearrange("p (h s) -> p h s", h=H)
                msk = lambda n: C(n, 64).unsqueeze(1).to_broadcast([64, H, CHUNK])
                dve.wait_ge(S["rows"], g + 1)
                for i, o in enumerate((Vr, bdr, kdr)):
                    dve.tensor_copy(o, bank(i))
                dve.wait_ge(S["RK"], g + 1)
                dve.tensor_tensor(X8, bank(3), msk("m8p"), ALU.mult)
                dve.tensor_tensor(X8T, bank(4), msk("m8Tp"), ALU.mult)
                if not sample:
                    for o, n in ((Xo16, "o16T"), (Xo32, "o32T"), (Xo64, "o64T")):
                        dve.tensor_tensor(o, bank(4), msk(n), ALU.mult)
                dve.tensor_tensor(KK, bank(5), msk("sTs" if sample else "sTp"), ALU.mult)
                dve.tensor_tensor(RB, bank(6), msk("iTs" if sample else "iTp"), ALU.mult)
                dve.tensor_tensor(RK, bank(7), msk("iTs" if sample else "iTp"), ALU.mult).then_inc(S["masked"], 1)
                dve.wait_ge(S["masked"], g + 1)
                dve.wait_ge(S["X2T"], g + 1)
                dve.tensor_copy(X2, bank(0))
                dve.tensor_copy(X2T, bank(1)).then_inc(S["x2"], 1)
                dve.wait_ge(S["x2"], g + 1)
                dve.wait_ge(S["X4"], g + 1)
                dve.tensor_copy(X4, bank(2)).then_inc(S["x4"], 1)
                dve.wait_ge(S["x4"], g + 1)
                link(dve.tensor_tensor(Pm, X2, X4, ALU.add))
                link(dve.tensor_tensor(Pm, Pm, msk_id(), ALU.add))
                dve.wait_ge(S["X6"], g + 1)
                dve.tensor_tensor(Pm, bank(3), Pm, ALU.add).then_inc(S["pm"], 1)
                dve.wait_ge(S["pm"], g + 1)
                dve.wait_ge(S["XP"], g + 1)
                dve.tensor_tensor(Tt, bank(4), Pm, ALU.add).then_inc(S["t"], 1)
                dve.wait_ge(S["t"], g + 1)
                dve.wait_ge(S["TT"], g + 1)
                dve.tensor_copy(TT, bank(5)).then_inc(S["tt"], 1)
                dve.wait_ge(S["tt"], g + 1)
                if not sample:
                    for i in range(3):
                        dve.wait_ge(S["G"], 3 * g + i + 1)
                        dve.tensor_copy(G, bank(0)).then_inc(S["g_level" ], 1)
                        dve.wait_ge(S["g_level" ], 3 * g + i + 1)
                        dve.wait_ge(S["dTT"], 3 * g + i + 1)
                        dve.tensor_tensor(Tt, bank(1), Tt, ALU.add)
                        dve.tensor_tensor(TT, bank(2), TT, ALU.add).then_inc(S["t_level" ], 1)
                        dve.wait_ge(S["t_level" ], 3 * g + i + 1)
                    dve.wait_ge(S["rhs"], g + 1)
                    dve.tensor_copy(RHS, bank(3)).then_inc(S["rhs_ev"], 1)
                    dve.wait_ge(S["rhs_ev"], g + 1)
                else:
                    bm = C("bmask", 64).unsqueeze(2).to_broadcast([64, NB, DH])
                    for hd in range(H):
                        dve.wait_ge(S["zh_mm"], hd + 1)
                        dve.tensor_tensor(Tm, ps[0:64, hd % 2, :].rearrange("p (b v) -> p b v", b=NB), bm, ALU.mult).then_inc(S["zh"], 1)
                        dve.wait_ge(S["zh"], hd + 1)
                        link(dve.tensor_reduce(RHS[:, hd], Tm.rearrange("p b v -> p v b"), AX, ALU.add))
                    dve.wait_ge(S["rhs"], g + 1)
                    dve.tensor_tensor(RHS, bank(3), RHS, ALU.add).then_inc(S["rhs_ev"], 1)
                    dve.wait_ge(S["rhs_ev"], g + 1)
                dve.wait_ge(S["u"], g + 1)
                dve.tensor_scalar(U, bank(4), -1.0, None, ALU.mult).then_inc(S["u_ev"], 1)
                dve.wait_ge(S["u_ev"], g + 1)
                dve.wait_ge(S["y"], g + 1)
                dve.tensor_copy(S_[8][:, :, t0:t0 + CHUNK], ps[:, 5, 0:256].rearrange("p (m t) -> p m t", m=4))
                EL = S_[5]
                if not sample:
                    dve.wait_ge(S["h"], g + 1)
                    link(dve.tensor_tensor(Hp, bank(6), Hp, ALU.add))
                    pairs = Hp.rearrange("p (m r) v -> p r m v", r=2)
                    dve.wait_ge(S["odd"], 5 * g + 5)
                    for r, el in ((0, EL[0:64, :, t0 + CHUNK - 1:t0 + CHUNK]), (1, Odd[4][:, :, CHUNK - 1:CHUNK])):
                        q = dve.tensor_tensor(pairs[:, r], pairs[:, r], el.to_broadcast([64, 4, DH]), ALU.mult)
                    q.then_inc(S["group"], 1)
                    dve.wait_ge(S["group"], g + 1)
                else:
                    for hd in range(H):
                        if hd:
                            dve.wait_ge(S["hs"], hd)
                        dve.tensor_tensor(Ue, U[:, hd].unsqueeze(1).to_broadcast([64, NB, DH]), bm, ALU.mult)
                        dve.tensor_tensor(Ve, Vr[:, hd].unsqueeze(1).to_broadcast([64, NB, DH]), bm, ALU.mult).then_inc(S["ue"], 1)
                        dve.wait_ge(S["ue"], hd + 1)
                        dve.wait_ge(S["hs"], hd + 1)
                        Hh = Hs(hd)
                        link(dve.tensor_tensor(Hh, ps[0:64, 6 + hd % 2, :], Hh, ALU.add))
                        Hh = Hh.rearrange("p (b v) -> p b v", b=NB)
                        el = Odd[4][:, hd // 2, :] if hd % 2 else EL[0:64, hd // 2, SEQ:T]
                        el = el.rearrange("p (b j) -> p b j", b=NB)[:, :, TS - 1:TS]
                        q = dve.tensor_tensor(Hh, Hh, el.to_broadcast([64, NB, DH]), ALU.mult)
                    q.then_inc(S["group"], 1)
                    dve.wait_ge(S["group"], g + 1)

            def msk_id():
                return cst[0:64, CONST["ident"][0]:CONST["ident"][0] + 64].unsqueeze(1).to_broadcast([64, H, CHUNK])

            def rope(v, heads, half, cos, sin, tmp):
                rows = v.shape[0]
                a, b = v[:, :, 0:half], v[:, :, half:2 * half]
                cos, sin = [c.unsqueeze(1).to_broadcast([rows, heads, half]) for c in (cos, sin)]
                n = heads * half
                t = [tmp[0:rows, i * n:i * n + n].rearrange("p (h d) -> p h d", h=heads) for i in range(4)]
                dve.tensor_tensor(t[0], a, cos, ALU.mult)
                dve.tensor_tensor(t[1], b, sin, ALU.mult)
                dve.tensor_tensor(t[2], b, cos, ALU.mult)
                link(dve.tensor_tensor(t[3], a, sin, ALU.mult))
                dve.tensor_tensor(a, t[0], t[1], ALU.subtract)
                return dve.tensor_tensor(b, t[2], t[3], ALU.add)

            def bc_rows():
                link(dve.memset(sml[:, 8:14], 1.0))
                parts = ((0, Q_LORA), (Q_LORA, KV_LORA))
                for i, _, rows in TOK_TILES:
                    dve.wait_ge(S["pbc_ev"], 3 + i + 1)
                    for j, (c0, w) in enumerate(parts):
                        part, ms = PBc[0:rows, i, c0:c0 + w], sml[0:rows, 8 + 2 * i + j:9 + 2 * i + j]
                        link(dve.tensor_tensor_reduce(rt[0:rows, 0:w], part, part, 1.0, 0.0, ALU.mult, ALU.add, ms))
                        dve.tensor_scalar(ms, ms, 1.0 / w, 1e-6, ALU.mult, ALU.add).then_inc(S["latent_ms"], 1)
                        dve.wait_ge(S["latent_ms"], 2 * i + j + 1)
                dve.wait_ge(S["latent_root"], 1)
                link(dve.reciprocal(sml[:, 8:14], sml[:, 8:14]))
                for i, _, rows in TOK_TILES:
                    q_part, kv_part = [PBc[0:rows, i, c0:c0 + w] for c0, w in parts]
                    link(dve.tensor_scalar(q_part, q_part, sml[0:rows, 8 + 2 * i:9 + 2 * i], None, ALU.mult))
                    link(dve.scalar_tensor_tensor(out=kv_part, in0=kv_part, scalar=sml[0:rows, 9 + 2 * i:10 + 2 * i], in1=kvn[0:rows, :], op0=ALU.mult, op1=ALU.mult))
                    link(rope(PBc[0:rows, i:i + 1, Q_LORA + KV_LORA:], 1, DROPE // 2, C("cosc")[0:rows, 16 * i:16 * i + 16],
                              C("sinc")[0:rows, 16 * i:16 * i + 16], rt))
                dve.wait_ge(S["pbc_ev"], 21)
                for i, _, rows in TOK_TILES:
                    rope(PBq[0:rows, i, :].rearrange("p (h d) -> p h d", h=32), 32, ROT, C("cosb")[0:rows, 8 * i:8 * i + 8],
                         C("sinb")[0:rows, 8 * i:8 * i + 8], rt).then_inc(S["rows_ready"], 1)
                    dve.wait_ge(S["rows_ready"], i + 1)

            def softmax_in(tag, n, src, mask, scores):
                i, base = n % 2, PROMPT0[tag]
                dve.tensor_tensor(scores, src, mask, ALU.add).then_inc(S["prompt_s"], 1)
                dve.wait_ge(S["prompt_s"], base + n + 1)
                link(dve.tensor_reduce(sml[:, i:i + 1], scores, mybir.AxisListType.XY if len(scores.shape) == 3 else AX, ALU.max))
                dve.tensor_scalar(sml[:, 2 + i:3 + i], sml[:, i:i + 1], -(SCB if tag == "swp" else SCC), None, ALU.mult).then_inc(S["prompt_nm"], 1)
                dve.wait_ge(S["prompt_nm"], base + n + 1)

            def prompt_attention(tag, y, one_group):
                base = PROMPT0[tag]
                src = lambda n: (ps[:, n % 2, 0:SEQ] if one_group else
                                 ps[:, 2 * (n % 2):2 * (n % 2) + 2, :].rearrange("p b k -> p (b k)")[:, 0:768].rearrange("p (g k) -> p g k", g=3))

                def finish(n):
                    r0, m, t = 64 * (n % 2), (n % H) // 2, n // H
                    dve.wait_ge(S["prompt_o"], base + n + 1)
                    dve.tensor_copy(y[r0:r0 + 64, m, t * P:t * P + P], ps[r0:r0 + 64, 6 + n % 2, 0:P]).then_inc(S["prompt_y"], 1)
                    dve.wait_ge(S["prompt_y"], base + n + 1)

                for i in range(17):
                    if i < 16:
                        t = i // H
                        dve.wait_ge(S["prompt_mm"], base + i + 1)
                        scores = Sp[i % 2][:, 0, :] if one_group else Sp[i % 2]
                        mask = (C("mlp")[:, t * SEQ:t * SEQ + SEQ] if one_group else
                                C("swp")[:, t * 768:t * 768 + 768].rearrange("p (g k) -> p g k", g=3))
                        softmax_in(tag, i, src(i), mask, scores)
                    if i >= 2:
                        finish(i - 2)
                    if i >= 1:
                        n = i - 1
                        dve.wait_ge(S["prompt_e"], base + n + 1)
                        probs, rs = Sp[n % 2], sml[:, 4 + n % 2:5 + n % 2]
                        link(dve.reciprocal(rs, rs))
                        if one_group:
                            dve.tensor_scalar(Pc[n % 2], probs[:, 0, :], rs, None, ALU.mult).then_inc(S["prompt_p"], 1)
                            dve.wait_ge(S["prompt_p"], base + n + 1)
                        else:
                            link(dve.tensor_tensor(Pc[n % 2], probs[:, 0, :], probs[:, 1, :], ALU.add))
                            link(dve.tensor_tensor(Pc[n % 2], Pc[n % 2], probs[:, 2, :], ALU.add))
                            dve.tensor_scalar(Pc[n % 2], Pc[n % 2], rs, None, ALU.mult).then_inc(S["prompt_p"], 1)
                            dve.wait_ge(S["prompt_p"], base + n + 1)
                        dve.wait_ge(S["prompt_T"], base + n + 1)
                        dve.tensor_copy(PTp[n % 2], ps[:, (2 if one_group else 4) + n % 2, 0:256].rearrange("p (c k) -> p c k", c=2)).then_inc(S["prompt_pt"], 1)
                        dve.wait_ge(S["prompt_pt"], base + n + 1)
                        if one_group:
                            dve.wait_ge(S["prompt_ol"], n + 1)
                            dve.tensor_copy(OLp[n % 2], ps[:, 4 + n % 2, 0:256].rearrange("p (c k) -> p c k", c=2)).then_inc(S["prompt_olev"], 1)
                            dve.wait_ge(S["prompt_olev"], n + 1)
                finish(15)

            def sw_sample():
                dve.memset(Qbd, 0.0)
                link(dve.memset(PnF, 0.0))
                q4 = qT.rearrange("p (g c) t -> p g c t", g=3)
                tokens = lambda b: slice(SEQ + TS * b, SEQ + TS * b + TS)

                def queries(b):
                    for c in range(4):
                        for r in range(2):
                            o = Qbd[64 * r:64 * r + 64, c, :, 16 * c + 8 * r:16 * c + 8 * r + 8]
                            dve.tensor_copy(o, q4[64 * r:64 * r + 64, :, c, tokens(b)]).then_inc(S["qbd"], 1)

                def softmax(b):
                    Sb = Sw[b % 2]
                    dve.wait_ge(S["sw_e"], b + 1)
                    link(dve.reciprocal(sml[0:NS, 6 + b % 2:7 + b % 2], sml[0:NS, 4:5]))
                    n0 = SW_TILES * P
                    if b:
                        dve.memset(PnF[:, TS * (b - 1):TS * b], 0.0)
                    o = PnF[:, TS * b:TS * b + TS]
                    link(dve.tensor_tensor(o, Sb[:, n0:n0 + TS], Sb[:, n0 + TS:n0 + 2 * TS], ALU.add))
                    dve.tensor_tensor(o, o, Sb[:, n0 + 2 * TS:n0 + 3 * TS], ALU.add).then_inc(S["sw_p"], 1)
                    dve.wait_ge(S["sw_p"], b + 1)

                def probs_out(b):
                    dve.wait_ge(S["sw_PT"], b + 1)
                    dve.tensor_copy(PTw[:, 0:8, :], ps[:, 6, :].rearrange("p (t n) -> p t n", t=8))
                    dve.tensor_copy(PTw[:, 8:13, :], ps[:, 7, 0:320].rearrange("p (t n) -> p t n", t=5))
                    dve.tensor_copy(PTn, ps[0:NS, 7, 320:384]).then_inc(S["sw_pt"], 1)
                    dve.wait_ge(S["sw_pt"], b + 1)

                def own_values(b):
                    dve.wait_ge(S["sw_pv"], b + 1)
                    dve.scalar_tensor_tensor(out=Ow, in0=ps[0:NS, 7, :].rearrange("p (h v) -> p h v", h=H),
                                             scalar=sml[0:NS, 6 + b % 2:7 + b % 2],
                                             in1=C("bmask", NS).unsqueeze(2).to_broadcast([NS, H, DH]),
                                             op0=ALU.mult, op1=ALU.mult).then_inc(S["sw_own"], 1)
                    dve.wait_ge(S["sw_own"], b + 1)

                def result(b):
                    dve.wait_ge(S["sw_y"], b + 1)
                    dve.tensor_copy(yb[:, :, tokens(b)], ps[:, 6, 0:4 * TS].rearrange("p (c j) -> p c j", c=4)).then_inc(S["sws_done"], 1)
                    dve.wait_ge(S["sws_done"], b + 1)

                queries(0)
                dve.wait_ge(s_out, N_ROWS_OUT)
                for b in range(NB):
                    if b:
                        probs_out(b - 1)
                    Sb = Sw[b % 2]
                    dve.wait_ge(S["sw_s"], b + 1)
                    dve.tensor_tensor(Sb, ps[0:NS, 0:4, :].rearrange("p b k -> p (b k)")[:, 0:SW_COLS], C("sws", NS), ALU.add).then_inc(S["sw_masked"], 1)
                    dve.wait_ge(S["sw_masked"], b + 1)
                    if b + 1 < NB:
                        queries(b + 1)
                    link(dve.tensor_reduce(sml[0:NS, 0:1], Sb, AX, ALU.max))
                    dve.tensor_scalar(sml[0:NS, 2:3], sml[0:NS, 0:1], -SCB, None, ALU.mult).then_inc(S["sw_nm"], 1)
                    dve.wait_ge(S["sw_nm"], b + 1)
                    if b:
                        own_values(b - 1)
                    softmax(b)
                    if b:
                        result(b - 1)
                probs_out(NB - 1)
                own_values(NB - 1)
                result(NB - 1)

            def latent_prep():
                dve.wait_ge(s_out, N_ROWS_OUT)
                dve.wait_ge(S["cqT"], 1)
                for k in range(3):
                    dve.tensor_scalar(cqT[:, k, :], ps[:, k, 0:T], pp("c_q_norm", k), None, ALU.mult)
                dve.wait_ge(S["kvT"], 1)
                dve.tensor_copy(kvT[0:64].rearrange("p (a b) k -> p a (b k)", b=2), ps[0:64, 3:7, :]).then_inc(S["kvT_ev"], 1)
                dve.wait_ge(S["kvT_ev"], 1)
                dve.wait_ge(S["qrow_ev"], 6)
                for i, _, rows in TOK_TILES:
                    v = qrow[0:rows, i, :].rearrange("p (h d) -> p h d", h=H)[:, :, DNOPE:]
                    rope(v, H, DROPE // 2, C("cosc")[0:rows, 16 * i:16 * i + 16], C("sinc")[0:rows, 16 * i:16 * i + 16], rt2).then_inc(S["q_rope"], 1)
                    dve.wait_ge(S["q_rope"], i + 1)
                dve.wait_ge(S["qcT_ev"], H)
                dve.tensor_copy(QR[64:96], qcT[64:96, :, SEQ:T].rearrange("p h (b j) -> p b h j", b=NB))
                dve.wait_ge(S["ql_ev"], 16)
                dve.memset(PnL, 0.0).then_inc(S["ml_prep"], 1)
                dve.wait_ge(S["ml_prep"], 1)

            def ml_sample():

                def pages_out(part):
                    for n in range(4 * part + 1, 4 * part + 4, 2):
                        dve.wait_ge(S["lt_T"], n + 1)
                        if part >= 2:
                            dve.wait_ge(S["ml_mm"], part - 1)
                        kt = KTl[(n // 4) % 2][:, :, (n % 4) * P:(n % 4) * P + P]
                        dve.tensor_copy(kt[:, 0:2, :], ps[:, 5 + n % 2, 0:2 * P].rearrange("p (c k) -> p c k", c=2))
                        dve.tensor_copy(kt[64:96, 2, :], ps[64:96, 5 + n % 2, 2 * P:3 * P]).then_inc(S["lt_odd"], 1)

                def new_scores(b):
                    dve.wait_ge(S["ml_s"], b + 1)
                    link(dve.tensor_tensor(Pl[:, PAST:], ps[0:NS, 4, 0:TS], C("mls", NS), ALU.add))

                def maximum(b):
                    dve.tensor_reduce(sml[0:NS, 0:1], ps[0:NS, 0:4, :], mybir.AxisListType.XY, ALU.max)
                    link(dve.tensor_reduce(sml[0:NS, 1:2], Pl[:, PAST:], AX, ALU.max))
                    link(dve.tensor_tensor(sml[0:NS, 0:1], sml[0:NS, 0:1], sml[0:NS, 1:2], ALU.max))
                    dve.tensor_scalar(sml[0:NS, 2:3], sml[0:NS, 0:1], -SCC, None, ALU.mult).then_inc(S["ml_nm"], 1)
                    dve.wait_ge(S["ml_nm"], b + 1)

                def softmax(b):
                    dve.wait_ge(S["ml_exp"], b + 1)
                    link(dve.tensor_tensor(sml[0:NS, 3:4], sml[0:NS, 4:5], sml[0:NS, 5:6], ALU.add))
                    dve.reciprocal(sml[0:NS, 6 + b % 2:7 + b % 2], sml[0:NS, 3:4])
                    if b:
                        dve.memset(PnL[:, TS * (b - 1):TS * b], 0.0)
                    dve.tensor_copy(PnL[:, TS * b:TS * b + TS], Pl[:, PAST:]).then_inc(S["ml_p"], 1)
                    dve.wait_ge(S["ml_p"], b + 1)

                def probs_out(b):
                    dve.wait_ge(S["ml_PT"], b + 1)
                    for half in range(2):
                        dve.tensor_copy(PTL[:, 8 * half:8 * half + 8, :], ps[:, 5 + 2 * half, :].rearrange("p (t n) -> p t n", t=8))
                    dve.tensor_copy(PTl, ps[0:NS, 6, 0:NS]).then_inc(S["ml_pt"], 1)
                    dve.wait_ge(S["ml_pt"], b + 1)

                def divided(b):
                    dve.wait_ge(S["ml_pv"], b + 1)
                    dve.tensor_scalar(Osb, ps[0:NS, 4, 256:512], sml[0:NS, 6 + b % 2:7 + b % 2], None, ALU.mult).then_inc(S["ml_osb"], 1)
                    dve.wait_ge(S["ml_osb"], b + 1)

                def result(b):
                    dve.wait_ge(S["ml_oT"], b + 1)
                    dve.tensor_copy(olT[:, :, :, TS * b:TS * b + TS], ps[:, 7, 0:2 * NS].rearrange("p (c h j) -> p c h j", c=2, h=H)).then_inc(S["ml_olT"], 1)
                    dve.wait_ge(S["ml_olT"], b + 1)

                pages_out(0)
                for part in range(4 * NB):
                    if part + 1 < 4 * NB:
                        pages_out(part + 1)
                    if part % 4 == 0 and part >= 8:
                        result(part // 4 - 2)
                    if part % 4 == 3:
                        b = part // 4
                        new_scores(b)
                        if b:
                            probs_out(b - 1)
                        maximum(b)
                        softmax(b)
                        if b:
                            divided(b - 1)
                result(NB - 2)
                probs_out(NB - 1)
                divided(NB - 1)
                result(NB - 1)
                dve.wait_ge(S["ml_yc"], 1)
                dve.tensor_copy(yc[:, :, SEQ:T], ps[:, 0, 0:4 * NS].rearrange("p (m t) -> p m t", m=4)).then_inc(S["ml_done"], 1)
                dve.wait_ge(S["ml_done"], 1)

            def mix():
                for n in range(24):
                    m = n % KD
                    dve.wait_ge(S["brm"], n + 1)
                    if n < KD:
                        dve.tensor_tensor(mt[:, m, :], ps[:, m, 0:T], gates[:, n, :], ALU.mult).then_inc(S["br_ev"], 1)
                        dve.wait_ge(S["br_ev"], n + 1)
                    else:
                        link(dve.tensor_tensor(gates[:, n, :], ps[:, m, 0:T], gates[:, n, :], ALU.mult))
                        dve.tensor_tensor(mt[:, m, :], gates[:, n, :], mt[:, m, :], ALU.add).then_inc(S["br_ev"], 1)
                        dve.wait_ge(S["br_ev"], n + 1)
                post("mix_post", "mix")

            with dve.Fori(0, DEPTH) as l:
                dve.wait_ge(s_par, 16 * 5)
                ffn("f1")
                rwkv()
                bc_rows()
                prompt_attention("swp", yb, False)
                sw_sample()
                latent_prep()
                prompt_attention("mlp", yc, True)
                ml_sample()
                mix()
                ffn("f2")
                layer_end(dve, l)


_IN = ["consts", "params", "xT", "shiftT", "wkvT", "page_table", "cache_mla_ckv", "cache_mla_krope", "cache_swa_k",
       "cache_swa_v", "c_kv_norm", "a_w2", "a_a2", "a_g2", "w_in", "w_branch_a", "w_branch_b", "w_branch_c", "w_out",
       "c_q_up", "c_kv_up", "f1_wg", "f1_wu", "f1_wd", "f2_wg", "f2_wu", "f2_wd"]
_OUT = {"yT": (P, KD, T), "o_ckv_p": (DEPTH, 1, SEQ, KV_LORA), "o_ckv_s": (DEPTH, NB, TS, KV_LORA),
        "o_krope_p": (DEPTH, 1, SEQ, DROPE), "o_krope_s": (DEPTH, NB, TS, DROPE),
        "o_swa_k_p": (DEPTH, 1, SEQ, W_A), "o_swa_k_s": (DEPTH, NB, PAST, W_A),
        "o_swa_v_p": (DEPTH, 1, SEQ, W_A), "o_swa_v_s": (DEPTH, NB, PAST, W_A),
        "o_wkv_p": (DEPTH, DH, H, DH), "o_wkv_s": (DEPTH, 2, DH, 4, NB * DH), "o_shift": (DEPTH, P, NAT, 9)}


def kernel(**inputs):
    import concourse.bacc as bacc
    from concourse.bass_utils import run_bass_kernel_spmd

    a = {k: np.ascontiguousarray(v) for k, v in inputs.items()}

    def by_channel(v, tiles):
        out = np.zeros((v.shape[0], P, len(tiles)) + v.shape[2:], v.dtype)
        for m, (c0, rows) in enumerate(tiles):
            out[:, :rows, m] = v[:, c0:c0 + rows]
        return out

    full = lambda n: [(i * P, P) for i in range(n)]
    names = {"f1_pre": "n_f1_pre", "f1_post": "n_f1_post", "mix_pre": "n_mix_pre", "mix_post": "n_mix_post",
             "f2_pre": "n_f2_pre", "f2_post": "n_f2_post"}
    params = [by_channel(a[names.get(n, n)].reshape(DEPTH, -1), A_TILES if n == "a_mu" else full(w))
              for n, (_, w) in PAR.items()]
    tokens = np.concatenate([a["x_prompt"].reshape(SEQ, D_MODEL), a["x_sample"].reshape(NS, D_MODEL)])
    states = a["state_rwkv_wkv"].reshape(DEPTH, NB, 4, 2, DH, DH).transpose(0, 3, 5, 2, 1, 4).reshape(DEPTH, 2, DH, 4, NB * DH)
    arrays = {
        "consts": constants(), "params": np.concatenate(params, axis=2),
        "xT": np.ascontiguousarray(tokens.T.reshape(KD, P, T).transpose(1, 0, 2)),
        "shiftT": by_channel(a["state_rwkv_shift"].transpose(0, 2, 1), A_TILES),
        "wkvT": np.ascontiguousarray(states),
        "cache_swa_k": a["cache_swa_k"].reshape(DEPTH, NB, PAST, W_A),
        "cache_swa_v": a["cache_swa_v"].reshape(DEPTH, NB, PAST, W_A),
    }
    for n in _IN:
        if n not in arrays:
            arrays[n] = a[n]

    nc = bacc.Bacc("TRN2", target_bir_lowering=False, num_devices=1)
    io = {n: nc.dram_tensor(f"in_{n}_dram", arrays[n].shape, mybir.dt.from_np(arrays[n].dtype), kind="ExternalInput").ap()
          for n in _IN}
    for n, shape in _OUT.items():
        io[n] = nc.dram_tensor(f"out_{n}_dram", shape, F32, kind="ExternalOutput").ap()
    build(nc, io)
    r = run_bass_kernel_spmd(nc, [{f"in_{n}_dram": arrays[n] for n in _IN}], core_ids=[0]).results[0]
    o = {n: r[f"out_{n}_dram"] for n in _OUT}

    tokens = o["yT"].transpose(1, 0, 2).reshape(D_MODEL, T).T
    rows = np.concatenate([o["o_shift"][:, :n, m] for m, (_, n) in enumerate(A_TILES)], axis=1)
    wkv_p = o["o_wkv_p"].transpose(0, 2, 3, 1)[:, None]
    wkv_s = o["o_wkv_s"].reshape(DEPTH, 2, DH, 4, NB, DH).transpose(0, 4, 3, 1, 5, 2).reshape(DEPTH, NB, H, DH, DH)
    heads = lambda v: v.reshape(v.shape[:3] + (H, DH))
    c = np.ascontiguousarray
    return (c(tokens[:SEQ].reshape(1, SEQ, D_MODEL)), c(tokens[SEQ:].reshape(NB, TS, D_MODEL)),
            o["o_ckv_p"], o["o_ckv_s"], o["o_krope_p"], o["o_krope_s"],
            heads(o["o_swa_k_p"]), heads(o["o_swa_k_s"]), heads(o["o_swa_v_p"]), heads(o["o_swa_v_s"]),
            c(wkv_p), c(wkv_s), c(rows[:, None, :, 0]), c(rows[:, :, 1:].transpose(0, 2, 1)))
```

```python
from contextlib import ExitStack

import numpy as np
import concourse.bass as bass
from concourse import mybir

F32 = mybir.dt.float32
I32 = mybir.dt.int32
ALU = mybir.AluOpType
ACT = mybir.ActivationFunctionType
AX = mybir.AxisListType.X

P = 128
D_MODEL, DEPTH, D_FF = 1024, 2, 2816
SEQ, NB, TS, PAST, PAGE, N_POOL = 256, 8, 8, 2048, 128, 160
NS = NB * TS
T = SEQ + NS
KD, KF = D_MODEL // P, D_FF // P
H, DH = 8, 64
W_A = H * DH
A_COLS, B_COLS, C_COLS = 3 * W_A + 160, 5 * W_A, 672
Q_LORA, KV_LORA, DROPE, DNOPE = 384, 256, 32, 64
CB, CC, CG = A_COLS, A_COLS + B_COLS, A_COLS + B_COLS + C_COLS
ROT, N_PAGES = 8, PAST // PAGE
A_TILES = [(m * P, P) for m in range(12)] + [(3 * W_A, 64), (3 * W_A + 64, 96)]
NAT = len(A_TILES)
PADT = 1 + SEQ + NB * (TS + 1)
TOK_TILES = [(0, 0, P), (1, P, P), (2, SEQ, NS)]
GROUPS_B = ((128, 1), (512, 4), (2048, 16))
CHUNK = 64
SW_TILES = 8 + 4 + 1
SW_COLS = SW_TILES * P + 3 * TS
NEG = -1.0e30

PAR = {}
_at = 0
for _n, _w in [("f1_pre", 8), ("f1_post", 8), ("mix_pre", 8), ("mix_post", 8), ("f2_pre", 8), ("f2_post", 8),
               ("b_gate", 24), ("a_mu", NAT), ("a_w0", 4), ("a_a0", 4), ("a_kk", 4), ("a_ka", 4), ("a_rk", 4),
               ("a_ln_w", 4), ("a_ln_b", 4), ("c_q_norm", 3)]:
    PAR[_n] = (_at, _w)
    _at += _w
NPAR = _at

CONST = {}
_at = 0
for _n, _w in [("ident", P), ("ones", P), ("onesblk", P), ("reset", T), ("cosb", 24), ("sinb", 24), ("cosc", 48),
               ("sinc", 48), ("bmask", 8), ("tsel", 8), ("m8p", 64), ("m8Tp", 64), ("o16T", 64), ("o32T", 64), ("o64T", 64),
               ("sTp", 64), ("iTp", 64), ("sTs", 64), ("iTs", 64), ("swp", 2 * 3 * SEQ),
               ("mlp", 2 * SEQ), ("sws", SW_COLS), ("mls", TS)]:
    CONST[_n] = (_at, _w)
    _at += _w
NCONST = _at


def constants():
    c = np.zeros((P, NCONST), np.float32)

    def put(name, a):
        at, w = CONST[name]
        c[:a.shape[0], at:at + w] = a.reshape(a.shape[0], w)

    put("ident", np.eye(P))
    put("ones", np.ones((P, P)))
    blk = np.arange(P) // DH
    put("onesblk", (blk[:, None] == blk[None, :]) * 1.0)
    reset = np.ones(T)
    reset[0:SEQ:CHUNK] = 0
    reset[SEQ::TS] = 0
    put("reset", np.broadcast_to(reset, (P, T)))
    pos = np.zeros((P, 3), np.float32)
    pos[:, 0], pos[:, 1] = np.arange(P), P + np.arange(P)
    pos[:, 2] = PAST + np.arange(P) % TS
    for tag, half in (("b", ROT), ("c", DROPE // 2)):
        inv = np.float32(500000.0) ** (-(np.arange(half, dtype=np.float32) * np.float32(2.0) / np.float32(2 * half)))
        ang = pos[:, :, None] * inv.astype(np.float32)[None, None, :]
        put("cos" + tag, np.cos(ang))
        put("sin" + tag, np.sin(ang))
    t = np.arange(CHUNK)
    put("bmask", (t[:, None] // TS == np.arange(NB)[None, :]) * 1.0)
    put("tsel", (t[:, None] % TS == np.arange(TS)[None, :]) * 1.0)
    low = t[None, :] < t[:, None]
    same = lambda n: t[:, None] // n == t[None, :] // n
    put("m8p", (low & same(8)) * -1.0)
    put("m8Tp", (low & same(8)).T * -1.0)
    for n in (16, 32, 64):
        put(f"o{n}T", (low & same(n) & ~same(n // 2)).T * -1.0)
    put("sTp", low.T * 1.0)
    put("iTp", (low | same(1)).T * 1.0)
    put("sTs", (low & same(8)).T * 1.0)
    put("iTs", ((low & same(8)) | same(1)).T * 1.0)
    q = np.arange(SEQ)[:, None]
    k = np.arange(SEQ)[None, :]
    swp = np.stack([np.where((q >= k) & ((q - k) % d == 0) & (q - k <= w), 0.0, NEG) for w, d in GROUPS_B], 1)
    put("swp", swp.reshape(2, P, 3, SEQ).transpose(1, 0, 2, 3))
    put("mlp", np.where(q >= k, 0.0, NEG).reshape(2, P, SEQ).transpose(1, 0, 2))
    j = np.arange(NS) % TS
    m = np.full((NS, SW_COLS), NEG)
    a = np.arange(P)
    for r in range(8):
        m[:, r * P:(r + 1) * P] = np.where(j[:, None] == r, 0.0, NEG)
    for r in range(4):
        ok = (j[:, None] % 4 == r) & ((j[:, None] < 4) | (a[None, :] >= 1))
        m[:, (8 + r) * P:(9 + r) * P] = np.where(ok, 0.0, NEG)
    m[:, 12 * P:13 * P] = np.where(a[None, :] >= j[:, None], 0.0, NEG)
    n = np.arange(TS)[None, :]
    for g, (w, d) in enumerate(GROUPS_B):
        ok = (j[:, None] >= n) & ((j[:, None] - n) % d == 0)
        m[:, SW_TILES * P + g * TS:SW_TILES * P + (g + 1) * TS] = np.where(ok, 0.0, NEG)
    put("sws", m)
    put("mls", np.where(j[:, None] >= n, 0.0, NEG))
    return c


ROOTS = {t: i + 1 for i, t in enumerate(("f1_pre", "f1_post", "mix_pre", "kk", "y", "mix_post", "f2_pre", "f2_post"))}
NORMS = {t: i + 1 for i, t in enumerate(("f1_pre", "f1_post", "mix_pre", "mix_post", "f2_pre", "f2_post"))}
PRES = {t: i + 1 for i, t in enumerate(("f1_pre", "mix_pre", "f2_pre"))}
FFN0, DOWN0, PROMPT0 = {"f1": 0, "f2": KF}, {"f1": 0, "mix": KD, "f2": 2 * KD}, {"swp": 0, "mlp": 2 * H}
NSLOT = 3
N_ROWS_OUT = 16 * (4 + 2 * NB + 2)
SLOT = 4096
SWK, SWV = SW_TILES * W_A, SW_TILES * W_A


def weight_units(io):
    out = []

    def cols(w, k, c0, c1):
        return lambda l: w[bass.ds(l, 1), :, c0:c1].rearrange("a (k p) n -> p (a k) n", p=P), k, c1 - c0

    def ffn(f):
        for u in range(KF // 2):
            out.append(((f, "gu", u), [cols(io[f + "_wg"], KD, u * 256, u * 256 + 256),
                                       cols(io[f + "_wu"], KD, u * 256, u * 256 + 256)]))
        for u in range(KD):
            out.append(((f, "d", u), [cols(io[f + "_wd"], KF, u * P, (u + 1) * P)]))

    ffn("f1")
    for u, (c0, c1) in enumerate([(0, 512), (512, 1024), (1024, 1536), (1536, 1696)]):
        out.append((("pa", u), [cols(io["w_in"], KD, c0, c1)]))
    for u, (c0, c1) in enumerate([(CC, CC + 512), (CC + 512, CG)] + [(CB + 512 * i, CB + 512 * i + 512) for i in range(5)]):
        out.append((("pbc", u), [cols(io["w_in"], KD, c0, c1)]))
    for u in range(6):
        out.append((("pg", u), [cols(io["w_in"], KD, CG + 512 * u, CG + 512 * u + 512)]))
    for br in "abc":
        out.append((("br", br), [cols(io["w_branch_" + br], 4, 0, D_MODEL)]))
    for u in range(2):
        out.append((("wo", u), [cols(io["w_out"], KD, 512 * u, 512 * u + 512)]))
    ffn("f2")
    return out


STEPS = (
    "inverse_mm",
    "inverse_part",
    "G", "L", "RK", "a_ready", "bonus_in", "bonus_ss", "br_ev", "brm", "ckvT",
    "ckvT_ev", "cqT", "dTT", "down_d", "down_y", "exps", "ffn_a", "ffn_gu", "ffn_sg", "g_level", "g_ready", "gate",
    "group", "h", "hs", "kk0", "kk_sq", "kk_ss", "kt_T", "kt_ev", "kvT", "kvT_ev", "last_rows", "latent_ms",
    "latent_root", "lora_g", "lora_wa", "lt_T", "lt_even", "lt_odd", "masked", "mean_squares", "mixed", "ml_PT", "ml_done",
    "ml_exp", "ml_mm", "ml_nm", "ml_oT", "ml_olT", "ml_osb", "ml_p", "ml_prep", "ml_pt", "ml_pv", "ml_s", "ml_yc",
    "norm_sums", "normed", "odd", "pa", "pa_zeroed", "pam", "pbc_ev", "pbc_mm", "pgm", "prompt_T", "prompt_e",
    "prompt_mm", "prompt_nm", "prompt_o", "prompt_ol", "prompt_olev", "prompt_p", "prompt_pt", "prompt_s",
    "prompt_y", "q_rope", "q_rows", "qbd", "qcT", "qcT_ev", "qkT", "qk_ev", "ql", "ql_ev", "qrow_ev", "rhs",
    "rhs_ev", "roots", "rows", "rows_ready", "rwkv_done", "squared", "streams", "sw_PT", "sw_e", "sw_masked",
    "sw_mm", "sw_nm", "sw_p", "sw_pt", "sw_pv", "sw_own", "sw_y", "sw_s", "sws_done", "t_level", "tanh", "u", "u_ev", "ue",
    "x_f1", "x_f2", "x_mix", "y", "y_centred", "y_mean", "y_sq", "y_var", "zh", "zh_mm",
)


def build(nc, io):
    SCB, SCC = DH ** -0.5, (DNOPE + DROPE) ** -0.5
    with ExitStack() as ctx:
        def sb(name, cols):
            return ctx.enter_context(nc.sbuf_tensor(name, [P, cols], F32))

        def sem(name):
            return ctx.enter_context(nc.semaphore(name))

        x = sb("x", KD * T)[:, :].rearrange("p (k t) -> p k t", k=KD)
        h = sb("h", KD * T)[:, :].rearrange("p (k t) -> p k t", k=KD)
        cst = sb("cst", NCONST)
        par = sb("par", NPAR)
        kvn = sb("kvn", KV_LORA)
        ya, yb, yc = [sb(n, 4 * T)[:, :].rearrange("p (k t) -> p k t", k=4) for n in ("ya", "yb", "yc")]
        lora = sb("lora", 2 * W_A)
        sml = sb("sml", 16)
        big = sb("big", 7680)
        ring = sb("ring", NSLOT * SLOT)
        reg = sb("reg", 17408)
        ptab = ctx.enter_context(nc.sbuf_tensor("ptab", [1, NB * N_PAGES], I32))
        ps = ctx.enter_context(nc.psum_tensor("ps", [P, 8, 512], F32))

        def C(name, rows=P):
            at, w = CONST[name]
            return cst[0:rows, at:at + w]

        def pp(name, m, rows=P):
            return par[0:rows, PAR[name][0] + m:PAR[name][0] + m + 1]

        def cut(buf, at, a, b, rows=P):
            return buf[0:rows, at:at + a * b].rearrange("p (a b) -> p a b", a=a)

        ident, ones, onesblk = C("ident"), C("ones"), C("onesblk")
        act_t = cut(big, 0, KF, T)
        sqb = cut(big, 0, KD, T)
        yt = cut(reg, 0, KD, T)
        sg2 = cut(reg, 2560, 2, T)
        rstd = reg[:, 3200:3200 + T]
        gates = cut(big, 0, 24, T)
        mt = cut(reg, 4096, KD, T)
        pa = cut(reg, 0, NAT, PADT)
        xs = cut(big, 0, NAT, T)
        S_ = [cut(reg, NAT * PADT + 1280 * i, 4, T) for i in range(10)]
        th, sgd = reg[:, 0:T], reg[:, T:2 * T]
        Hp = cut(reg, 640, H, DH, 64)
        Ue, Ve, Tm = [cut(reg, 1152 + 512 * i, NB, DH, CHUNK) for i in range(3)]
        UV = [(Ue, Ve), [cut(ring, 512 * i, NB, DH, CHUNK) for i in (2, 3)]]
        Odd = [cut(reg, 2688 + 256 * i, 4, CHUNK, 64) for i in range(5)]
        MX = [cut(ring, 512 * i, H, CHUNK, CHUNK) for i in range(20)]
        (X8, X8T, Xo16, Xo32, Xo64, KK, RB, RK, X2, X2T, X4, Pm, Tt, TT, G, RHS, U, Vr, bdr, kdr) = MX
        Hse, Hso = cut(ring, 10240, 4, NB * DH, 64), cut(big, NAT * T, 4, NB * DH, 64)
        Hs = lambda hd: (Hso if hd % 2 else Hse)[:, hd // 2, :]
        lastT = cut(reg, 16126, NAT, 9)
        shin = cut(reg, 16326, NAT, NB)
        PBc = cut(reg, 0, 3, C_COLS)
        PBq = cut(reg, 2016, 3, 2048)
        PBv = cut(reg, 8160, 3, W_A)
        qT = cut(reg, 9696, 12, T)
        kT = cut(reg, 13536, 4, T)
        rt = reg[:, 14816:14816 + 1024]
        Sp = [ring[:, 8344 + 768 * i:9112 + 768 * i].rearrange("p (g k) -> p g k", g=3) for i in range(2)]
        Pc = [ring[:, 9880 + 256 * i:10136 + 256 * i] for i in range(2)]
        PTp = [cut(ring, 10392 + 256 * i, 2, P) for i in range(2)]
        OLp = [cut(ring, 10904 + 256 * i, 2, P) for i in range(2)]
        Kw = cut(big, 0, SW_TILES, W_A)
        Qbd = big[:, 6656:6656 + 768].rearrange("p (c g n) -> p c g n", c=4, g=3)
        Vw = cut(ring, 0, SW_TILES, W_A)
        Sw = [ring[0:NS, 6656:6656 + SW_COLS], reg[0:NS, 4064:4064 + SW_COLS]]
        KTw = [cut(ring, 8344, 4, 512), cut(reg, 2016, 4, 512)]
        PTw = cut(ring, 10392, SW_TILES, NS)
        Ow = cut(reg, 5752, H, DH, NS)
        PTn = ring[0:NS, 11224:11224 + NS]
        PnF = ring[0:NS, 11288:11288 + NS]
        cqT = cut(reg, 2016, 3, T)
        cup = cut(reg, 2976, 3, H * 96)
        kvup = cut(reg, 5280, 2, 1024)
        qrow = cut(reg, 7328, 3, H * 96)
        qcT = cut(reg, 9632, H, T)
        kvT = cut(reg, 12192, H, KV_LORA, DNOPE)
        ckvT = cut(reg, 16448, 3, T)
        rt2 = reg[:, 14240:14240 + 1024]
        olT = rt2.rearrange("p (c h t) -> p c h t", c=2, h=H)
        QR = reg[:, 15264:15264 + 512].rearrange("p (b h j) -> p b h j", b=NB, h=H)
        Osb = reg[0:NS, 15776:15776 + 256]
        PnL = reg[0:NS, 16032:16032 + NS]
        PTl = reg[0:NS, 16096:16096 + NS]
        KR = [cut(big, 3072, N_PAGES, 288), cut(ring, 0, N_PAGES, 288), cut(reg, 7328, N_PAGES, 288)]
        qlT = ring[:, 0:4096].rearrange("p (h c t) -> p h c t", h=H, c=2)
        QL = ring[:, 4608:5632].rearrange("p (c b n) -> p c b n", c=2, b=NB)
        KTl = [cut(ring, 5632 + 1536 * i, 3, 512) for i in range(2)]
        Pl = ring[0:NS, 8704:8704 + PAST + TS]
        PTL = cut(ring, 10760, N_PAGES, NS)

        s_dve = sem("vector_step")
        s_par, s_sml, s_out = sem("params_in"), sem("small_in"), sem("rows_out")
        s_slot = [sem(f"weights_in_{i}") for i in range(NSLOT)]
        s_kw = [sem(f"window_keys_in_{i}") for i in range(4)]
        s_vw, s_copy = sem("window_values_in"), sem("window_copied")
        s_kr = [[sem(f"pages_in_{i}_{half}") for half in range(2)] for i in range(3)]
        s_shin, s_shout, s_state, s_wkv = sem("shift_in"), sem("shift_out"), sem("states_in"), sem("states_out")
        s_once, s_arrive, s_go, s_pad = sem("constants_in"), sem("engines_at_layer_end"), sem("layer_begun"), sem("pad")
        S = {n: sem(n) for n in STEPS}
        per_layer = [s_dve, s_par, s_sml, s_out, s_vw, s_state, s_wkv, s_shin, s_shout] + s_kw + sum(s_kr, []) + s_slot + list(S.values())
        units = weight_units(io)
        uidx = {name: i for i, (name, _) in enumerate(units)}

        def landed(name):
            i = uidx[name]
            return s_slot[i % NSLOT], 16 * sum(len(units[j][1]) for j in range(i % NSLOT, i + 1, NSLOT))

        def used(name):
            kind, u = name[0], name[-1]
            if kind in ("f1", "f2"):
                return (S["ffn_gu"], FFN0[kind] + 2 * u + 2) if name[1] == "gu" else (S["down_d"], DOWN0[kind] + u + 1)
            return {"pa": lambda: (S["pam"], min(4 * u + 4, NAT)), "pbc": lambda: (S["pbc_mm"], 3 * u + 3),
                    "pg": lambda: (S["pgm"], 4 * u + 4), "br": lambda: (S["brm"], KD * "abc".index(str(u)) + KD),
                    "wo": lambda: (S["down_d"], DOWN0["mix"] + 4 * u + 4)}[kind]()

        def wslot(name, k, n, at=0):
            o = (uidx[name] % NSLOT) * SLOT + at
            return ring[:, o:o + k * n].rearrange("p (k n) -> p k n", k=k)

        def layer_end(eng, l):
            eng.sem_inc(s_arrive, 1)
            eng.wait_ge(s_go, l + 1)
            eng.sem_inc(s_pad, 1)

        def lay(ap, l):
            return ap[bass.ds(l, 1)]

        block = ctx.enter_context(nc.Block())

        def rwkv_sync(sp, l):
            sp.wait_ge(S["pa_zeroed"], 1)
            sp.dma_start(shin, lay(io["shiftT"], l).rearrange("a p n b -> p (a n) b")).then_inc(s_shin, 16)
            sp.wait_ge(*used(("pa", 3)))
            for r, buf in ((0, Hse), (1, Hso)):
                sp.dma_start(buf, lay(io["wkvT"], l)[:, r].rearrange("a p n v -> p (a n) v")).then_inc(s_state, 16)
            sp.wait_ge(S["last_rows"], 1)
            sp.dma_start(lay(io["o_shift"], l).rearrange("a p n b -> p (a n) b"), lastT).then_inc(s_shout, 16)
            sp.wait_ge(S["group"], 9)
            sp.dma_start(lay(io["o_wkv_p"], l).rearrange("a p n v -> p (a n) v"), Hp).then_inc(s_wkv, 16)
            for r, buf in ((0, Hse), (1, Hso)):
                sp.dma_start(lay(io["o_wkv_s"], l)[:, r].rearrange("a p n v -> p (a n) v"), buf).then_inc(s_wkv, 16)
            sp.wait_ge(s_wkv, 16 * 3)

        def attention_sync(sp, l):
            sp.wait_ge(S["rows_ready"], 3)
            for name, src in (("swa_k", PBq[:, :, 1536:2048]), ("swa_v", PBv), ("ckv", PBc[:, :, Q_LORA:Q_LORA + KV_LORA]),
                              ("krope", PBc[:, :, Q_LORA + KV_LORA:C_COLS])):
                sp.dma_start(lay(io[f"o_{name}_p"], l).rearrange("a b (t p) n -> p (a b t) n", p=P), src[:, 0:2, :]).then_inc(s_out, 16)
                if name.startswith("swa"):
                    for b in range(NB):
                        dst = lay(io[f"o_{name}_s"], l)[:, b, PAST - TS:PAST, :].rearrange("a r n -> (a r) n")
                        sp.dma_start(dst, src[TS * b:TS * b + TS, 2, :]).then_inc(s_out, 16)
                else:
                    dst = lay(io[f"o_{name}_s"], l).rearrange("a b t n -> (a b t) n")
                    sp.dma_start(dst, src[0:NS, 2, :]).then_inc(s_out, 16)

            def window(cache, b, part):
                src = lay(cache, l)[:, b]
                if part < 2:
                    return src.rearrange("a (p r) n -> p (a r) n", r=16)[:, 4 * part:4 * part + 4, :]
                if part == 2:
                    return src[:, PAST - 512:PAST].rearrange("a (p r) n -> p (a r) n", r=4)
                return src[:, PAST - P:PAST].rearrange("a p n -> p a n")

            def keys(b, parts):
                for i in parts:
                    if b:
                        sp.wait_ge(S["kt_T"], 16 * (b - 1) + 4 * i + 4)
                    sp.dma_start(Kw[:, 4 * i:min(4 * i + 4, SW_TILES), :], window(io["cache_swa_k"], b, i)).then_inc(s_kw[i], 16)

            keys(0, range(4))
            for b in range(NB):
                if b:
                    sp.wait_ge(S["sw_pv"], b)
                for i in range(4):
                    sp.dma_start(Vw[:, 4 * i:min(4 * i + 4, SW_TILES), :], window(io["cache_swa_v"], b, i)).then_inc(s_vw, 16)
                if b == 0:
                    keys(1, range(4))
                if b + 2 < NB:
                    keys(b + 2, range(4))
            sp.wait_ge(S["sws_done"], NB)
            sp.wait_ge(s_out, N_ROWS_OUT)
            sp.dma_start(cup, lay(io["c_q_up"], l).rearrange("a (k p) n -> p (a k) n", p=P)).then_inc(s_sml, 16)
            sp.dma_start(kvup, lay(io["c_kv_up"], l).rearrange("a (k p) n -> p (a k) n", p=P)).then_inc(s_sml, 16)
            for b in range(NB):
                if b in (1, 2):
                    sp.wait_ge(S["prompt_y"], 2 * H + 16)
                elif b:
                    sp.wait_ge(S["ml_pv"], b - 2)
                for n in range(N_PAGES):
                    i = b * N_PAGES + n
                    page = sp.value_load(ptab[0:1, i:i + 1], min_val=0, max_val=N_POOL - 1)
                    for c0, cache, w in ((0, "ckv", KV_LORA), (KV_LORA, "krope", DROPE)):
                        src = lay(io["cache_mla_" + cache], l)[:, bass.ds(page, 1)].rearrange("a b p n -> p (a b n)")
                        sp.dma_start(KR[b % 3][:, n, c0:c0 + w], src).then_inc(s_kr[b % 3][n // 8], 16)
            sp.wait_ge(S["ml_done"], 1)

        @block.sync
        def _(sp):
            sp.dma_start(cst[:, :], io["consts"]).then_inc(s_once, 16)
            sp.dma_start(x, io["xT"]).then_inc(s_once, 16)
            sp.dma_start(ptab[:, :], io["page_table"].rearrange("b n -> (b n)").unsqueeze(0)).then_inc(s_once, 16)
            sp.wait_ge(s_once, 48)
            with sp.Fori(0, DEPTH) as l:
                sp.dma_start(par[:, :], lay(io["params"], l).rearrange("a p n -> p (a n)")).then_inc(s_par, 16)
                sp.dma_start(kvn[:, :], lay(io["c_kv_norm"], l).rearrange("a n -> (a n)").partition_broadcast(P)).then_inc(s_par, 16)
                for lo, hi, name in ((0, 32, "a_w2"), (32, 64, "a_a2")):
                    sp.dma_start(lora[lo:hi, 0:W_A], lay(io[name], l).rearrange("a p n -> p (a n)")).then_inc(s_par, 16)
                sp.dma_start(lora[0:96, W_A:2 * W_A], lay(io["a_g2"], l).rearrange("a p n -> p (a n)")).then_inc(s_par, 16)
                for i, (name, srcs) in enumerate(units):
                    if name == ("pbc", 0):
                        rwkv_sync(sp, l)
                    if name == ("pg", 0):
                        attention_sync(sp, l)
                    if i >= NSLOT:
                        sp.wait_ge(*used(units[i - NSLOT][0]))
                    at = (i % NSLOT) * SLOT
                    for src, k, n in srcs:
                        sp.dma_start(ring[:, at:at + k * n].rearrange("p (k n) -> p k n", k=k), src(l)).then_inc(s_slot[i % NSLOT], 16)
                        at += k * n
                sp.wait_ge(S["x_f2"], KD)
                sp.wait_ge(S["roots"], ROOTS["f2_post"])
                sp.wait_ge(S["norm_sums"], NORMS["f2_post"])
                sp.wait_ge(s_out, N_ROWS_OUT)
                sp.wait_ge(s_wkv, 16 * 3)
                sp.wait_ge(s_shout, 16)
                sp.wait_ge(s_arrive, 4 * (l + 1))
                sp.sem_inc(s_pad, 1)
                for s in per_layer:
                    sp.sem_clear(s)
                sp.sem_inc(s_go, 1)
            sp.dma_start(io["yT"], x).then_inc(s_once, 16)
            sp.wait_ge(s_once, 64)

        @block.gpsimd
        def _(pool):
            with pool.Fori(0, DEPTH) as l:
                rows = PAST - TS
                copies = 0
                pool.wait_ge(S["ffn_gu"], 2)
                for b in range(NB):
                    for n in ("k", "v"):
                        if copies:
                            pool.wait_ge(s_copy, l * (16 * 2 * NB) + 16 * copies)
                            pool.sem_inc(s_pad, 1)
                        copies += 1
                        src = lay(io["cache_swa_" + n], l)[:, b, TS:PAST].rearrange("a r n -> (a r n)")
                        dst = lay(io[f"o_swa_{n}_s"], l)[:, b, 0:rows].rearrange("a r n -> (a r n)")
                        pool.dma_start(dst.rearrange("(q n) -> q n", q=240),
                                       src.rearrange("(q n) -> q n", q=240)).then_inc(s_copy, 16)
                pool.wait_ge(s_copy, (l + 1) * (16 * 2 * NB))
                layer_end(pool, l)

        @block.tensor
        def _(pe):
            pe.wait_ge(s_once, 48)

            def mm(out, lhsT, rhs, first=True, last=True):
                return pe.matmul(out, lhsT, rhs, start=first, stop=last, skip_group_check=True)

            def tr(out, in_, rows=P):
                return pe.transpose(out, in_, ident[0:rows, 0:rows])


            def square_sum(src, k):
                q = mm(ps[:, 7, 0:T], ones, src[:, k, :], k == 0, k == KD - 1)
                if k == KD - 1:
                    q.then_inc(S["norm_sums"], 1)

            def pre_sum(tag):
                for k in range(KD):
                    pe.wait_ge(S["squared"], KD * (PRES[tag] - 1) + k + 1)
                    square_sum(sqb, k)

            def ffn(f):
                pre_sum(f + "_pre")
                for m in range(KF):
                    u = (f, "gu", m // 2)
                    pe.wait_ge(*landed(u))
                    if m >= 3:
                        pe.wait_ge(S["ffn_a"], FFN0[f] + m - 2)
                    for bank, at in ((m % 3, 0), (3 + m % 3, 2048)):
                        w = wslot(u, KD, 256, at)
                        for k in range(KD):
                            if m == 0 and at == 0:
                                pe.wait_ge(S["normed"], KD * (PRES[f + "_pre"] - 1) + k + 1)
                            q = mm(ps[:, bank, 0:T], w[:, k, (m % 2) * P:(m % 2) * P + P], h[:, k, :], k == 0, k == KD - 1)
                    q.then_inc(S["ffn_gu"], 1)
                pe.wait_ge(S["ffn_a"], FFN0[f] + KF)
                for m in range(KD):
                    u = (f, "d", m)
                    pe.wait_ge(*landed(u))
                    if m >= 4:
                        pe.wait_ge(S["down_y"], DOWN0[f] + m - 3)
                    w = wslot(u, KF, P)
                    for k in range(KF):
                        q = mm(ps[:, m % 4, 0:T], w[:, k, :], act_t[:, k, :], k == 0, k == KF - 1)
                    q.then_inc(S["down_d"], 1)
                    if m:
                        pe.wait_ge(S["down_y"], DOWN0[f] + m)
                        square_sum(h, m - 1)
                pe.wait_ge(S["down_y"], DOWN0[f] + KD)
                square_sum(h, KD - 1)

            def a_proj():
                pre_sum("mix_pre")
                pe.wait_ge(S["normed"], KD * PRES["mix_pre"])
                for m, (c0, rows) in enumerate(A_TILES):
                    u = ("pa", min(c0 // 512, 3))
                    pe.wait_ge(*landed(u))
                    if m >= 6:
                        pe.wait_ge(S["pa"], m - 5)
                    n = 512 if c0 < 1536 else 160
                    w, at = wslot(u, KD, n), c0 - 512 * (c0 // 512)
                    for k in range(KD):
                        q = mm(ps[0:rows, m % 6, 0:T], w[:, k, at:at + rows], h[:, k, :], k == 0, k == KD - 1)
                    q.then_inc(S["pam"], 1)

            def rwkv():
                pe.wait_ge(S["tanh"], 1)
                for m in range(4):
                    mm(ps[:, m, 0:T], lora[0:32, m * P:m * P + P], th[0:32, :])
                    q = mm(ps[:, 4 + m, 0:T], lora[32:64, m * P:m * P + P], xs[32:64, 12, :])
                q.then_inc(S["lora_wa"], 1)
                pe.wait_ge(S["a_ready"], 4)
                for m in range(4):
                    q = mm(ps[:, m, 0:T], lora[0:96, W_A + m * P:W_A + m * P + P], sgd[0:96, :])
                q.then_inc(S["lora_g"], 1)
                pe.wait_ge(S["kk_sq"], 1)
                for m in range(4):
                    q = mm(ps[:, 4 + m, 0:T], onesblk, S_[9][:, m, :])
                q.then_inc(S["kk_ss"], 1)
                pe.wait_ge(S["bonus_in"], 1)
                pe.wait_ge(S["g_ready"], 1)
                for m in range(4):
                    q = mm(ps[:, m, 0:T], onesblk, S_[9][:, m, :])
                q.then_inc(S["bonus_ss"], 1)
                pe.wait_ge(S["streams"], 1)
                ZT, bdT, kdT, RqT, vT = S_[6], S_[0], S_[7], S_[3], xs[:, 8:12]
                for g in range(5):
                    t0, sample = g * CHUNK, g == 4
                    odd = {id(ZT): Odd[0], id(bdT): Odd[1], id(kdT): Odd[2], id(RqT): Odd[3]}
                    at = lambda a, hd: odd[id(a)][:, hd // 2, :] if hd % 2 else a[0:64, hd // 2, t0:t0 + CHUNK]
                    halves = [(hf, range(4 * hf, 4 * hf + 4)) for hf in range(2)]
                    part = lambda b, k, hd: ps[0:64, 4 * (hd // 4) + b, 256 * k + 64 * (hd % 4):256 * k + 64 * (hd % 4) + 64]

                    def each(b, k, heads, f):
                        for hd in heads:
                            q = f(part(b, k, hd), hd)
                        return q

                    for hf, heads in halves:
                        if g:
                            pe.wait_ge(S["group"], 2 * g - 1 + hf)
                        for b, k, a in ((0, 0, vT), (0, 1, bdT), (1, 0, kdT)):
                            for m in range(2):
                                tr(ps[0:64, 4 * hf + b, 256 * k + m * P:256 * k + m * P + P], a[:, 2 * hf + m, t0:t0 + CHUNK])
                        pe.wait_ge(S["odd"], 5 * g + 5)
                        each(1, 1, heads, lambda o, hd: mm(o, at(kdT, hd), at(RqT, hd))).then_inc(S["rows"], 1)
                        each(2, 0, heads, lambda o, hd: mm(o, at(ZT, hd), at(bdT, hd)))
                        each(2, 1, heads, lambda o, hd: mm(o, at(bdT, hd), at(ZT, hd)))
                        each(3, 0, heads, lambda o, hd: mm(o, at(kdT, hd), at(ZT, hd)))
                        each(3, 1, heads, lambda o, hd: mm(o, at(bdT, hd), at(RqT, hd))).then_inc(S["RK"], 1)
                    for hf, heads in halves:
                        pe.wait_ge(S["masked"], 2 * g + hf + 1)
                        each(0, 0, heads, lambda o, hd: mm(o, X8T[:, hd], X8[:, hd]))
                        each(0, 1, heads, lambda o, hd: mm(o, X8[:, hd], X8T[:, hd])).then_inc(S["inverse_mm"], 1)
                    for i, (b, f) in enumerate(((1, lambda o, hd: mm(o, X2T[:, hd], X2[:, hd])),
                                                (2, lambda o, hd: mm(o, X2T[:, hd], X4[:, hd])),
                                                (3, lambda o, hd: mm(o, X8T[:, hd], Pm[:, hd])),
                                                (0, lambda o, hd: tr(o, Tt[:, hd], 64)))):
                        for hf, heads in halves:
                            pe.wait_ge(S["inverse_part"], 10 * g + 2 * i + hf + 1)
                            each(b, 0, heads, f).then_inc(S["inverse_mm"], 1)
                    if not sample:
                        for i, xo in enumerate((Xo16, Xo32, Xo64)):
                            for hf, heads in halves:
                                if i:
                                    pe.wait_ge(S["t_level"], 6 * g + 2 * i - 1 + hf)
                                else:
                                    pe.wait_ge(S["inverse_part"], 10 * g + 9 + hf)
                                each(1, 0, heads, lambda o, hd: mm(o, xo[:, hd], Tt[:, hd])).then_inc(S["G"], 1)
                            for hf, heads in halves:
                                pe.wait_ge(S["g_level"], 6 * g + 2 * i + hf + 1)
                                each(2, 0, heads, lambda o, hd: mm(o, TT[:, hd], G[:, hd]))
                                each(2, 1, heads, lambda o, hd: mm(o, G[:, hd], TT[:, hd])).then_inc(S["dTT"], 1)
                        for hf, heads in halves:
                            pe.wait_ge(S["t_level"], 6 * g + 5 + hf)
                            for hd in heads:
                                mm(part(3, 0, hd), at(ZT, hd), Hp[:, hd, :], True, False)
                                q = mm(part(3, 0, hd), KK[:, hd], Vr[:, hd], False, True)
                            q.then_inc(S["rhs"], 1)
                        for hf, heads in halves:
                            pe.wait_ge(S["rhs_ev"], 2 * g + hf + 1)
                            each(0, 0, heads, lambda o, hd: mm(o, TT[:, hd], RHS[:, hd])).then_inc(S["u"], 1)
                        for hf, heads in halves:
                            pe.wait_ge(S["u_ev"], 2 * g + hf + 1)
                            for hd in heads:
                                r0 = 64 * (hd % 2)
                                o = ps[r0:r0 + 64, 4 * hf + 1, 64 * (hd % 4 // 2):64 * (hd % 4 // 2) + 64]
                                mm(o, U[:, hd], RB[:, hd], True, False)
                                mm(o, Vr[:, hd], RK[:, hd], False, False)
                                q = mm(o, Hp[:, hd, :], at(RqT, hd), False, True)
                            q.then_inc(S["y"], 1)
                            for hd in heads:
                                mm(part(2, 0, hd), bdr[:, hd], U[:, hd], True, False)
                                q = mm(part(2, 0, hd), kdr[:, hd], Vr[:, hd], False, True)
                            q.then_inc(S["h"], 1)
                        continue
                    bank = lambda b, hd: ps[0:64, b, 64 * hd:64 * hd + 64]
                    pe.wait_ge(S["inverse_part"], 10 * g + 10)
                    pe.wait_ge(s_state, 32)
                    for hd in range(H):
                        if hd >= 2:
                            pe.wait_ge(S["zh"], hd - 1)
                        mm(ps[0:64, hd % 2, :], at(ZT, hd), Hs(hd)).then_inc(S["zh_mm"], 1)
                    for hd in range(H):
                        q = mm(bank(3, hd), KK[:, hd], Vr[:, hd])
                    q.then_inc(S["rhs"], 1)
                    pe.wait_ge(S["rhs_ev"], 2 * g + 1)
                    for hd in range(H):
                        q = mm(bank(4, hd), TT[:, hd], RHS[:, hd])
                    q.then_inc(S["u"], 1)
                    pe.wait_ge(S["u_ev"], 2 * g + 1)
                    for hd in range(H):
                        r0 = 64 * (hd % 2)
                        o = ps[r0:r0 + 64, 5, 64 * (hd // 2):64 * (hd // 2) + 64]
                        mm(o, U[:, hd], RB[:, hd], True, False)
                        mm(o, Vr[:, hd], RK[:, hd], False, False)
                        for b in range(NB):
                            q = mm(o[:, TS * b:TS * b + TS], Hs(hd)[:, DH * b:DH * b + DH],
                                   at(RqT, hd)[:, TS * b:TS * b + TS], False, b == NB - 1)
                    q.then_inc(S["y"], 1)
                    for hd in range(H):
                        pe.wait_ge(S["ue"], hd + 1)
                        ue, ve = [a.rearrange("p b v -> p (b v)") for a in UV[hd % 2]]
                        mm(ps[0:64, 6 + hd % 2, :], bdr[:, hd], ue, True, False)
                        q = mm(ps[0:64, 6 + hd % 2, :], kdr[:, hd], ve, False, True)
                        q.then_inc(S["hs"], 1)
                Y = S_[8]
                pe.wait_ge(S["group"], 9)
                for m in range(4):
                    q = mm(ps[:, m, 0:T], onesblk, Y[:, m, :])
                q.then_inc(S["y_mean"], 1)
                pe.wait_ge(S["y_sq"], 1)
                for m in range(4):
                    q = mm(ps[:, 4 + m, 0:T], onesblk, S_[0][:, m, :])
                q.then_inc(S["y_var"], 1)

            def bc_proj():
                pe.wait_ge(S["rwkv_done"], 1)
                n = 0
                for u in range(7):
                    pe.wait_ge(*landed(("pbc", u)))
                    cols = 160 if u == 1 else 512
                    w = wslot(("pbc", u), KD, cols)
                    for i, t0, rows in TOK_TILES:
                        if n >= 6:
                            pe.wait_ge(S["pbc_ev"], n - 5)
                        for k in range(KD):
                            q = mm(ps[0:rows, n % 6, 0:cols], h[:, k, t0:t0 + rows], w[:, k, :], k == 0, k == KD - 1)
                        q.then_inc(S["pbc_mm"], 1)
                        n += 1
                pe.wait_ge(S["rows_ready"], 3)
                n = 0
                for c in range(16):
                    if c >= 4:
                        pe.wait_ge(S["qk_ev"], c - 3)
                    for i, t0, rows in TOK_TILES:
                        q = tr(ps[:, c % 4, t0:t0 + rows], PBq[0:rows, i, c * P:c * P + P], rows)
                    q.then_inc(S["qkT"], 1)
                pe.wait_ge(S["qk_ev"], 16)
                for j, c0 in enumerate((Q_LORA, Q_LORA + P, C_COLS - 96)):
                    w = 96 if j == 2 else P
                    for i, t0, rows in TOK_TILES:
                        q = tr(ps[0:w, j, t0:t0 + rows], PBc[0:rows, i, c0:c0 + w], rows)
                q.then_inc(S["ckvT"], 1)

            def sw_prompt():
                pe.wait_ge(S["ckvT_ev"], 1)

                def scores(n):
                    t, hd = n // H, n % H
                    r0 = 64 * (hd % 2)
                    if n >= 2:
                        pe.wait_ge(S["prompt_s"], n - 1)
                    for g in range(3):
                        col = (n % 2) * 1024 + g * 256
                        o = ps[:, col // 512, col % 512:col % 512 + (t + 1) * P]
                        q = mm(o, qT[r0:r0 + 64, 4 * g + hd // 2, t * P:t * P + P], kT[r0:r0 + 64, hd // 2, 0:(t + 1) * P])
                    q.then_inc(S["prompt_mm"], 1)

                def values(n):
                    hd = n % H
                    pe.wait_ge(S["prompt_pt"], n + 1)
                    if n >= 2:
                        pe.wait_ge(S["prompt_y"], n - 1)
                    r0 = 64 * (hd % 2)
                    for i in range(n // H + 1):
                        q = mm(ps[r0:r0 + 64, 6 + n % 2, 0:P], PBv[:, i, hd * 64:hd * 64 + 64], PTp[n % 2][:, i, :], i == 0, i == n // H)
                    q.then_inc(S["prompt_o"], 1)

                scores(0)
                scores(1)
                for n in range(17):
                    if n + 2 < 16:
                        scores(n + 2)
                    if n < 16:
                        pe.wait_ge(S["prompt_p"], n + 1)
                        for i in range(n // H + 1):
                            q = tr(ps[:, 4 + n % 2, i * P:i * P + P], Pc[n % 2][:, i * P:i * P + P])
                        q.then_inc(S["prompt_T"], 1)
                    if n:
                        values(n - 1)

            def sw_sample():
                pe.wait_ge(S["prompt_y"], 16)

                def transposes(part, c):
                    b, q4, n = part // 4, part % 4, 4 * part + c
                    if c == 0:
                        pe.wait_ge(s_kw[q4], 16 * (b + 1))
                    if n >= 2:
                        pe.wait_ge(S["kt_ev"], n - 1)
                    for t in range(4 if q4 < 3 else 1):
                        q = tr(ps[:, 4 + n % 2, t * P:t * P + P], Kw[:, 4 * q4 + t, c * P:c * P + P])
                    q.then_inc(S["kt_T"], 1)

                def scores(part, ahead):
                    b, q4 = part // 4, part % 4
                    nt = 4 if q4 < 3 else 1
                    g = 2 if q4 < 2 else 1 if q4 == 2 else 0
                    if q4 == 0:
                        pe.wait_ge(S["qbd"], 8 * b + 8)
                        if b:
                            pe.wait_ge(S["sw_masked"], b)
                    for c in range(4):
                        if ahead:
                            transposes(part + 1, c)
                        pe.wait_ge(S["kt_ev"], 4 * part + c + 1)
                        q = mm(ps[0:NS, q4, 0:nt * P], Qbd[:, c, g, :], KTw[part % 2][:, c, 0:nt * P], c == 0, c == 3)
                    q.then_inc(S["sw_mm"], 1)
                    if q4 == 3:
                        for g in range(3):
                            for c in range(4):
                                q = mm(ps[0:NS, 3, P + g * TS:P + g * TS + TS], Qbd[:, c, g, :],
                                       kT[:, c, SEQ + TS * b:SEQ + TS * b + TS], c == 0, c == 3)
                        q.then_inc(S["sw_s"], 1)

                def shares(b):
                    pe.wait_ge(S["sw_p"], b + 1)
                    if b:
                        pe.wait_ge(S["sws_done"], b)
                    for t in range(SW_TILES):
                        q = tr(ps[:, 6 + t // 8, (t % 8) * NS:(t % 8) * NS + NS], Sw[b % 2][:, t * P:t * P + P], NS)
                    q = tr(ps[0:NS, 7, 320:384], PnF, NS)
                    q.then_inc(S["sw_PT"], 1)

                def values(b):
                    pe.wait_ge(S["sw_pt"], b + 1)
                    pe.wait_ge(s_vw, 64 * (b + 1))
                    for t in range(SW_TILES):
                        mm(ps[0:NS, 7, :], PTw[:, t, :], Vw[:, t, :], t == 0, False)
                    mm(ps[0:NS, 7, :], PTn, PBv[0:NS, 2, :], False, True).then_inc(S["sw_pv"], 1)

                def by_channel(b):
                    pe.wait_ge(S["sw_own"], b + 1)
                    for c in range(4):
                        q = mm(ps[:, 6, c * TS:c * TS + TS], Ow.rearrange("p h v -> p (h v)")[:, c * P:c * P + P], C("tsel", NS))
                    q.then_inc(S["sw_y"], 1)

                for c in range(4):
                    transposes(0, c)
                for part in range(4 * NB):
                    scores(part, part + 1 < 4 * NB)
                    if part % 4 == 0 and part >= 8:
                        by_channel(part // 4 - 2)
                    if part % 4 == 2 and part > 4:
                        shares(part // 4 - 1)
                    if part % 4 == 3 and part > 4:
                        values(part // 4 - 1)
                by_channel(NB - 2)
                shares(NB - 1)
                values(NB - 1)
                by_channel(NB - 1)

            def latent_prep():
                pe.wait_ge(S["sws_done"], NB)
                for k in range(3):
                    for i, t0, rows in TOK_TILES:
                        q = tr(ps[:, k, t0:t0 + rows], PBc[0:rows, i, k * P:k * P + P], rows)
                q.then_inc(S["cqT"], 1)
                pe.wait_ge(s_sml, 32)
                for hd in range(H):
                    for c in range(2):
                        q = tr(ps[:, 3 + hd // 2, (hd % 2) * 256 + c * P:(hd % 2) * 256 + c * P + P], kvup[:, c, hd * P:hd * P + P])
                q.then_inc(S["kvT"], 1)
                pe.wait_ge(S["kvT_ev"], 1)
                n = 0
                for i, t0, rows in TOK_TILES:
                    for j in range(2):
                        for k in range(3):
                            q = mm(ps[0:rows, n, 0:384], cqT[:, k, t0:t0 + rows], cup[:, k, j * 384:j * 384 + 384], k == 0, k == 2)
                        n += 1
                q.then_inc(S["q_rows"], 1)
                pe.wait_ge(S["q_rope"], 3)
                for hd in range(H):
                    if hd >= 4:
                        pe.wait_ge(S["qcT_ev"], hd - 3)
                    for i, t0, rows in TOK_TILES:
                        q = tr(ps[0:96, hd % 4, t0:t0 + rows], qrow[0:rows, i, hd * 96:hd * 96 + 96], rows)
                    q.then_inc(S["qcT"], 1)
                for n in range(16):
                    pe.wait_ge(S["qcT_ev"], max(n // 2, 7) + 1)
                    if n >= 4:
                        pe.wait_ge(S["ql_ev"], n - 3)
                    mm(ps[:, 4 + n % 4, 0:T], kvT[:, n // 2, (n % 2) * P:(n % 2) * P + P], qcT[0:64, n // 2, :]).then_inc(S["ql"], 1)

            def ml_prompt():
                pe.wait_ge(S["ml_prep"], 1)

                def scores(n):
                    t, hd = n // H, n % H
                    if n >= 2:
                        pe.wait_ge(S["prompt_s"], 2 * H + n - 1)
                    w = (t + 1) * P
                    o = ps[:, n % 2, 0:w]
                    for c in range(2):
                        mm(o, qlT[:, hd, c, t * P:t * P + P], ckvT[:, c, 0:w], c == 0, False)
                    mm(o, qcT[64:96, hd, t * P:t * P + P], ckvT[64:96, 2, 0:w], False, True).then_inc(S["prompt_mm"], 1)

                def latents(n):
                    pe.wait_ge(S["prompt_pt"], 2 * H + n + 1)
                    if n >= 2:
                        pe.wait_ge(S["prompt_olev"], n - 1)
                    for c in range(2):
                        for i in range(n // H + 1):
                            q = mm(ps[:, 4 + n % 2, c * P:c * P + P], PBc[:, i, Q_LORA + c * P:Q_LORA + c * P + P],
                                   PTp[n % 2][:, i, :], i == 0, i == n // H)
                    q.then_inc(S["prompt_ol"], 1)

                def values(n):
                    hd = n % H
                    pe.wait_ge(S["prompt_olev"], n + 1)
                    if n >= 2:
                        pe.wait_ge(S["prompt_y"], 2 * H + n - 1)
                    r0 = 64 * (hd % 2)
                    for c in range(2):
                        q = mm(ps[r0:r0 + 64, 6 + n % 2, 0:P], kvup[:, c, hd * P + 64:hd * P + P], OLp[n % 2][:, c, :], c == 0, c == 1)
                    q.then_inc(S["prompt_o"], 1)

                scores(0)
                scores(1)
                for n in range(18):
                    if n + 2 < 16:
                        scores(n + 2)
                    if n < 16:
                        pe.wait_ge(S["prompt_p"], 2 * H + n + 1)
                        for i in range(n // H + 1):
                            q = tr(ps[:, 2 + n % 2, i * P:i * P + P], Pc[n % 2][:, i * P:i * P + P])
                        q.then_inc(S["prompt_T"], 1)
                    if 1 <= n < 17:
                        latents(n - 1)
                    if n >= 2:
                        values(n - 2)

            def ml_sample():
                pe.wait_ge(S["prompt_y"], 2 * H + 16)

                def transposes(n):
                    b, part = n // N_PAGES, n // 4
                    if n % 4 == 0:
                        pe.wait_ge(s_kr[b % 3][part % 4 // 2], 16 * N_PAGES * (b // 3 + 1))
                    if n >= 2:
                        pe.wait_ge(S["lt_odd" if n % 2 else "lt_even"], n // 2)
                    o, page = ps[:, 5 + n % 2, :], KR[b % 3][:, n % N_PAGES, :]
                    tr(o[:, 0:P], page[:, 0:P])
                    tr(o[:, P:2 * P], page[:, P:2 * P])
                    tr(o[0:96, 2 * P:3 * P], page[:, 192:288]).then_inc(S["lt_T"], 1)

                def scores(part, ahead):
                    b, q4 = part // 4, part % 4
                    if b and q4 == 0:
                        pe.wait_ge(S["ml_exp"], b)
                    pe.wait_ge(S["lt_even"], 2 * part + 2)
                    pe.wait_ge(S["lt_odd"], 2 * part + 2)
                    kt, qr = KTl[part % 2], QR[64:96, b].rearrange("p h j -> p (h j)")
                    for c in range(2):
                        if ahead:
                            transposes(4 * part + 4 + c)
                        mm(ps[0:NS, q4, :], QL[:, c, b, :], kt[:, c, :], c == 0, False)
                    if ahead:
                        transposes(4 * part + 6)
                    mm(ps[0:NS, q4, :], qr, kt[64:96, 2, :], False, True).then_inc(S["ml_mm"], 1)
                    if ahead:
                        transposes(4 * part + 7)
                    if q4 == 3:
                        o = ps[0:NS, 4, 0:TS]
                        tk = slice(SEQ + TS * b, SEQ + TS * b + TS)
                        for c in range(2):
                            mm(o, QL[:, c, b, :], ckvT[:, c, tk], c == 0, False)
                        mm(o, qr, ckvT[64:96, 2, tk], False, True).then_inc(S["ml_s"], 1)

                def values(b, tiles):
                    pe.wait_ge(S["ml_p"], b + 1)
                    if b:
                        pe.wait_ge(S["ml_olT"], b)
                    pe.wait_ge(S["lt_even"], tiles // 2)
                    pe.wait_ge(S["lt_odd"], tiles // 2)
                    for t in range(N_PAGES):
                        tr(ps[:, 5 + 2 * (t // 8), (t % 8) * NS:(t % 8) * NS + NS], Pl[:, t * P:t * P + P], NS)
                    tr(ps[0:NS, 6, 0:NS], PnL, NS).then_inc(S["ml_PT"], 1)
                    pe.wait_ge(S["ml_pt"], b + 1)
                    o = ps[0:NS, 4, 256:512]
                    for t in range(N_PAGES):
                        mm(o, PTL[:, t, :], KR[b % 3][:, t, 0:KV_LORA], t == 0, False)
                    mm(o, PTl, PBc[0:NS, 2, Q_LORA:Q_LORA + KV_LORA], False, True).then_inc(S["ml_pv"], 1)

                def by_channel(b):
                    pe.wait_ge(S["ml_osb"], b + 1)
                    for c in range(2):
                        q = tr(ps[:, 7, c * NS:c * NS + NS], Osb[:, c * P:c * P + P], NS)
                    q.then_inc(S["ml_oT"], 1)

                for n in range(4):
                    transposes(n)
                for part in range(4 * NB):
                    scores(part, part + 1 < 4 * NB)
                    if part % 4 == 0 and part >= 8:
                        by_channel(part // 4 - 2)
                    if part % 4 == 3 and part > 4:
                        values(part // 4 - 1, min(4 * part + 8, NB * N_PAGES))
                by_channel(NB - 2)
                values(NB - 1, NB * N_PAGES)
                by_channel(NB - 1)
                pe.wait_ge(S["ml_olT"], NB)
                for hd in range(H):
                    r0 = 64 * (hd % 2)
                    for c in range(2):
                        q = mm(ps[r0:r0 + 64, 0, (hd // 2) * NS:(hd // 2) * NS + NS], kvup[:, c, hd * P + 64:hd * P + P], olT[:, c, hd, :], c == 0, c == 1)
                q.then_inc(S["ml_yc"], 1)

            def mix():
                pe.wait_ge(S["ml_done"], 1)
                for m in range(24):
                    u = ("pg", m // 4)
                    pe.wait_ge(*landed(u))
                    if m >= 8:
                        pe.wait_ge(S["gate"], m - 7)
                    w = wslot(u, KD, 512)
                    for k in range(KD):
                        q = mm(ps[:, m % 8, 0:T], w[:, k, (m % 4) * P:(m % 4) * P + P], h[:, k, :], k == 0, k == KD - 1)
                    q.then_inc(S["pgm"], 1)
                pe.wait_ge(S["gate"], 24)
                for i, (br, y) in enumerate((("a", ya), ("b", yb), ("c", yc))):
                    u = ("br", br)
                    pe.wait_ge(*landed(u))
                    w = wslot(u, 4, D_MODEL)
                    for m in range(KD):
                        if 8 * i + m >= 8:
                            pe.wait_ge(S["br_ev"], 8 * i + m - 7)
                        for k in range(4):
                            q = mm(ps[:, m, 0:T], w[:, k, m * P:m * P + P], y[:, k, :], k == 0, k == 3)
                        q.then_inc(S["brm"], 1)
                pe.wait_ge(S["br_ev"], 24)
                for m in range(KD):
                    u = ("wo", m // 4)
                    pe.wait_ge(*landed(u))
                    if m >= 4:
                        pe.wait_ge(S["down_y"], DOWN0["mix"] + m - 3)
                    w = wslot(u, KD, 512)
                    for k in range(KD):
                        q = mm(ps[:, m % 4, 0:T], w[:, k, (m % 4) * P:(m % 4) * P + P], mt[:, k, :], k == 0, k == KD - 1)
                    q.then_inc(S["down_d"], 1)
                    if m:
                        pe.wait_ge(S["down_y"], DOWN0["mix"] + m)
                        square_sum(h, m - 1)
                pe.wait_ge(S["down_y"], DOWN0["mix"] + KD)
                square_sum(h, KD - 1)

            with pe.Fori(0, DEPTH) as l:
                ffn("f1")
                a_proj()
                rwkv()
                bc_proj()
                sw_prompt()
                sw_sample()
                latent_prep()
                ml_prompt()
                ml_sample()
                mix()
                ffn("f2")
                layer_end(pe, l)

        @block.scalar
        def _(act):
            act.wait_ge(s_once, 48)

            def root(tag, v):
                act.wait_ge(S["mean_squares"], ROOTS[tag])
                act.activation(v, v, ACT.Sqrt).then_inc(S["roots"], 1)

            def square_x(tag, f=None):
                for k in range(KD):
                    if f:
                        act.wait_ge(S["x_" + f], k + 1)
                    act.activation(sqb[:, k, :], x[:, k, :], ACT.Square).then_inc(S["squared"], 1)
                root(tag, rstd)

            def down(f):
                for m in range(KD):
                    act.wait_ge(S["down_d"], DOWN0[f] + m + 1)
                    act.activation(yt[:, m, :], ps[:, m % 4, 0:T], ACT.Copy)
                    act.activation(h[:, m, :], ps[:, m % 4, 0:T], ACT.Square).then_inc(S["down_y"], 1)
                root(f + "_post", rstd)

            def ffn(f):
                for m in range(KF):
                    act.wait_ge(S["ffn_gu"], FFN0[f] + m + 1)
                    if m >= 2:
                        act.wait_ge(S["ffn_a"], FFN0[f] + m - 1)
                    act.activation(sg2[:, m % 2, :], ps[:, m % 3, 0:T], ACT.Sigmoid).then_inc(S["ffn_sg"], 1)
                down(f)

            def rwkv():
                act.wait_ge(s_par, 16 * 5)
                act.wait_ge(S["pa_zeroed"], 1)
                for m, (_, rows) in enumerate(A_TILES):
                    act.wait_ge(S["pam"], m + 1)
                    act.activation(pa[0:rows, m, 1:1 + SEQ], ps[0:rows, m % 6, 0:SEQ], ACT.Copy)
                    act.activation(pa[0:rows, m, 1 + SEQ:].rearrange("p (b j) -> p b j", b=NB)[:, :, 1:], ps[0:rows, m % 6, SEQ:T].rearrange("p (b j) -> p b j", b=NB), ACT.Copy).then_inc(S["pa"], 1)
                act.wait_ge(S["mixed"], 1)
                act.activation(th[0:32, :], xs[0:32, 12, :], ACT.Tanh)
                act.activation(sgd[0:96, :], xs[0:96, 13, :], ACT.Sigmoid).then_inc(S["tanh"], 1)
                act.wait_ge(S["lora_wa"], 1)
                for m in range(4):
                    act.activation(S_[0][:, m, :], ps[:, m, 0:T], ACT.Sigmoid, bias=pp("a_w0", m))
                    act.activation(S_[1][:, m, :], ps[:, 4 + m, 0:T], ACT.Sigmoid, bias=pp("a_a0", m)).then_inc(S["a_ready"], 1)
                act.wait_ge(S["lora_g"], 1)
                act.activation(S_[2], ps[:, 0:4, 0:T], ACT.Copy).then_inc(S["g_ready"], 1)
                act.wait_ge(S["kk0"], 1)
                act.wait_ge(s_shout, 16)
                act.activation(S_[9], S_[8], ACT.Square).then_inc(S["kk_sq"], 1)
                act.wait_ge(S["L"], 1)
                act.activation(S_[5], S_[3], ACT.Exp)
                act.activation(S_[6], S_[4], ACT.Exp)
                act.activation(S_[7], S_[3], ACT.Exp, scale=-1.0).then_inc(S["exps"], 1)
                root("kk", S_[9])
                for g in range(5):
                    if g:
                        act.wait_ge(S["group"], 2 * g)
                    else:
                        act.wait_ge(S["streams"], 1)
                    for o, a in zip(Odd, (S_[6], S_[0], S_[7], S_[3], S_[5])):
                        act.activation(o, a[64:128, :, g * CHUNK:(g + 1) * CHUNK], ACT.Copy).then_inc(S["odd"], 1)
                act.wait_ge(S["y_centred"], 1)
                act.activation(S_[0], S_[8], ACT.Square).then_inc(S["y_sq"], 1)
                root("y", S_[1])

            def bc_proj():
                n = 0
                for u in range(7):
                    for i, _, rows in TOK_TILES:
                        act.wait_ge(S["pbc_mm"], n + 1)
                        dst = (PBc[0:rows, i, 0:512] if u == 0 else PBc[0:rows, i, 512:672] if u == 1 else
                               PBv[0:rows, i, :] if u == 6 else PBq[0:rows, i, (u - 2) * 512:(u - 1) * 512])
                        act.activation(dst, ps[0:rows, n % 6, 0:160 if u == 1 else 512], ACT.Copy).then_inc(S["pbc_ev"], 1)
                        n += 1
                act.wait_ge(S["latent_ms"], 6)
                act.activation(sml[:, 8:14], sml[:, 8:14], ACT.Sqrt).then_inc(S["latent_root"], 1)
                for c in range(16):
                    act.wait_ge(S["qkT"], c + 1)
                    act.activation(qT[:, c, :] if c < 12 else kT[:, c - 12, :], ps[:, c % 4, 0:T], ACT.Copy).then_inc(S["qk_ev"], 1)
                act.wait_ge(S["ckvT"], 1)
                act.activation(ckvT[:, 0:2, :], ps[:, 0:2, 0:T], ACT.Copy)
                act.activation(ckvT[0:96, 2, :], ps[0:96, 2, 0:T], ACT.Copy).then_inc(S["ckvT_ev"], 1)

            def sw_prompt():
                for n in range(16):
                    act.wait_ge(S["prompt_nm"], n + 1)
                    scores = Sp[n % 2][:, :, 0:(n // H + 1) * P]
                    act.activation(scores, scores, ACT.Exp, scale=SCB, bias=sml[:, 2 + n % 2:3 + n % 2], accum_out=sml[:, 4 + n % 2:5 + n % 2]).then_inc(S["prompt_e"], 1)

            def sw_sample():

                def keys_out(part):
                    for c in range(4):
                        n = 4 * part + c
                        w = P if part % 4 == 3 else 512
                        act.wait_ge(S["kt_T"], n + 1)
                        if part >= 2:
                            act.wait_ge(S["sw_mm"], part - 1)
                        act.activation(KTw[part % 2][:, c, 0:w], ps[:, 4 + n % 2, 0:w], ACT.Copy).then_inc(S["kt_ev"], 1)

                act.wait_ge(s_out, N_ROWS_OUT)
                keys_out(0)
                for part in range(4 * NB):
                    if part + 1 < 4 * NB:
                        keys_out(part + 1)
                    if part % 4 == 3:
                        b = part // 4
                        act.wait_ge(S["sw_nm"], b + 1)
                        act.activation(Sw[b % 2], Sw[b % 2], ACT.Exp, scale=SCB, bias=sml[0:NS, 2:3], accum_out=sml[0:NS, 4:5]).then_inc(S["sw_e"], 1)

            def latent_prep():
                act.wait_ge(S["q_rows"], 1)
                n = 0
                for i, _, rows in TOK_TILES:
                    for j in range(2):
                        act.activation(qrow[0:rows, i, j * 384:j * 384 + 384], ps[0:rows, n, 0:384], ACT.Copy).then_inc(S["qrow_ev"], 1)
                        n += 1
                for hd in range(H):
                    act.wait_ge(S["qcT"], hd + 1)
                    act.activation(qcT[0:96, hd, :], ps[0:96, hd % 4, 0:T], ACT.Copy).then_inc(S["qcT_ev"], 1)
                for n in range(16):
                    hd, c = n // 2, n % 2
                    act.wait_ge(S["ql"], n + 1)
                    act.activation(qlT[:, hd, c, :], ps[:, 4 + n % 4, 0:SEQ], ACT.Copy)
                    act.activation(QL[:, c, :, TS * hd:TS * hd + TS], ps[:, 4 + n % 4, SEQ:T].rearrange("p (b j) -> p b j", b=NB), ACT.Copy).then_inc(S["ql_ev"], 1)

            def ml_prompt():
                for n in range(16):
                    act.wait_ge(S["prompt_nm"], 2 * H + n + 1)
                    scores = Sp[n % 2][:, 0, 0:(n // H + 1) * P]
                    act.activation(scores, scores, ACT.Exp, scale=SCC, bias=sml[:, 2 + n % 2:3 + n % 2], accum_out=sml[:, 4 + n % 2:5 + n % 2]).then_inc(S["prompt_e"], 1)

            def ml_sample():

                def pages_out(part):
                    for n in range(4 * part, 4 * part + 4, 2):
                        act.wait_ge(S["lt_T"], n + 1)
                        if part >= 2:
                            act.wait_ge(S["ml_mm"], part - 1)
                        kt = KTl[(n // 4) % 2][:, :, (n % 4) * P:(n % 4) * P + P]
                        act.activation(kt[:, 0:2, :], ps[:, 5 + n % 2, 0:2 * P].rearrange("p (c k) -> p c k", c=2), ACT.Copy)
                        act.activation(kt[64:96, 2, :], ps[64:96, 5 + n % 2, 2 * P:3 * P], ACT.Copy).then_inc(S["lt_even"], 1)

                pages_out(0)
                for part in range(4 * NB):
                    if part + 1 < 4 * NB:
                        pages_out(part + 1)
                    if part % 4 < 3:
                        continue
                    b = part // 4
                    act.wait_ge(S["ml_nm"], b + 1)
                    if b:
                        act.wait_ge(S["ml_PT"], b)
                    act.activation(Pl[:, 0:PAST].rearrange("p (a k) -> p a k", a=4), ps[0:NS, 0:4, :], ACT.Exp, scale=SCC, bias=sml[0:NS, 2:3], accum_out=sml[0:NS, 4:5])
                    act.activation(Pl[:, PAST:], Pl[:, PAST:], ACT.Exp, scale=SCC, bias=sml[0:NS, 2:3], accum_out=sml[0:NS, 5:6]).then_inc(S["ml_exp"], 1)

            def mix():
                for m in range(24):
                    act.wait_ge(S["pgm"], m + 1)
                    act.activation(gates[:, m, :], ps[:, m % 8, 0:T], ACT.Sigmoid, bias=pp("b_gate", m)).then_inc(S["gate"], 1)
                down("mix")

            with act.Fori(0, DEPTH) as l:
                square_x("f1_pre")
                ffn("f1")
                square_x("mix_pre", "f1")
                rwkv()
                bc_proj()
                sw_prompt()
                sw_sample()
                latent_prep()
                ml_prompt()
                ml_sample()
                mix()
                square_x("f2_pre", "mix")
                ffn("f2")
                layer_end(act, l)

        @block.vector
        def _(dve):
            dve.wait_ge(s_once, 48)

            chain = [0]

            def link(ins):
                chain[0] += 1
                ins.then_inc(s_dve, 1)
                dve.wait_ge(s_dve, chain[0])

            def root(tag, half=1.0):
                dve.wait_ge(S["norm_sums"], NORMS[tag])
                dve.tensor_scalar(rstd, ps[:, 7, 0:T], half ** -2 / D_MODEL, half ** -2 * 1e-6, ALU.mult, ALU.add).then_inc(S["mean_squares"], 1)
                dve.wait_ge(S["mean_squares"], ROOTS[tag])
                dve.wait_ge(S["roots"], ROOTS[tag])
                link(dve.reciprocal(rstd, rstd))

            def pre(tag):
                root(tag)
                for k in range(KD):
                    dve.scalar_tensor_tensor(out=h[:, k, :], in0=x[:, k, :], scalar=pp(tag, k), in1=rstd, op0=ALU.mult, op1=ALU.mult).then_inc(S["normed"], 1)
                dve.wait_ge(S["normed"], KD * PRES[tag])

            def post(tag, f, half=1.0):
                root(tag, half)
                for k in range(KD):
                    q = dve.scalar_tensor_tensor(out=yt[:, k, :], in0=yt[:, k, :], scalar=pp(tag, k), in1=rstd, op0=ALU.mult, op1=ALU.mult)
                link(q)
                for k in range(KD):
                    dve.tensor_tensor(x[:, k, :], x[:, k, :], yt[:, k, :], ALU.add).then_inc(S["x_" + f], 1)
                dve.wait_ge(S["x_" + f], KD)

            def ffn(f):
                pre(f + "_pre")
                for m in range(KF):
                    dve.wait_ge(S["ffn_sg"], FFN0[f] + m + 1)
                    link(dve.tensor_tensor(act_t[:, m, :], ps[:, m % 3, 0:T], sg2[:, m % 2, :], ALU.mult))
                    dve.tensor_tensor(act_t[:, m, :], ps[:, 3 + m % 3, 0:T], act_t[:, m, :], ALU.mult).then_inc(S["ffn_a"], 1)
                dve.wait_ge(S["ffn_a"], FFN0[f] + KF)
                post(f + "_post", f, 0.5)

            def rwkv():
                pre("mix_pre")
                dve.memset(pa, 0.0).then_inc(S["pa_zeroed"], 1)
                dve.wait_ge(S["pa_zeroed"], 1)
                link(dve.memset(xs, 0.0))
                pas = pa[:, :, 1 + SEQ:].rearrange("p m (b j) -> p m b j", b=NB)
                dve.wait_ge(s_shin, 16)
                for m in range(NAT):
                    dve.wait_ge(S["pa"], m + 1)
                    dve.tensor_tensor(xs[:, m, 0:SEQ], pa[:, m, 0:SEQ], pa[:, m, 1:1 + SEQ], ALU.subtract)
                    link(dve.tensor_copy(pas[:, m, :, 0], shin[:, m, :]))
                    link(dve.tensor_tensor(xs[:, m, SEQ:T].rearrange("p (b j) -> p b j", b=NB), pas[:, m, :, 0:TS], pas[:, m, :, 1:], ALU.subtract))
                    if m == NAT - 1:
                        dve.tensor_copy(lastT[:, :, 0], pa[:, :, SEQ])
                        dve.tensor_copy(lastT[:, :, 1:9], pas[:, :, :, TS]).then_inc(S["last_rows"], 1)
                    mu = pp("a_mu", m)
                    xm = xs[:, m, SEQ:T].rearrange("p (b j) -> p b j", b=NB)
                    dve.scalar_tensor_tensor(out=xs[:, m, 0:SEQ], in0=xs[:, m, 0:SEQ], scalar=mu, in1=pa[:, m, 1:1 + SEQ], op0=ALU.mult, op1=ALU.add)
                    q = dve.scalar_tensor_tensor(out=xm, in0=xm, scalar=mu, in1=pas[:, m, :, 1:], op0=ALU.mult, op1=ALU.add)
                q.then_inc(S["mixed"], 1)
                dve.wait_ge(S["mixed"], 1)
                r, k, v = xs[:, 0:4], xs[:, 4:8], xs[:, 8:12]
                link(dve.memset(Hp, 0.0))
                for m in range(4):
                    q = dve.tensor_scalar(S_[8][:, m, :], k[:, m, :], pp("a_kk", m), None, ALU.mult)
                q.then_inc(S["kk0"], 1)
                dve.wait_ge(S["kk0"], 1)
                link(dve.tensor_scalar(sml[:, 8:12], par[:, PAR["a_ka"][0]:PAR["a_ka"][0] + 4], -1.0, 1.0, ALU.mult, ALU.add))
                dve.wait_ge(S["a_ready"], 4)
                link(dve.tensor_scalar(S_[0], S_[0], -float(np.exp(-0.5)), None, ALU.mult))
                for m in range(4):
                    q = dve.tensor_tensor_scan(S_[3][:, m, :], C("reset"), S_[0][:, m, :], 0.0, ALU.mult, ALU.add)
                link(q)
                dve.tensor_tensor(S_[4], S_[3], S_[0], ALU.subtract).then_inc(S["L"], 1)
                dve.wait_ge(S["L"], 1)
                dve.wait_ge(S["kk_ss"], 1)
                dve.tensor_scalar(S_[9], ps[:, 4:8, 0:T], 1e-24, None, ALU.max).then_inc(S["mean_squares"], 1)
                dve.wait_ge(S["mean_squares"], ROOTS["kk"])
                dve.wait_ge(S["roots"], ROOTS["kk"])
                link(dve.reciprocal(S_[9], S_[9]))
                link(dve.tensor_tensor(S_[8], S_[8], S_[9], ALU.mult))
                dve.wait_ge(S["exps"], 1)
                for m in range(4):
                    q = dve.tensor_scalar(S_[4][:, m, :], S_[1][:, m, :], pp("a_ka", m), sml[:, 8 + m:9 + m], ALU.mult, ALU.add)
                link(q)
                link(dve.tensor_tensor(S_[4], S_[4], k, ALU.mult))
                link(dve.tensor_tensor(S_[9], r, S_[4], ALU.mult))
                for m in range(4):
                    q = dve.tensor_scalar(S_[9][:, m, :], S_[9][:, m, :], pp("a_rk", m), None, ALU.mult)
                q.then_inc(S["bonus_in"], 1)
                dve.wait_ge(S["bonus_in"], 1)
                link(dve.tensor_tensor(S_[1], S_[8], S_[1], ALU.mult))
                dve.tensor_tensor(S_[0], S_[1], S_[7], ALU.mult)
                link(dve.tensor_tensor(S_[6], S_[8], S_[6], ALU.mult))
                dve.tensor_tensor(S_[7], S_[4], S_[7], ALU.mult)
                link(dve.tensor_tensor(S_[3], r, S_[5], ALU.mult))
                dve.wait_ge(S["bonus_ss"], 1)
                dve.tensor_tensor(S_[9], ps[:, 0:4, 0:T], v, ALU.mult).then_inc(S["streams"], 1)
                dve.wait_ge(S["streams"], 1)
                for g in range(5):
                    rwkv_group(g)
                Y = S_[8]
                dve.wait_ge(S["y_mean"], 1)
                dve.scalar_tensor_tensor(out=Y, in0=ps[:, 0:4, 0:T], scalar=-1.0 / DH, in1=Y, op0=ALU.mult, op1=ALU.add).then_inc(S["y_centred"], 1)
                dve.wait_ge(S["y_centred"], 1)
                dve.wait_ge(S["y_var"], 1)
                dve.tensor_scalar(S_[1], ps[:, 4:8, 0:T], 1.0 / DH, 64e-5, ALU.mult, ALU.add).then_inc(S["mean_squares"], 1)
                dve.wait_ge(S["mean_squares"], ROOTS["y"])
                dve.wait_ge(S["roots"], ROOTS["y"])
                link(dve.reciprocal(S_[1], S_[1]))
                link(dve.tensor_tensor(Y, Y, S_[1], ALU.mult))
                for m in range(4):
                    q = dve.tensor_scalar(Y[:, m, :], Y[:, m, :], pp("a_ln_w", m), pp("a_ln_b", m), ALU.mult, ALU.add)
                link(q)
                link(dve.tensor_tensor(Y, Y, S_[9], ALU.add))
                dve.tensor_tensor(ya, Y, S_[2], ALU.mult).then_inc(S["rwkv_done"], 1)
                dve.wait_ge(S["rwkv_done"], 1)

            def rwkv_group(g):
                sample = g == 4
                t0 = g * CHUNK
                bank = lambda b: ps[0:64, b, :].rearrange("p (h s) -> p h s", h=H)
                part = lambda b, k, hf: ps[0:64, 4 * hf + b, 256 * k:256 * k + 256].rearrange("p (h s) -> p h s", h=4)
                half = lambda a, hf: a[:, 4 * hf:4 * hf + 4]
                msk = lambda n: C(n, 64).unsqueeze(1).to_broadcast([64, 4, CHUNK])
                unit = cst[0:64, CONST["ident"][0]:CONST["ident"][0] + 64].unsqueeze(1).to_broadcast([64, 4, CHUNK])
                incl = "iTs" if sample else "iTp"
                for hf in range(2):
                    dve.wait_ge(S["rows"], 2 * g + hf + 1)
                    for o, (b, k) in ((Vr, (0, 0)), (bdr, (0, 1)), (kdr, (1, 0))):
                        dve.tensor_copy(half(o, hf), part(b, k, hf))
                    dve.tensor_tensor(half(RK, hf), part(1, 1, hf), msk(incl), ALU.mult)
                    dve.wait_ge(S["RK"], 2 * g + hf + 1)
                    dve.tensor_tensor(half(X8, hf), part(2, 0, hf), msk("m8p"), ALU.mult)
                    dve.tensor_tensor(half(X8T, hf), part(2, 1, hf), msk("m8Tp"), ALU.mult).then_inc(S["masked"], 1)
                for hf in range(2):
                    if not sample:
                        for o, n in ((Xo16, "o16T"), (Xo32, "o32T"), (Xo64, "o64T")):
                            dve.tensor_tensor(half(o, hf), part(2, 1, hf), msk(n), ALU.mult)
                    dve.tensor_tensor(half(KK, hf), part(3, 0, hf), msk("sTs" if sample else "sTp"), ALU.mult)
                    dve.tensor_tensor(half(RB, hf), part(3, 1, hf), msk(incl), ALU.mult)
                    dve.wait_ge(S["inverse_mm"], 10 * g + hf + 1)
                    dve.tensor_tensor(half(Pm, hf), part(0, 0, hf), unit, ALU.add)
                    dve.tensor_copy(half(X2, hf), part(0, 0, hf))
                    dve.tensor_copy(half(X2T, hf), part(0, 1, hf)).then_inc(S["inverse_part"], 1)
                for hf in range(2):
                    dve.wait_ge(S["inverse_part"], 10 * g + hf + 1)
                    dve.wait_ge(S["inverse_mm"], 10 * g + 2 + hf + 1)
                    dve.tensor_copy(half(X4, hf), part(1, 0, hf))
                    dve.tensor_tensor(half(Pm, hf), part(1, 0, hf), half(Pm, hf), ALU.add).then_inc(S["inverse_part"], 1)
                for hf in range(2):
                    dve.wait_ge(S["inverse_part"], 10 * g + 2 + hf + 1)
                    dve.wait_ge(S["inverse_mm"], 10 * g + 4 + hf + 1)
                    dve.tensor_tensor(half(Pm, hf), part(2, 0, hf), half(Pm, hf), ALU.add).then_inc(S["inverse_part"], 1)
                for hf in range(2):
                    dve.wait_ge(S["inverse_part"], 10 * g + 4 + hf + 1)
                    dve.wait_ge(S["inverse_mm"], 10 * g + 6 + hf + 1)
                    dve.tensor_tensor(half(Tt, hf), part(3, 0, hf), half(Pm, hf), ALU.add).then_inc(S["inverse_part"], 1)
                for hf in range(2):
                    dve.wait_ge(S["inverse_mm"], 10 * g + 8 + hf + 1)
                    dve.tensor_copy(half(TT, hf), part(0, 0, hf)).then_inc(S["inverse_part"], 1)
                if not sample:
                    for i in range(3):
                        for hf in range(2):
                            dve.wait_ge(S["G"], 6 * g + 2 * i + hf + 1)
                            dve.tensor_copy(half(G, hf), part(1, 0, hf)).then_inc(S["g_level"], 1)
                        for hf in range(2):
                            if i:
                                dve.wait_ge(S["t_level"], 6 * g + 2 * i - 1 + hf)
                            else:
                                dve.wait_ge(S["inverse_part"], 10 * g + 9 + hf)
                            dve.wait_ge(S["dTT"], 6 * g + 2 * i + hf + 1)
                            dve.tensor_tensor(half(Tt, hf), part(2, 0, hf), half(Tt, hf), ALU.add)
                            dve.tensor_tensor(half(TT, hf), part(2, 1, hf), half(TT, hf), ALU.add).then_inc(S["t_level"], 1)
                    for hf in range(2):
                        dve.wait_ge(S["rhs"], 2 * g + hf + 1)
                        dve.tensor_copy(half(RHS, hf), part(3, 0, hf)).then_inc(S["rhs_ev"], 1)
                    for hf in range(2):
                        dve.wait_ge(S["u"], 2 * g + hf + 1)
                        dve.tensor_scalar(half(U, hf), part(0, 0, hf), -1.0, None, ALU.mult).then_inc(S["u_ev"], 1)
                    pairs = Hp.rearrange("p (m r) v -> p r m v", r=2)
                    dve.wait_ge(S["odd"], 5 * g + 5)
                    for hf in range(2):
                        dve.wait_ge(S["y"], 2 * g + hf + 1)
                        dve.tensor_copy(S_[8][:, 2 * hf:2 * hf + 2, t0:t0 + CHUNK], ps[:, 4 * hf + 1, 0:2 * CHUNK].rearrange("p (m t) -> p m t", m=2))
                        dve.wait_ge(S["h"], 2 * g + hf + 1)
                        if g:
                            dve.wait_ge(S["group"], 2 * g - 1 + hf)
                        link(dve.tensor_tensor(half(Hp, hf), part(2, 0, hf), half(Hp, hf), ALU.add))
                        for r, el in ((0, S_[5][0:64, 2 * hf:2 * hf + 2, t0 + CHUNK - 1:t0 + CHUNK]),
                                      (1, Odd[4][:, 2 * hf:2 * hf + 2, CHUNK - 1:CHUNK])):
                            own = pairs[:, r, 2 * hf:2 * hf + 2]
                            q = dve.tensor_tensor(own, own, el.to_broadcast([64, 2, DH]), ALU.mult)
                        q.then_inc(S["group"], 1)
                    return
                bm = C("bmask", 64).unsqueeze(2).to_broadcast([64, NB, DH])
                for hd in range(H):
                    dve.wait_ge(S["zh_mm"], hd + 1)
                    dve.tensor_tensor(Tm, ps[0:64, hd % 2, :].rearrange("p (b v) -> p b v", b=NB), bm, ALU.mult).then_inc(S["zh"], 1)
                    dve.wait_ge(S["zh"], hd + 1)
                    link(dve.tensor_reduce(RHS[:, hd], Tm.rearrange("p b v -> p v b"), AX, ALU.add))
                dve.wait_ge(S["rhs"], 2 * g + 1)
                dve.tensor_tensor(RHS, bank(3), RHS, ALU.add).then_inc(S["rhs_ev"], 1)
                dve.wait_ge(S["u"], 2 * g + 1)
                dve.tensor_scalar(U, bank(4), -1.0, None, ALU.mult).then_inc(S["u_ev"], 1)
                dve.wait_ge(S["u_ev"], 2 * g + 1)
                dve.wait_ge(S["y"], 2 * g + 1)
                dve.tensor_copy(S_[8][:, :, t0:t0 + CHUNK], ps[:, 5, 0:256].rearrange("p (m t) -> p m t", m=4))
                dve.wait_ge(S["odd"], 5 * g + 5)

                def by_sample(hd):
                    for o, a in zip(UV[hd % 2], (U, Vr)):
                        q = dve.tensor_tensor(o, a[:, hd].unsqueeze(1).to_broadcast([64, NB, DH]), bm, ALU.mult)
                    q.then_inc(S["ue"], 1)

                by_sample(0)
                by_sample(1)
                for hd in range(H):
                    dve.wait_ge(S["hs"], hd + 1)
                    Hh = Hs(hd)
                    link(dve.tensor_tensor(Hh, ps[0:64, 6 + hd % 2, :], Hh, ALU.add))
                    Hh = Hh.rearrange("p (b v) -> p b v", b=NB)
                    el = Odd[4][:, hd // 2, :] if hd % 2 else S_[5][0:64, hd // 2, SEQ:T]
                    el = el.rearrange("p (b j) -> p b j", b=NB)[:, :, TS - 1:TS]
                    q = dve.tensor_tensor(Hh, Hh, el.to_broadcast([64, NB, DH]), ALU.mult)
                    if hd + 2 < H:
                        by_sample(hd + 2)
                q.then_inc(S["group"], 1)
                dve.wait_ge(S["group"], 2 * g + 1)

            def rope(v, heads, half, cos, sin, tmp):
                rows = v.shape[0]
                a, b = v[:, :, 0:half], v[:, :, half:2 * half]
                cos, sin = [c.unsqueeze(1).to_broadcast([rows, heads, half]) for c in (cos, sin)]
                n = heads * half
                t = [tmp[0:rows, i * n:i * n + n].rearrange("p (h d) -> p h d", h=heads) for i in range(4)]
                dve.tensor_tensor(t[0], a, cos, ALU.mult)
                dve.tensor_tensor(t[1], b, sin, ALU.mult)
                dve.tensor_tensor(t[2], b, cos, ALU.mult)
                link(dve.tensor_tensor(t[3], a, sin, ALU.mult))
                dve.tensor_tensor(a, t[0], t[1], ALU.subtract)
                return dve.tensor_tensor(b, t[2], t[3], ALU.add)

            def bc_rows():
                link(dve.memset(sml[:, 8:14], 1.0))
                parts = ((0, Q_LORA), (Q_LORA, KV_LORA))
                for i, _, rows in TOK_TILES:
                    dve.wait_ge(S["pbc_ev"], 3 + i + 1)
                    for j, (c0, w) in enumerate(parts):
                        part, ms = PBc[0:rows, i, c0:c0 + w], sml[0:rows, 8 + 2 * i + j:9 + 2 * i + j]
                        link(dve.tensor_tensor_reduce(rt[0:rows, 0:w], part, part, 1.0, 0.0, ALU.mult, ALU.add, ms))
                        dve.tensor_scalar(ms, ms, 1.0 / w, 1e-6, ALU.mult, ALU.add).then_inc(S["latent_ms"], 1)
                        dve.wait_ge(S["latent_ms"], 2 * i + j + 1)
                dve.wait_ge(S["latent_root"], 1)
                link(dve.reciprocal(sml[:, 8:14], sml[:, 8:14]))
                for i, _, rows in TOK_TILES:
                    q_part, kv_part = [PBc[0:rows, i, c0:c0 + w] for c0, w in parts]
                    link(dve.tensor_scalar(q_part, q_part, sml[0:rows, 8 + 2 * i:9 + 2 * i], None, ALU.mult))
                    link(dve.scalar_tensor_tensor(out=kv_part, in0=kv_part, scalar=sml[0:rows, 9 + 2 * i:10 + 2 * i], in1=kvn[0:rows, :], op0=ALU.mult, op1=ALU.mult))
                    link(rope(PBc[0:rows, i:i + 1, Q_LORA + KV_LORA:], 1, DROPE // 2, C("cosc")[0:rows, 16 * i:16 * i + 16],
                              C("sinc")[0:rows, 16 * i:16 * i + 16], rt))
                dve.wait_ge(S["pbc_ev"], 21)
                for i, _, rows in TOK_TILES:
                    rope(PBq[0:rows, i, :].rearrange("p (h d) -> p h d", h=32), 32, ROT, C("cosb")[0:rows, 8 * i:8 * i + 8],
                         C("sinb")[0:rows, 8 * i:8 * i + 8], rt).then_inc(S["rows_ready"], 1)
                    dve.wait_ge(S["rows_ready"], i + 1)

            def softmax_in(tag, n, src, mask, scores):
                i, base = n % 2, PROMPT0[tag]
                dve.tensor_tensor_reduce(scores, src, mask, 1.0, NEG, ALU.add, ALU.max, sml[:, i:i + 1]).then_inc(S["prompt_s"], 1)
                dve.wait_ge(S["prompt_s"], base + n + 1)
                dve.tensor_scalar(sml[:, 2 + i:3 + i], sml[:, i:i + 1], -(SCB if tag == "swp" else SCC), None, ALU.mult).then_inc(S["prompt_nm"], 1)
                dve.wait_ge(S["prompt_nm"], base + n + 1)

            def prompt_attention(tag, y, one_group):
                base = PROMPT0[tag]
                w = lambda n: (n // H + 1) * P
                src = lambda n: (ps[:, n % 2, 0:w(n)] if one_group else
                                 ps[:, 2 * (n % 2):2 * (n % 2) + 2, :].rearrange("p b k -> p (b k)")[:, 0:768].rearrange("p (g k) -> p g k", g=3)[:, :, 0:w(n)])

                def finish(n):
                    r0, m, t = 64 * (n % 2), (n % H) // 2, n // H
                    dve.wait_ge(S["prompt_o"], base + n + 1)
                    dve.tensor_copy(y[r0:r0 + 64, m, t * P:t * P + P], ps[r0:r0 + 64, 6 + n % 2, 0:P]).then_inc(S["prompt_y"], 1)
                    dve.wait_ge(S["prompt_y"], base + n + 1)

                for i in range(20):
                    if i < 16:
                        t = i // H
                        dve.wait_ge(S["prompt_mm"], base + i + 1)
                        scores = Sp[i % 2][:, 0, 0:w(i)] if one_group else Sp[i % 2][:, :, 0:w(i)]
                        mask = (C("mlp")[:, t * SEQ:t * SEQ + w(i)] if one_group else
                                C("swp")[:, t * 768:t * 768 + 768].rearrange("p (g k) -> p g k", g=3)[:, :, 0:w(i)])
                        softmax_in(tag, i, src(i), mask, scores)
                    if 1 <= i < 17:
                        n = i - 1
                        dve.wait_ge(S["prompt_e"], base + n + 1)
                        probs, rs, pc = Sp[n % 2][:, :, 0:w(n)], sml[:, 4 + n % 2:5 + n % 2], Pc[n % 2][:, 0:w(n)]
                        link(dve.reciprocal(rs, rs))
                        if one_group:
                            dve.tensor_scalar(pc, probs[:, 0, :], rs, None, ALU.mult).then_inc(S["prompt_p"], 1)
                            dve.wait_ge(S["prompt_p"], base + n + 1)
                        else:
                            link(dve.tensor_tensor(pc, probs[:, 0, :], probs[:, 1, :], ALU.add))
                            link(dve.tensor_tensor(pc, pc, probs[:, 2, :], ALU.add))
                            dve.tensor_scalar(pc, pc, rs, None, ALU.mult).then_inc(S["prompt_p"], 1)
                            dve.wait_ge(S["prompt_p"], base + n + 1)
                    if 2 <= i < 18:
                        n = i - 2
                        dve.wait_ge(S["prompt_T"], base + n + 1)
                        t = n // H + 1
                        dve.tensor_copy(PTp[n % 2][:, 0:t, :], ps[:, (2 if one_group else 4) + n % 2, 0:t * P].rearrange("p (c k) -> p c k", c=t)).then_inc(S["prompt_pt"], 1)
                        dve.wait_ge(S["prompt_pt"], base + n + 1)
                    if one_group and 3 <= i < 19:
                        n = i - 3
                        dve.wait_ge(S["prompt_ol"], n + 1)
                        dve.tensor_copy(OLp[n % 2], ps[:, 4 + n % 2, 0:256].rearrange("p (c k) -> p c k", c=2)).then_inc(S["prompt_olev"], 1)
                        dve.wait_ge(S["prompt_olev"], n + 1)
                    if not one_group and 3 <= i < 19:
                        finish(i - 3)
                    if one_group and 4 <= i:
                        finish(i - 4)

            def sw_sample():
                dve.memset(Qbd, 0.0)
                link(dve.memset(PnF, 0.0))
                q4 = qT.rearrange("p (g c) t -> p g c t", g=3)
                tokens = lambda b: slice(SEQ + TS * b, SEQ + TS * b + TS)

                def queries(b):
                    for c in range(4):
                        for r in range(2):
                            o = Qbd[64 * r:64 * r + 64, c, :, 16 * c + 8 * r:16 * c + 8 * r + 8]
                            dve.tensor_copy(o, q4[64 * r:64 * r + 64, :, c, tokens(b)]).then_inc(S["qbd"], 1)

                def softmax(b):
                    Sb = Sw[b % 2]
                    dve.wait_ge(S["sw_e"], b + 1)
                    link(dve.reciprocal(sml[0:NS, 6 + b % 2:7 + b % 2], sml[0:NS, 4:5]))
                    n0 = SW_TILES * P
                    if b:
                        dve.memset(PnF[:, TS * (b - 1):TS * b], 0.0)
                    o = PnF[:, TS * b:TS * b + TS]
                    link(dve.tensor_tensor(o, Sb[:, n0:n0 + TS], Sb[:, n0 + TS:n0 + 2 * TS], ALU.add))
                    dve.tensor_tensor(o, o, Sb[:, n0 + 2 * TS:n0 + 3 * TS], ALU.add).then_inc(S["sw_p"], 1)
                    dve.wait_ge(S["sw_p"], b + 1)

                def probs_out(b):
                    dve.wait_ge(S["sw_PT"], b + 1)
                    dve.tensor_copy(PTw[:, 0:8, :], ps[:, 6, :].rearrange("p (t n) -> p t n", t=8))
                    dve.tensor_copy(PTw[:, 8:13, :], ps[:, 7, 0:320].rearrange("p (t n) -> p t n", t=5))
                    dve.tensor_copy(PTn, ps[0:NS, 7, 320:384]).then_inc(S["sw_pt"], 1)
                    dve.wait_ge(S["sw_pt"], b + 1)

                def own_values(b):
                    dve.wait_ge(S["sw_pv"], b + 1)
                    dve.scalar_tensor_tensor(out=Ow, in0=ps[0:NS, 7, :].rearrange("p (h v) -> p h v", h=H),
                                             scalar=sml[0:NS, 6 + b % 2:7 + b % 2],
                                             in1=C("bmask", NS).unsqueeze(2).to_broadcast([NS, H, DH]),
                                             op0=ALU.mult, op1=ALU.mult).then_inc(S["sw_own"], 1)
                    dve.wait_ge(S["sw_own"], b + 1)

                def result(b):
                    dve.wait_ge(S["sw_y"], b + 1)
                    dve.tensor_copy(yb[:, :, tokens(b)], ps[:, 6, 0:4 * TS].rearrange("p (c j) -> p c j", c=4)).then_inc(S["sws_done"], 1)
                    dve.wait_ge(S["sws_done"], b + 1)

                queries(0)
                dve.wait_ge(s_out, N_ROWS_OUT)
                for b in range(NB):
                    if b:
                        probs_out(b - 1)
                    Sb = Sw[b % 2]
                    dve.wait_ge(S["sw_s"], b + 1)
                    dve.tensor_tensor_reduce(Sb, ps[0:NS, 0:4, :].rearrange("p b k -> p (b k)")[:, 0:SW_COLS], C("sws", NS), 1.0, NEG,
                                             ALU.add, ALU.max, sml[0:NS, 0:1]).then_inc(S["sw_masked"], 1)
                    dve.wait_ge(S["sw_masked"], b + 1)
                    if b + 1 < NB:
                        queries(b + 1)
                    dve.tensor_scalar(sml[0:NS, 2:3], sml[0:NS, 0:1], -SCB, None, ALU.mult).then_inc(S["sw_nm"], 1)
                    dve.wait_ge(S["sw_nm"], b + 1)
                    if b:
                        own_values(b - 1)
                    softmax(b)
                    if b:
                        result(b - 1)
                probs_out(NB - 1)
                own_values(NB - 1)
                result(NB - 1)

            def latent_prep():
                dve.wait_ge(s_out, N_ROWS_OUT)
                dve.wait_ge(S["cqT"], 1)
                for k in range(3):
                    dve.tensor_scalar(cqT[:, k, :], ps[:, k, 0:T], pp("c_q_norm", k), None, ALU.mult)
                dve.wait_ge(S["kvT"], 1)
                dve.tensor_copy(kvT[0:64].rearrange("p (a b) k -> p a (b k)", b=2), ps[0:64, 3:7, :]).then_inc(S["kvT_ev"], 1)
                dve.wait_ge(S["kvT_ev"], 1)
                dve.wait_ge(S["qrow_ev"], 6)
                for i, _, rows in TOK_TILES:
                    v = qrow[0:rows, i, :].rearrange("p (h d) -> p h d", h=H)[:, :, DNOPE:]
                    rope(v, H, DROPE // 2, C("cosc")[0:rows, 16 * i:16 * i + 16], C("sinc")[0:rows, 16 * i:16 * i + 16], rt2).then_inc(S["q_rope"], 1)
                    dve.wait_ge(S["q_rope"], i + 1)
                dve.wait_ge(S["qcT_ev"], H)
                dve.tensor_copy(QR[64:96], qcT[64:96, :, SEQ:T].rearrange("p h (b j) -> p b h j", b=NB))
                dve.wait_ge(S["ql_ev"], 16)
                dve.memset(PnL, 0.0).then_inc(S["ml_prep"], 1)
                dve.wait_ge(S["ml_prep"], 1)

            def ml_sample():

                def pages_out(part):
                    for n in range(4 * part + 1, 4 * part + 4, 2):
                        dve.wait_ge(S["lt_T"], n + 1)
                        if part >= 2:
                            dve.wait_ge(S["ml_mm"], part - 1)
                        kt = KTl[(n // 4) % 2][:, :, (n % 4) * P:(n % 4) * P + P]
                        dve.tensor_copy(kt[:, 0:2, :], ps[:, 5 + n % 2, 0:2 * P].rearrange("p (c k) -> p c k", c=2))
                        dve.tensor_copy(kt[64:96, 2, :], ps[64:96, 5 + n % 2, 2 * P:3 * P]).then_inc(S["lt_odd"], 1)

                def new_scores(b):
                    dve.wait_ge(S["ml_s"], b + 1)
                    link(dve.tensor_tensor(Pl[:, PAST:], ps[0:NS, 4, 0:TS], C("mls", NS), ALU.add))

                def maximum(b):
                    dve.tensor_reduce(sml[0:NS, 0:1], ps[0:NS, 0:4, :], mybir.AxisListType.XY, ALU.max)
                    link(dve.tensor_reduce(sml[0:NS, 1:2], Pl[:, PAST:], AX, ALU.max))
                    link(dve.tensor_tensor(sml[0:NS, 0:1], sml[0:NS, 0:1], sml[0:NS, 1:2], ALU.max))
                    dve.tensor_scalar(sml[0:NS, 2:3], sml[0:NS, 0:1], -SCC, None, ALU.mult).then_inc(S["ml_nm"], 1)
                    dve.wait_ge(S["ml_nm"], b + 1)

                def softmax(b):
                    dve.wait_ge(S["ml_exp"], b + 1)
                    link(dve.tensor_tensor(sml[0:NS, 3:4], sml[0:NS, 4:5], sml[0:NS, 5:6], ALU.add))
                    dve.reciprocal(sml[0:NS, 6 + b % 2:7 + b % 2], sml[0:NS, 3:4])
                    if b:
                        dve.memset(PnL[:, TS * (b - 1):TS * b], 0.0)
                    dve.tensor_copy(PnL[:, TS * b:TS * b + TS], Pl[:, PAST:]).then_inc(S["ml_p"], 1)
                    dve.wait_ge(S["ml_p"], b + 1)

                def probs_out(b):
                    dve.wait_ge(S["ml_PT"], b + 1)
                    for half in range(2):
                        dve.tensor_copy(PTL[:, 8 * half:8 * half + 8, :], ps[:, 5 + 2 * half, :].rearrange("p (t n) -> p t n", t=8))
                    dve.tensor_copy(PTl, ps[0:NS, 6, 0:NS]).then_inc(S["ml_pt"], 1)
                    dve.wait_ge(S["ml_pt"], b + 1)

                def divided(b):
                    dve.wait_ge(S["ml_pv"], b + 1)
                    dve.tensor_scalar(Osb, ps[0:NS, 4, 256:512], sml[0:NS, 6 + b % 2:7 + b % 2], None, ALU.mult).then_inc(S["ml_osb"], 1)
                    dve.wait_ge(S["ml_osb"], b + 1)

                def result(b):
                    dve.wait_ge(S["ml_oT"], b + 1)
                    dve.tensor_copy(olT[:, :, :, TS * b:TS * b + TS], ps[:, 7, 0:2 * NS].rearrange("p (c h j) -> p c h j", c=2, h=H)).then_inc(S["ml_olT"], 1)
                    dve.wait_ge(S["ml_olT"], b + 1)

                pages_out(0)
                for part in range(4 * NB):
                    if part + 1 < 4 * NB:
                        pages_out(part + 1)
                    if part % 4 == 0 and part >= 8:
                        result(part // 4 - 2)
                    if part % 4 == 3:
                        b = part // 4
                        new_scores(b)
                        if b:
                            probs_out(b - 1)
                        maximum(b)
                        softmax(b)
                        if b:
                            divided(b - 1)
                result(NB - 2)
                probs_out(NB - 1)
                divided(NB - 1)
                result(NB - 1)
                dve.wait_ge(S["ml_yc"], 1)
                dve.tensor_copy(yc[:, :, SEQ:T], ps[:, 0, 0:4 * NS].rearrange("p (m t) -> p m t", m=4)).then_inc(S["ml_done"], 1)
                dve.wait_ge(S["ml_done"], 1)

            def mix():
                for n in range(24):
                    m = n % KD
                    dve.wait_ge(S["brm"], n + 1)
                    if n < KD:
                        dve.tensor_tensor(mt[:, m, :], ps[:, m, 0:T], gates[:, n, :], ALU.mult).then_inc(S["br_ev"], 1)
                        dve.wait_ge(S["br_ev"], n + 1)
                    else:
                        link(dve.tensor_tensor(gates[:, n, :], ps[:, m, 0:T], gates[:, n, :], ALU.mult))
                        dve.tensor_tensor(mt[:, m, :], gates[:, n, :], mt[:, m, :], ALU.add).then_inc(S["br_ev"], 1)
                        dve.wait_ge(S["br_ev"], n + 1)
                post("mix_post", "mix")

            with dve.Fori(0, DEPTH) as l:
                dve.wait_ge(s_par, 16 * 5)
                ffn("f1")
                rwkv()
                bc_rows()
                prompt_attention("swp", yb, False)
                sw_sample()
                latent_prep()
                prompt_attention("mlp", yc, True)
                ml_sample()
                mix()
                ffn("f2")
                layer_end(dve, l)


_IN = ["consts", "params", "xT", "shiftT", "wkvT", "page_table", "cache_mla_ckv", "cache_mla_krope", "cache_swa_k",
       "cache_swa_v", "c_kv_norm", "a_w2", "a_a2", "a_g2", "w_in", "w_branch_a", "w_branch_b", "w_branch_c", "w_out",
       "c_q_up", "c_kv_up", "f1_wg", "f1_wu", "f1_wd", "f2_wg", "f2_wu", "f2_wd"]
_OUT = {"yT": (P, KD, T), "o_ckv_p": (DEPTH, 1, SEQ, KV_LORA), "o_ckv_s": (DEPTH, NB, TS, KV_LORA),
        "o_krope_p": (DEPTH, 1, SEQ, DROPE), "o_krope_s": (DEPTH, NB, TS, DROPE),
        "o_swa_k_p": (DEPTH, 1, SEQ, W_A), "o_swa_k_s": (DEPTH, NB, PAST, W_A),
        "o_swa_v_p": (DEPTH, 1, SEQ, W_A), "o_swa_v_s": (DEPTH, NB, PAST, W_A),
        "o_wkv_p": (DEPTH, DH, H, DH), "o_wkv_s": (DEPTH, 2, DH, 4, NB * DH), "o_shift": (DEPTH, P, NAT, 9)}


def kernel(**inputs):
    import concourse.bacc as bacc
    from concourse.bass_utils import run_bass_kernel_spmd

    a = {k: np.ascontiguousarray(v) for k, v in inputs.items()}

    def by_channel(v, tiles):
        out = np.zeros((v.shape[0], P, len(tiles)) + v.shape[2:], v.dtype)
        for m, (c0, rows) in enumerate(tiles):
            out[:, :rows, m] = v[:, c0:c0 + rows]
        return out

    full = lambda n: [(i * P, P) for i in range(n)]
    names = {"f1_pre": "n_f1_pre", "f1_post": "n_f1_post", "mix_pre": "n_mix_pre", "mix_post": "n_mix_post",
             "f2_pre": "n_f2_pre", "f2_post": "n_f2_post"}
    params = [by_channel(a[names.get(n, n)].reshape(DEPTH, -1), A_TILES if n == "a_mu" else full(w))
              for n, (_, w) in PAR.items()]
    tokens = np.concatenate([a["x_prompt"].reshape(SEQ, D_MODEL), a["x_sample"].reshape(NS, D_MODEL)])
    states = a["state_rwkv_wkv"].reshape(DEPTH, NB, 4, 2, DH, DH).transpose(0, 3, 5, 2, 1, 4).reshape(DEPTH, 2, DH, 4, NB * DH)
    arrays = {
        "consts": constants(), "params": np.concatenate(params, axis=2),
        "xT": np.ascontiguousarray(tokens.T.reshape(KD, P, T).transpose(1, 0, 2)),
        "shiftT": by_channel(a["state_rwkv_shift"].transpose(0, 2, 1), A_TILES),
        "wkvT": np.ascontiguousarray(states),
        "cache_swa_k": a["cache_swa_k"].reshape(DEPTH, NB, PAST, W_A),
        "cache_swa_v": a["cache_swa_v"].reshape(DEPTH, NB, PAST, W_A),
    }
    for n in _IN:
        if n not in arrays:
            arrays[n] = a[n]

    nc = bacc.Bacc("TRN2", target_bir_lowering=False, num_devices=1)
    io = {n: nc.dram_tensor(f"in_{n}_dram", arrays[n].shape, mybir.dt.from_np(arrays[n].dtype), kind="ExternalInput").ap()
          for n in _IN}
    for n, shape in _OUT.items():
        io[n] = nc.dram_tensor(f"out_{n}_dram", shape, F32, kind="ExternalOutput").ap()
    build(nc, io)
    r = run_bass_kernel_spmd(nc, [{f"in_{n}_dram": arrays[n] for n in _IN}], core_ids=[0]).results[0]
    o = {n: r[f"out_{n}_dram"] for n in _OUT}

    tokens = o["yT"].transpose(1, 0, 2).reshape(D_MODEL, T).T
    rows = np.concatenate([o["o_shift"][:, :n, m] for m, (_, n) in enumerate(A_TILES)], axis=1)
    wkv_p = o["o_wkv_p"].transpose(0, 2, 3, 1)[:, None]
    wkv_s = o["o_wkv_s"].reshape(DEPTH, 2, DH, 4, NB, DH).transpose(0, 4, 3, 1, 5, 2).reshape(DEPTH, NB, H, DH, DH)
    heads = lambda v: v.reshape(v.shape[:3] + (H, DH))
    c = np.ascontiguousarray
    return (c(tokens[:SEQ].reshape(1, SEQ, D_MODEL)), c(tokens[SEQ:].reshape(NB, TS, D_MODEL)),
            o["o_ckv_p"], o["o_ckv_s"], o["o_krope_p"], o["o_krope_s"],
            heads(o["o_swa_k_p"]), heads(o["o_swa_k_s"]), heads(o["o_swa_v_p"]), heads(o["o_swa_v_s"]),
            c(wkv_p), c(wkv_s), c(rows[:, None, :, 0]), c(rows[:, :, 1:].transpose(0, 2, 1)))
```
